# Optimizing a Trainium2 kernel written in Bass

```python
import math
import jax, jax.numpy as jnp
from jax import lax
import numpy as np
import jax
import jax.numpy as jnp

D_MODEL = 2048
BATCH = 1
SEQ = 256
DEPTH = 1

S5_WIDTH = D_MODEL // 2
S5_GROUP = 16
S5_GROUPS = S5_WIDTH // S5_GROUP
S5_STATE = 64
S5_DT_MIN = 0.001
S5_DT_MAX = 0.1
DN_HEADS = 8
DN_DK = 128
DN_DV = 128
DN_QK_WIDTH = DN_HEADS * DN_DK
DN_V_WIDTH = DN_HEADS * DN_DV
DN_CONV = 4
DN_CHUNK = 64
DN_DT_MIN = 0.001
DN_DT_MAX = 0.1
FFN_DIM = 5632
FFN_CONV = 3
NORM_EPS = 1e-6

OFF_U = S5_WIDTH
OFF_QKV = OFF_U + 2 * DN_QK_WIDTH + DN_V_WIDTH
OFF_Z = OFF_QKV + DN_V_WIDTH
OFF_BETA = OFF_Z + DN_HEADS
OFF_ALPHA = OFF_BETA + DN_HEADS
OFF_GS = OFF_ALPHA + D_MODEL
N_IN = OFF_GS + D_MODEL
SPLITS = [OFF_U, OFF_QKV, OFF_Z, OFF_BETA, OFF_ALPHA, OFF_GS]


def rmsnorm(x, w):
    xf = x.astype(jnp.float32)
    y = xf * lax.rsqrt(jnp.mean(xf * xf, axis=-1, keepdims=True) + NORM_EPS) * w.astype(jnp.float32)
    return y.astype(x.dtype)

def l2norm(x):
    return x * lax.rsqrt(jnp.sum(x * x, axis=-1, keepdims=True) + NORM_EPS)

def causal_dwconv(x, w):
    K, C = w.shape
    return lax.conv_general_dilated(
        x, w[:, None, :].astype(x.dtype), window_strides=(1,), padding=[(K - 1, 0)],
        dimension_numbers=("NWC", "WIO", "NWC"), feature_group_count=C)

def s5_branch(u, log_dt, a_re, a_im, b_re, b_im, c_re, c_im, d):
    Bn, L, _ = u.shape
    f32 = jnp.float32
    uf = u.astype(f32)
    ug = uf.reshape(Bn, L, S5_GROUPS, S5_GROUP)
    lr, li = a_re.astype(f32), a_im.astype(f32)
    dt = jnp.exp(log_dt.astype(f32))[:, None]
    mag = jnp.exp(lr * dt)
    abar_re, abar_im = mag * jnp.cos(li * dt), mag * jnp.sin(li * dt)
    den = lr * lr + li * li
    nr, ni = abar_re - 1.0, abar_im
    coef_re = (nr * lr + ni * li) / den
    coef_im = (ni * lr - nr * li) / den
    br, bi = b_re.astype(f32), b_im.astype(f32)
    bbar_re = coef_re[..., None] * br - coef_im[..., None] * bi
    bbar_im = coef_re[..., None] * bi + coef_im[..., None] * br
    bu_re = jnp.einsum("gph,blgh->blgp", bbar_re, ug)
    bu_im = jnp.einsum("gph,blgh->blgp", bbar_im, ug)
    ar_t = jnp.broadcast_to(abar_re, bu_re.shape)
    ai_t = jnp.broadcast_to(abar_im, bu_re.shape)

    def combine(e1, e2):
        a1r, a1i, b1r, b1i = e1
        a2r, a2i, b2r, b2i = e2
        return (a2r * a1r - a2i * a1i,
                a2r * a1i + a2i * a1r,
                a2r * b1r - a2i * b1i + b2r,
                a2r * b1i + a2i * b1r + b2i)

    _, _, xr, xi = lax.associative_scan(combine, (ar_t, ai_t, bu_re, bu_im), axis=1)
    y = (jnp.einsum("ghp,blgp->blgh", c_re.astype(f32), xr)
         - jnp.einsum("ghp,blgp->blgh", c_im.astype(f32), xi))
    y = y.reshape(Bn, L, S5_WIDTH) + d.astype(f32) * uf
    return jax.nn.gelu(y, approximate=False).astype(u.dtype)

def chunk_gated_delta_rule(q, k, v, g, beta):
    Bn, L, H, DK = q.shape
    DV = v.shape[-1]
    N, C = L // DN_CHUNK, DN_CHUNK

    def chunks(t):
        return t.reshape(Bn, N, C, H, -1).transpose(1, 0, 3, 2, 4)

    qc, kc, vc = chunks(q), chunks(k), chunks(v)
    bc = beta.reshape(Bn, N, C, H).transpose(1, 0, 3, 2)
    gc = jnp.cumsum(g.reshape(Bn, N, C, H).transpose(1, 0, 3, 2), axis=-1)
    tril = jnp.tril(jnp.ones((C, C), dtype=bool))
    strict = jnp.tril(jnp.ones((C, C), dtype=bool), -1)
    decay = jnp.exp(jnp.where(tril, gc[..., :, None] - gc[..., None, :], -jnp.inf))
    k_beta = kc * bc[..., None]
    v_beta = vc * bc[..., None]
    lmat = jnp.where(strict, jnp.einsum("nbhcd,nbhsd->nbhcs", k_beta, kc) * decay, 0.0)
    eye = jnp.eye(C, dtype=q.dtype)
    rhs = jnp.concatenate([v_beta, k_beta * jnp.exp(gc)[..., None]], axis=-1)
    sol = lax.linalg.triangular_solve(eye + lmat, rhs, left_side=True, lower=True, unit_diagonal=True)
    u_c, w_c = sol[..., :DV], sol[..., DV:]
    attn = jnp.where(tril, jnp.einsum("nbhcd,nbhsd->nbhcs", qc, kc) * decay, 0.0)

    def step(S, inp):
        q_i, k_i, u_i, w_i, g_i, a_i = inp
        v_new = u_i - jnp.einsum("bhcd,bhdv->bhcv", w_i, S)
        o_i = (jnp.einsum("bhcd,bhdv->bhcv", q_i * jnp.exp(g_i)[..., None], S)
               + jnp.einsum("bhcs,bhsv->bhcv", a_i, v_new))
        g_last = g_i[..., -1]
        S = (S * jnp.exp(g_last)[..., None, None]
             + jnp.einsum("bhcd,bhcv->bhdv", k_i * jnp.exp(g_last[..., None] - g_i)[..., None], v_new))
        return S, o_i

    S0 = jnp.zeros((Bn, H, DK, DV), q.dtype)
    _, o = lax.scan(step, S0, (qc, kc, u_c, w_c, gc, attn))
    return o.transpose(1, 0, 3, 2, 4).reshape(Bn, L, H, DV)

def deltanet_branch(qkv, z, b_raw, a_raw, conv_w, a_log, dt_bias, norm_w):
    Bn, L, _ = qkv.shape
    f32 = jnp.float32
    qkv = jax.nn.silu(causal_dwconv(qkv, conv_w))
    q, k, v = jnp.split(qkv, [DN_QK_WIDTH, 2 * DN_QK_WIDTH], axis=-1)
    q = l2norm(q.reshape(Bn, L, DN_HEADS, DN_DK).astype(f32)) * (DN_DK ** -0.5)
    k = l2norm(k.reshape(Bn, L, DN_HEADS, DN_DK).astype(f32))
    v = v.reshape(Bn, L, DN_HEADS, DN_DV).astype(f32)
    beta = jax.nn.sigmoid(b_raw.astype(f32))
    g = -jnp.exp(a_log.astype(f32)) * jax.nn.softplus(a_raw.astype(f32) + dt_bias.astype(f32))
    o = chunk_gated_delta_rule(q, k, v, g, beta)
    o = rmsnorm(o, norm_w) * jax.nn.silu(z.reshape(Bn, L, DN_HEADS, DN_DV).astype(f32))
    return o.reshape(Bn, L, DN_V_WIDTH).astype(qkv.dtype)

def first_inputs(seed: int = 0) -> dict:
    key = jax.random.key(seed)
    ks = jax.random.split(key, 26)
    f32 = jnp.float32

    def nrm(k, shape, scale):
        return jax.random.normal(k, shape, f32) * scale

    G, P, HG = S5_GROUPS, S5_STATE, S5_GROUP
    x = nrm(ks[0], (BATCH, SEQ, D_MODEL), 1.0)
    mix_norm_w = 1.0 + nrm(ks[1], (DEPTH, D_MODEL), 0.02)
    w_in = nrm(ks[2], (DEPTH, D_MODEL, N_IN), D_MODEL ** -0.5)
    s5_log_dt = jax.random.uniform(ks[3], (DEPTH, G), f32, math.log(S5_DT_MIN), math.log(S5_DT_MAX))
    s5_a_re = -0.5 + nrm(ks[4], (DEPTH, G, P), 0.01)
    s5_a_im = math.pi * jnp.arange(P, dtype=f32) + nrm(ks[5], (DEPTH, G, P), 0.01)
    s5_b_re = nrm(ks[6], (DEPTH, G, P, HG), (2 * HG) ** -0.5)
    s5_b_im = nrm(ks[7], (DEPTH, G, P, HG), (2 * HG) ** -0.5)
    s5_c_re = nrm(ks[8], (DEPTH, G, HG, P), (2 * P) ** -0.5)
    s5_c_im = nrm(ks[9], (DEPTH, G, HG, P), (2 * P) ** -0.5)
    s5_d = nrm(ks[10], (DEPTH, S5_WIDTH), 1.0)
    s5_glu_w = nrm(ks[11], (DEPTH, S5_WIDTH, 2 * D_MODEL), S5_WIDTH ** -0.5)
    dn_conv_w = nrm(ks[12], (DEPTH, DN_CONV, 2 * DN_QK_WIDTH + DN_V_WIDTH), DN_CONV ** -0.5)
    dn_a_log = jnp.log(jax.random.uniform(ks[13], (DEPTH, DN_HEADS), f32, 1.0, 16.0))
    dn_dt = jnp.exp(jax.random.uniform(ks[14], (DEPTH, DN_HEADS), f32, math.log(DN_DT_MIN), math.log(DN_DT_MAX)))
    dn_dt_bias = dn_dt + jnp.log(-jnp.expm1(-dn_dt))
    dn_norm_w = 1.0 + nrm(ks[15], (DEPTH, DN_DV), 0.02)
    dn_proj_w = nrm(ks[16], (DEPTH, DN_V_WIDTH, D_MODEL), DN_V_WIDTH ** -0.5)
    w_out = nrm(ks[17], (DEPTH, D_MODEL, D_MODEL), D_MODEL ** -0.5)
    ffn_norm_w = 1.0 + nrm(ks[18], (DEPTH, D_MODEL), 0.02)
    ffn_up = nrm(ks[19], (DEPTH, D_MODEL, 2 * FFN_DIM), D_MODEL ** -0.5)
    ffn_conv_w = nrm(ks[20], (DEPTH, FFN_CONV, 2 * FFN_DIM), FFN_CONV ** -0.5)
    ffn_down = nrm(ks[21], (DEPTH, FFN_DIM, D_MODEL), FFN_DIM ** -0.5)
    final_norm_w = 1.0 + nrm(ks[22], (D_MODEL,), 0.02)
    return {"x": x, "mix_norm_w": mix_norm_w, "w_in": w_in, "s5_log_dt": s5_log_dt,
            "s5_a_re": s5_a_re, "s5_a_im": s5_a_im, "s5_b_re": s5_b_re, "s5_b_im": s5_b_im,
            "s5_c_re": s5_c_re, "s5_c_im": s5_c_im, "s5_d": s5_d, "s5_glu_w": s5_glu_w,
            "dn_conv_w": dn_conv_w, "dn_a_log": dn_a_log, "dn_dt_bias": dn_dt_bias,
            "dn_norm_w": dn_norm_w, "dn_proj_w": dn_proj_w, "w_out": w_out,
            "ffn_norm_w": ffn_norm_w, "ffn_up": ffn_up, "ffn_conv_w": ffn_conv_w,
            "ffn_down": ffn_down, "final_norm_w": final_norm_w}

def first_block(x, mix_norm_w, w_in, s5_log_dt, s5_a_re, s5_a_im, s5_b_re, s5_b_im,
              s5_c_re, s5_c_im, s5_d, s5_glu_w, dn_conv_w, dn_a_log, dn_dt_bias,
              dn_norm_w, dn_proj_w, w_out, ffn_norm_w, ffn_up, ffn_conv_w, ffn_down,
              final_norm_w):
    for l in range(DEPTH):
        h = rmsnorm(x, mix_norm_w[l])
        proj = jnp.einsum("bld,de->ble", h, w_in[l])
        u, qkv, z, b_raw, a_raw, g_s5, g_dn = jnp.split(proj, SPLITS, axis=-1)
        y_s5 = s5_branch(u, s5_log_dt[l], s5_a_re[l], s5_a_im[l], s5_b_re[l], s5_b_im[l],
                         s5_c_re[l], s5_c_im[l], s5_d[l])
        glu_a, glu_b = jnp.split(jnp.einsum("blc,ce->ble", y_s5, s5_glu_w[l]), 2, axis=-1)
        br_s5 = glu_a * jax.nn.sigmoid(glu_b)
        y_dn = deltanet_branch(qkv, z, b_raw, a_raw, dn_conv_w[l], dn_a_log[l], dn_dt_bias[l], dn_norm_w[l])
        br_dn = jnp.einsum("blc,cd->bld", y_dn, dn_proj_w[l])
        merged = jax.nn.sigmoid(g_s5) * br_s5 + jax.nn.sigmoid(g_dn) * br_dn
        x = x + jnp.einsum("bld,de->ble", merged, w_out[l])
        h = rmsnorm(x, ffn_norm_w[l])
        up = causal_dwconv(jnp.einsum("bld,df->blf", h, ffn_up[l]), ffn_conv_w[l])
        act, val = jnp.split(up, 2, axis=-1)
        x = x + jnp.einsum("blf,fd->bld", jax.nn.silu(act) * val, ffn_down[l])
    return rmsnorm(x, final_norm_w)


GRID_W = 64
CTX_LEN = 256
D_MIX = D_MODEL
D_ATTN = D_MIX // 2
D_RWKV = D_MIX - D_ATTN
HEAD_DIM = 64
N_HEADS_A = D_ATTN // HEAD_DIM
N_KV_HEADS = 4
GQA_GROUP = N_HEADS_A // N_KV_HEADS
WINDOW = 128
BLOCK = 128
BAND = BLOCK + 2 * WINDOW
ROPE_BASE = 10000.0
RWKV_HEAD = 64
N_HEADS_R = D_RWKV // RWKV_HEAD
D_DECAY_LORA = max(32, int(round(1.8 * D_RWKV ** 0.5 / 32)) * 32)
D_AAA_LORA = max(32, int(round(1.8 * D_RWKV ** 0.5 / 32)) * 32)
D_GATE_LORA = max(32, int(round(0.6 * D_RWKV ** 0.8 / 32)) * 32)
D_FF = -(-(8 * D_MODEL) // (3 * 256)) * 256
LNX_EPS = 64e-5
MASK_VALUE = -1e30
ATTN_SPLITS = (D_ATTN, N_KV_HEADS * HEAD_DIM, N_KV_HEADS * HEAD_DIM)
RWKV_SPLITS = (D_RWKV, D_RWKV, D_RWKV, D_DECAY_LORA, D_DECAY_LORA, D_AAA_LORA, D_AAA_LORA, D_GATE_LORA)
D_IN_ATTN = sum(ATTN_SPLITS)
D_IN_RWKV = sum(RWKV_SPLITS)
D_IN = D_IN_ATTN + D_IN_RWKV
F32 = jnp.float32


def _split(z, sizes):
    return jnp.split(z, [int(s) for s in np.cumsum(sizes)[:-1]], axis=-1)

def rmsnorm_2(x, g):
    xf = x.astype(F32)
    y = xf * lax.rsqrt(jnp.mean(xf * xf, axis=-1, keepdims=True) + NORM_EPS)
    return (y * g.astype(F32)).astype(x.dtype)

def modulate(h, shift, scale):
    return h * (1 + scale) + shift

def swiglu(h, w1, w3, w2):
    return (jax.nn.silu(h @ w1) * (h @ w3)) @ w2

def axial_rope(x, row, col):
    half = HEAD_DIM // 2
    nf = half // 2
    freqs = 1.0 / (ROPE_BASE ** (jnp.arange(nf, dtype=F32) / nf))

    def rot(xa, pos):
        ang = pos.astype(F32)[:, None] * freqs[None, :]
        cos = jnp.cos(ang)[None, :, None, :]
        sin = jnp.sin(ang)[None, :, None, :]
        x1, x2 = xa[..., :nf], xa[..., nf:]
        return jnp.concatenate([x1 * cos - x2 * sin, x2 * cos + x1 * sin], axis=-1)

    xf = x.astype(F32)
    return jnp.concatenate([rot(xf[..., :half], row), rot(xf[..., half:], col)], axis=-1).astype(x.dtype)

def sink_softmax(s, sink_hg):
    sk = sink_hg[None, :, :, None, None]
    m = jnp.maximum(jnp.max(s, axis=-1, keepdims=True), sk)
    p = jnp.exp(s - m)
    return p / (jnp.sum(p, axis=-1, keepdims=True) + jnp.exp(sk - m))

def windowed_gqa(q, k, v, k_ctx, v_ctx, sink):
    B, T = q.shape[0], q.shape[1]
    nb = T // BLOCK
    scale = HEAD_DIM ** -0.5
    qb = (q.astype(F32) * scale).reshape(B, nb, BLOCK, N_KV_HEADS, GQA_GROUP, HEAD_DIM)
    qb = qb.transpose(1, 0, 2, 3, 4, 5)
    pad = ((0, 0), (WINDOW, WINDOW), (0, 0), (0, 0))
    kp = jnp.pad(k.astype(F32), pad)
    vp = jnp.pad(v.astype(F32), pad)
    kc = k_ctx.astype(F32)
    vc = v_ctx.astype(F32)
    sink_hg = sink.astype(F32).reshape(N_KV_HEADS, GQA_GROUP)
    offs_q = jnp.arange(BLOCK)
    offs_k = jnp.arange(BAND) - WINDOW
    in_window = jnp.abs(offs_q[:, None] - offs_k[None, :]) <= WINDOW

    def one_block(args):
        qi, bi = args
        start = bi * BLOCK
        kb = lax.dynamic_slice_in_dim(kp, start, BAND, axis=1)
        vb = lax.dynamic_slice_in_dim(vp, start, BAND, axis=1)
        kpos = start + offs_k
        valid = in_window & ((kpos >= 0) & (kpos < T))[None, :]
        s_band = jnp.where(valid, jnp.einsum('bqhgd,bkhd->bhgqk', qi, kb), MASK_VALUE)
        s_ctx = jnp.einsum('bqhgd,bkhd->bhgqk', qi, kc)
        p = sink_softmax(jnp.concatenate([s_band, s_ctx], axis=-1), sink_hg)
        return jnp.einsum('bhgqk,bkhd->bqhgd', p, jnp.concatenate([vb, vc], axis=1))

    out = lax.map(one_block, (qb, jnp.arange(nb)))
    return out.transpose(1, 0, 2, 3, 4, 5).reshape(B, T, D_ATTN).astype(q.dtype)

def context_gqa(q, k, v, sink):
    B, C = q.shape[0], q.shape[1]
    qf = (q.astype(F32) * HEAD_DIM ** -0.5).reshape(B, C, N_KV_HEADS, GQA_GROUP, HEAD_DIM)
    s = jnp.einsum('bqhgd,bkhd->bhgqk', qf, k.astype(F32))
    p = sink_softmax(s, sink.astype(F32).reshape(N_KV_HEADS, GQA_GROUP))
    return jnp.einsum('bhgqk,bkhd->bqhgd', p, v.astype(F32)).reshape(B, C, D_ATTN).astype(q.dtype)

def token_shift(h, mu_prev, mu_next):
    prev = jnp.pad(h, ((0, 0), (1, 0), (0, 0)))[:, :-1]
    nxt = jnp.pad(h, ((0, 0), (0, 1), (0, 0)))[:, 1:]
    return h + mu_prev * (prev - h) + mu_next * (nxt - h)

def _heads(t):
    return t.reshape(t.shape[0], t.shape[1], N_HEADS_R, RWKV_HEAD)

def rwkv_prepare(z, mu_prev, mu_next, w0, w_up, a0, a_up, k_k, k_a, g_up):
    zs = token_shift(z.astype(F32), mu_prev, mu_next)
    r, k, v, wdf, wdb, adf, adb, gd = _split(zs, RWKV_SPLITS)
    kk = _heads(k * k_k)
    kk = kk * lax.rsqrt(jnp.maximum(jnp.sum(kk * kk, axis=-1, keepdims=True), 1e-12))
    dirs = []
    for d, (wd, ad) in enumerate(((wdf, adf), (wdb, adb))):
        wlog = -jax.nn.softplus(-(w0[d] + jnp.tanh(wd) @ w_up[d])) - 0.5
        decay = jnp.exp(-jnp.exp(wlog))
        a = jax.nn.sigmoid(a0[d] + ad @ a_up[d])
        kd = k * (1 + (a - 1) * k_a)
        dirs.append((_heads(decay), _heads(kd), _heads(a)))
    gate = jax.nn.sigmoid(gd) @ g_up
    return _heads(r), _heads(v), kk, dirs, gate

def wkv_scan(state0, r, w, k, v, kk, a, reverse):
    tm = lambda t: jnp.swapaxes(t, 0, 1)
    xs = (tm(r), tm(w), tm(k), tm(v), tm(-kk), tm(kk * a))

    def step(S, inp):
        r_t, w_t, k_t, v_t, nkk_t, b_t = inp
        sa = jnp.einsum('bhvk,bhk->bhv', S, nkk_t)
        S = S * w_t[:, :, None, :] + sa[..., None] * b_t[:, :, None, :] + v_t[..., None] * k_t[:, :, None, :]
        return S, jnp.einsum('bhvk,bhk->bhv', S, r_t)

    S_final, ys = lax.scan(step, state0, xs, reverse=reverse)
    return S_final, jnp.swapaxes(ys, 0, 1)

def rwkv_output(y, r, v, dirs, gate, r_k, lnx_g, lnx_b):
    B, T = y.shape[0], y.shape[1]
    mean = jnp.mean(y, axis=-1, keepdims=True)
    var = jnp.mean(jnp.square(y - mean), axis=-1, keepdims=True)
    yn = ((y - mean) * lax.rsqrt(var + LNX_EPS)).reshape(B, T, D_RWKV) * lnx_g + lnx_b
    rk = r_k.reshape(N_HEADS_R, RWKV_HEAD)
    bonus = sum(jnp.sum(r * kd * rk, axis=-1, keepdims=True) * v for _, kd, _ in dirs)
    return (yn + bonus.reshape(B, T, D_RWKV)) * gate

def hybrid_layer(x, xc, c, c_ctx, row, col, ada_w, ada_b, norm1_g, norm2_g, w_in, attn_sink,
                 ts_prev, ts_next, w0, w_up, a0, a_up, k_k, k_a, r_k, g_up, lnx_g, lnx_b,
                 w_out, ffn_w1, ffn_w3, ffn_w2, update_ctx):
    B, T = x.shape[0], x.shape[1]
    C = xc.shape[1]
    mod = jax.nn.silu(c) @ ada_w + ada_b
    mod_c = jax.nn.silu(c_ctx) @ ada_w + ada_b
    sh1, sc1, g1, sh2, sc2, g2 = jnp.split(mod[:, None, :], 6, axis=-1)
    sh1c, sc1c, g1c, sh2c, sc2c, g2c = jnp.split(mod_c, 6, axis=-1)

    z = modulate(rmsnorm_2(x, norm1_g), sh1, sc1) @ w_in
    zc = modulate(rmsnorm_2(xc, norm1_g), sh1c, sc1c) @ w_in
    za, zr = z[..., :D_IN_ATTN], z[..., D_IN_ATTN:]
    zca, zcr = zc[..., :D_IN_ATTN], zc[..., D_IN_ATTN:]

    q, k, v = _split(za, ATTN_SPLITS)
    q = axial_rope(q.reshape(B, T, N_HEADS_A, HEAD_DIM), row, col)
    k = axial_rope(k.reshape(B, T, N_KV_HEADS, HEAD_DIM), row, col)
    v = v.reshape(B, T, N_KV_HEADS, HEAD_DIM)
    qc, kc, vc = _split(zca, ATTN_SPLITS)
    kc = kc.reshape(B, C, N_KV_HEADS, HEAD_DIM)
    vc = vc.reshape(B, C, N_KV_HEADS, HEAD_DIM)
    attn = windowed_gqa(q, k, v, kc, vc, attn_sink)

    rw_args = (ts_prev, ts_next, w0, w_up, a0, a_up, k_k, k_a, g_up)
    r, vr, kk, dirs, gate = rwkv_prepare(zr, *rw_args)
    rc, vrc, kkc, dirsc, gatec = rwkv_prepare(zcr, *rw_args)
    S0 = jnp.zeros((B, N_HEADS_R, RWKV_HEAD, RWKV_HEAD), F32)
    y_lat = jnp.zeros_like(r)
    yc_dirs = []
    for d in range(2):
        rev = d == 1
        wd, kd, ad = dirs[d]
        wdc, kdc, adc = dirsc[d]
        Sc, yc_d = wkv_scan(S0, rc, wdc, kdc, vrc, kkc, adc, rev)
        _, y_d = wkv_scan(Sc, r, wd, kd, vr, kk, ad, rev)
        y_lat = y_lat + y_d
        yc_dirs.append(yc_d)
    rw = rwkv_output(y_lat, r, vr, dirs, gate, r_k, lnx_g, lnx_b).astype(x.dtype)

    x = x + g1 * (jnp.concatenate([attn, rw], axis=-1) @ w_out)
    x = x + g2 * swiglu(modulate(rmsnorm_2(x, norm2_g), sh2, sc2), ffn_w1, ffn_w3, ffn_w2)

    if update_ctx:
        attn_c = context_gqa(qc.reshape(B, C, N_HEADS_A, HEAD_DIM), kc, vc, attn_sink)
        rw_c = rwkv_output(yc_dirs[0] + yc_dirs[1], rc, vrc, dirsc, gatec, r_k, lnx_g, lnx_b).astype(xc.dtype)
        xc = xc + g1c * (jnp.concatenate([attn_c, rw_c], axis=-1) @ w_out)
        xc = xc + g2c * swiglu(modulate(rmsnorm_2(xc, norm2_g), sh2c, sc2c), ffn_w1, ffn_w3, ffn_w2)
    return x, xc

def second_inputs(seed: int = 0) -> dict:
    key = jax.random.key(seed)
    ks = jax.random.split(key, 27)
    nrm = lambda k, shape, s: jax.random.normal(k, shape, jnp.float32) * s
    uni = lambda k, shape, lo, hi: jax.random.uniform(k, shape, jnp.float32, lo, hi)
    L = DEPTH
    return {
        'x': nrm(ks[0], (BATCH, SEQ, D_MODEL), 1.0),
        'c': nrm(ks[1], (BATCH, D_MODEL), 1.0),
        'ctx': nrm(ks[2], (BATCH, CTX_LEN, D_MODEL), 1.0),
        'c_ctx': nrm(ks[3], (D_MODEL,), 1.0),
        'ada_w': nrm(ks[4], (L, D_MODEL, 6 * D_MODEL), 0.5 * D_MODEL ** -0.5),
        'ada_b': nrm(ks[5], (L, 6 * D_MODEL), 0.02),
        'norm1_g': 1.0 + nrm(ks[6], (L, D_MODEL), 0.05),
        'norm2_g': 1.0 + nrm(ks[7], (L, D_MODEL), 0.05),
        'w_in': nrm(ks[8], (L, D_MODEL, D_IN), D_MODEL ** -0.5),
        'attn_sink': nrm(ks[9], (L, N_HEADS_A), 0.5),
        'ts_prev': uni(ks[10], (L, D_IN_RWKV), 0.0, 0.5),
        'ts_next': uni(ks[11], (L, D_IN_RWKV), 0.0, 0.5),
        'w0': uni(ks[12], (L, 2, D_RWKV), -4.0, 1.0),
        'w_up': nrm(ks[13], (L, 2, D_DECAY_LORA, D_RWKV), 0.1),
        'a0': nrm(ks[14], (L, 2, D_RWKV), 0.5),
        'a_up': nrm(ks[15], (L, 2, D_AAA_LORA, D_RWKV), 0.1),
        'k_k': 0.85 + nrm(ks[16], (L, D_RWKV), 0.05),
        'k_a': 1.0 + nrm(ks[17], (L, D_RWKV), 0.05),
        'r_k': nrm(ks[18], (L, D_RWKV), 0.1),
        'g_up': nrm(ks[19], (L, D_GATE_LORA, D_RWKV), D_GATE_LORA ** -0.5),
        'lnx_g': 1.0 + nrm(ks[20], (L, D_RWKV), 0.05),
        'lnx_b': nrm(ks[21], (L, D_RWKV), 0.02),
        'w_out': nrm(ks[22], (L, D_MIX, D_MODEL), D_MIX ** -0.5),
        'ffn_w1': nrm(ks[23], (L, D_MODEL, D_FF), D_MODEL ** -0.5),
        'ffn_w3': nrm(ks[24], (L, D_MODEL, D_FF), D_MODEL ** -0.5),
        'ffn_w2': nrm(ks[25], (L, D_FF, D_MODEL), D_FF ** -0.5),
        'final_norm_g': 1.0 + nrm(ks[26], (D_MODEL,), 0.05),
    }

def second_block(x, c, ctx, c_ctx, ada_w, ada_b, norm1_g, norm2_g, w_in, attn_sink, ts_prev, ts_next,
              w0, w_up, a0, a_up, k_k, k_a, r_k, g_up, lnx_g, lnx_b, w_out, ffn_w1, ffn_w3, ffn_w2,
              final_norm_g):
    seq_len = x.shape[1]
    rows = seq_len // GRID_W
    row = jnp.repeat(jnp.arange(rows, dtype=jnp.int32), GRID_W)
    col = jnp.tile(jnp.arange(GRID_W, dtype=jnp.int32), rows)
    xc = ctx
    for i in range(DEPTH):
        x, xc = hybrid_layer(x, xc, c, c_ctx, row, col, ada_w[i], ada_b[i], norm1_g[i], norm2_g[i],
                             w_in[i], attn_sink[i], ts_prev[i], ts_next[i], w0[i], w_up[i], a0[i],
                             a_up[i], k_k[i], k_a[i], r_k[i], g_up[i], lnx_g[i], lnx_b[i], w_out[i],
                             ffn_w1[i], ffn_w3[i], ffn_w2[i], update_ctx=(i < DEPTH - 1))
    return rmsnorm_2(x, final_norm_g)


def setup_inputs(seed=0):
    out = dict(first_inputs(seed))
    for name, value in second_inputs(seed + 1).items():
        if name != "x":
            out[name + "_2"] = value
    return out


def reference(
    x, mix_norm_w, w_in, s5_log_dt, s5_a_re, s5_a_im, s5_b_re, s5_b_im, s5_c_re, s5_c_im, s5_d,
    s5_glu_w, dn_conv_w, dn_a_log, dn_dt_bias, dn_norm_w, dn_proj_w, w_out, ffn_norm_w, ffn_up,
    ffn_conv_w, ffn_down, final_norm_w, c_2, ctx_2, c_ctx_2, ada_w_2, ada_b_2, norm1_g_2,
    norm2_g_2, w_in_2, attn_sink_2, ts_prev_2, ts_next_2, w0_2, w_up_2, a0_2, a_up_2, k_k_2,
    k_a_2, r_k_2, g_up_2, lnx_g_2, lnx_b_2, w_out_2, ffn_w1_2, ffn_w3_2, ffn_w2_2,
    final_norm_g_2,
):
    x = first_block(
        x, mix_norm_w, w_in, s5_log_dt, s5_a_re, s5_a_im, s5_b_re, s5_b_im, s5_c_re, s5_c_im,
        s5_d, s5_glu_w, dn_conv_w, dn_a_log, dn_dt_bias, dn_norm_w, dn_proj_w, w_out,
        ffn_norm_w, ffn_up, ffn_conv_w, ffn_down, final_norm_w,
    )
    return second_block(
        x, c_2, ctx_2, c_ctx_2, ada_w_2, ada_b_2, norm1_g_2, norm2_g_2, w_in_2, attn_sink_2,
        ts_prev_2, ts_next_2, w0_2, w_up_2, a0_2, a_up_2, k_k_2, k_a_2, r_k_2, g_up_2, lnx_g_2,
        lnx_b_2, w_out_2, ffn_w1_2, ffn_w3_2, ffn_w2_2, final_norm_g_2,
    )


_drawn_inputs = setup_inputs


def setup_inputs(seed=0):
    import zlib

    import numpy as np

    out = dict(_drawn_inputs(seed))
    spreads = {}
    factors = {'mix_norm_w': 4.271,
     's5_log_dt': 38.352,
     's5_a_re': 64.0,
     's5_a_im': 38.128,
     's5_b_re': 52.584,
     's5_b_im': 54.912,
     's5_c_re': 53.32,
     's5_c_im': 53.736,
     'dn_norm_w': 8.0,
     'ffn_norm_w': 3.855,
     'final_norm_w': 2.742,
     'ada_b_2': 2.781,
     'norm1_g_2': 5.249,
     'norm2_g_2': 26.113,
     'attn_sink_2': 8.0,
     'w_up_2': 13.557,
     'k_k_2': 200.0,
     'k_a_2': 5.173,
     'lnx_g_2': 172.43,
     'lnx_b_2': 200.0,
     'w0_2': 3.664}
    for name, (base, spread) in spreads.items():
        noise = np.random.default_rng([zlib.crc32(name.encode()), seed]).standard_normal(out[name].shape)
        drawn = base * np.exp(spread * noise) if base else spread * noise
        out[name] = jnp.asarray(drawn.astype(out[name].dtype))
    for name, factor in factors.items():
        out[name] = (out[name] * factor).astype(out[name].dtype)
    return out
```

```python
import concourse.bass as bass
from concourse import mybir
from contextlib import ExitStack, contextmanager
import numpy as np

F32 = mybir.dt.float32
F32R = mybir.dt.float32r
U32 = mybir.dt.uint32
ALU = mybir.AluOpType
ACT = mybir.ActivationFunctionType
AX = mybir.AxisListType
ds = bass.ds

P = 128
T = 256
D = 2048
KD = D // P
FFN = 5632
KF = FFN // P
EPS = 1e-6
S5_TILES = 32
HEADS = 8
C = 64
NCH = T // C
PIECE = 8
PW = PIECE * P
LOOK = 3
KB = 1024
MAGIC = 12582912.0
TWO_PI = 6.283185307179586
DECAY = float(np.float32(np.exp(-0.5)))
PI_IN = 3.1415925


class Steps:

    def __init__(self, sem, names):
        self.sem, self.names, self.k = sem, names, 0

    def did(self, name):
        assert self.names[self.k % len(self.names)] == name, (self.names[self.k % len(self.names)], name)
        self.k += 1
        return self.sem

    def at(self, i, name):
        return self.sem, i * len(self.names) + (self.names.index(name) + 1)

    def before(self, i, bodies=1):
        return self.sem, i * (bodies * len(self.names))


PHASES = [("w_in", 18), ("glu", 4), ("dn_proj", 2), ("w_out", 4), ("ffn_up", 22), ("ffn_down", 12),
          ("w_in2", 10), ("w_out2", 4), ("ffn_up2", 22), ("ffn_down2", 12)]
ROUND0, _r = {}, 0
for _n, _c in PHASES:
    ROUND0[_n] = _r
    _r += _c
ROUNDS = _r
OUTS = {"w_in": 72, "glu": 32, "dn_proj": 16, "w_out": 16, "ffn_up": 88, "ffn_down": 16,
        "w_in2": 40, "w_out2": 16, "ffn_up2": 88, "ffn_down2": 16}
TURN0, _t = {}, 0
for _n, _c in PHASES:
    TURN0[_n] = _t
    _t += OUTS[_n] // 4
TURN0["end"] = _t

PARAMS = [("mix_norm", 16), ("ffn_norm", 16), ("final_norm", 16), ("a_re", 32), ("a_im", 32),
          ("log_dt", 32), ("s5_d", 8), ("conv", 96), ("dn_norm", 1), ("a_log", 1), ("dt_bias", 1),
          ("ffn_conv", 264), ("ada_b", 96), ("norm1", 16), ("norm2", 16), ("final2", 16),
          ("sink", 16), ("ts_prev", 28), ("ts_next", 28), ("w0", 16), ("a0", 16), ("k_k", 8),
          ("k_a", 8), ("r_k", 8), ("lnx_g", 8), ("lnx_b", 8)]
COL, _c0 = {}, 0
for _n, _c in PARAMS:
    COL[_n] = _c0
    _c0 += _c
NPAR = _c0


def program(nc, d):
    ctx = ExitStack()
    with ctx:
        base = (nc.sbuf_base + 63) // 64 * 64

        def sb(name, shape, offset, dt=F32):
            return nc.alloc_sbuf_tensor_at(name, [P] + list(shape), dt, offset=base + int(offset * KB))

        def sem(name):
            return ctx.enter_context(nc.semaphore(name))

        def steps(name, names):
            return Steps(sem(name), names.split())

        x = sb("x", [KD, T], 0)
        raw = sb("raw", [4, 2 * PW], 16)
        w_hi = sb("w_hi", [4, PW], 48, F32R)
        w_lo = sb("w_lo", [4, PW], 64, F32R)
        par = sb("par", [NPAR], 80)
        ident = sb("ident", [P], 83.5)
        ones = sb("ones", [P], 84)
        rstd = sb("rstd", [T], 84.5)
        var = sb("var", [T], 85.5)
        conv_a = sb("conv_a", [T], 84.5)
        conv_v = sb("conv_v", [T], 85.5)
        mod = sb("mod", [96], 86.5)
        modc = sb("modc", [32], 86.875)
        cv = sb("cv", [KD, 2], 87)
        cve = sb("cve", [KD, 2], 87.125)
        nscale = sb("nscale", [2, KD], 87.25)
        H0, A0, TMP = 87.75, 119.75, 191.75
        h_hi = sb("h_hi", [KD, T], H0, F32R)
        h_lo = sb("h_lo", [KD, T], H0 + 16, F32R)
        hf = sb("hf", [KD, T], TMP)

        def pcol(name, n=0, width=1):
            return par[:, COL[name] + n:COL[name] + n + width]

        gates = sb("gates", [2 * KD, T], A0)
        w_ab = sb("w_ab", [KD, 16], A0)
        qkv = sb("qkv", [24, T], A0 + 32)
        u = sb("u", [8, T], A0 + 56)
        z = sb("z", [8, T], A0 + 64)
        cacc = sb("cacc", [4, T], TMP)
        graw = sb("graw", [2, T], 84.5)
        sg = sb("sg", [2, T], TMP)
        s_bt = sb("s_bt", [2, P], H0)
        s_ct = sb("s_ct", [4, 2, 32], H0 + 1)
        s_cp = sb("s_cp", [2, 4, P], H0 + 2)
        s_u = sb("s_u", [T], H0 + 6)
        s_cos = sb("s_cos", [2, T], H0 + 7)
        s_sin = sb("s_sin", [2, 2, T], H0 + 9)
        s_hs = sb("s_hs", [T], H0 + 13)
        s_fr = sb("s_fr", [2, T], H0 + 14)
        s_rd = sb("s_rd", [T], H0 + 16)
        s_v = sb("s_v", [2, T], H0 + 17)
        s_p = sb("s_p", [2, T], H0 + 19)
        s_z = sb("s_z", [2, T], H0 + 21)
        s_x = sb("s_x", [2, 2, T], H0 + 23)
        s_y = sb("s_y", [T], H0 + 27)
        s_w = sb("s_w", [12, S5_TILES], H0 + 28)
        s_c1 = sb("s_c1", [4, 2, 32], H0 + 29.5)
        s_io = sb("s_io", [T], H0 + 30.5)
        d_sq = sb("d_sq", [2, T], H0)
        d_rn = sb("d_rn", [2, T], H0 + 2)
        d_rows = sb("d_rows", [3, T], H0 + 4)
        d_g = sb("d_g", [2, T], H0 + 7)
        d_cols = sb("d_cols", [2, 3, 8], H0 + 9)
        d_sel = sb("d_sel", [2, 3, T], H0 + 9.25)
        d_k = sb("d_k", [2, T], H0 + 15.25)
        d_q = sb("d_q", [2, T], H0 + 17.25)
        d_v = sb("d_v", [2, T], H0 + 19.25)
        d_kg = sb("d_kg", [2, T], H0 + 21.25)
        d_qg = sb("d_qg", [2, T], H0 + 23.25)
        d_kd = sb("d_kd", [4, P], H0 + 25.25)
        d_bv = sb("d_bv", [4, P], H0 + 27.25)
        d_at = sb("d_at", [4, P], H0 + 29.25)
        d_el = sb("d_el", [2, NCH], H0 + 31.25)
        i_a = sb("i_a", [4, P], TMP)
        i_t = sb("i_t", [4, P], TMP + 2)
        i_tt = sb("i_tt", [4, P], TMP + 4)
        i_p = sb("i_p", [4, P], TMP + 6)
        d_s = sb("d_s", [2, P], TMP + 8)
        d_ur = sb("d_ur", [2, P], TMP + 9)
        d_vn = sb("d_vn", [2, P], TMP + 10)
        masks = sb("masks", [8, P], TMP + 11)
        d_e1 = sb("d_e1", [4, P], H0)
        d_kb = sb("d_kb", [2, T], H0 + 2)
        ys_hi = sb("ys_hi", [8, T], H0, F32R)
        ys_lo = sb("ys_lo", [8, T], H0 + 8, F32R)
        yd_hi = sb("yd_hi", [8, T], H0 + 16, F32R)
        yd_lo = sb("yd_lo", [8, T], H0 + 24, F32R)
        m_hi = sb("m_hi", [KD, T], A0 + 32, F32R)
        m_lo = sb("m_lo", [KD, T], A0 + 48, F32R)
        f_hi = sb("f_hi", [KF, T], A0, F32R)
        f_lo = sb("f_lo", [KF, T], A0 + 44, F32R)

        po = [ctx.enter_context(nc.psum_tensor(f"po{n}", [P, 512], F32)) for n in range(4)]
        pa = [ctx.enter_context(nc.psum_tensor(f"pa{n}", [P, 512], F32)) for n in range(4)]

        par_in = sem("par_in")
        settled = sem("settled")
        x_in = sem("x_in")
        landed = [sem(f"landed{n}") for n in range(4)]
        hi_ready, lo_ready, used = sem("hi_ready"), sem("lo_ready"), sem("used")
        free = [sem(f"free{n}") for n in range(4)]
        out_done = sem("out_done")
        na = steps("na", "sq0 sq1 sq2 sq3 sqrt")
        nv = steps("nv", "var rec h")
        np_ = steps("np_", "sum")
        sa = steps("split_act", "hi0 hi1 hi2 hi3")
        sv = steps("split_dve", "lo0 lo1 lo2 lo3")
        ab_in, ab_done, ab_read = sem("ab_in"), sem("ab_done"), sem("ab_read")
        conv_read = sem("conv_read")
        dv = sem("dve_chain")
        cc = [0]

        def load_round(sp, src, rnd, n, first=False):
            for c in range(4):
                if not first:
                    sp.wait_ge(hi_ready, rnd * 8 + (2 * c + 2 - 8))
                    sp.wait_ge(lo_ready, rnd * 8 + (2 * c + 2 - 8))
                sp.dma_start(raw[:, c, :], src(n, c)).then_inc(landed[c], 16)

        def split_hi(act, rnd, k, width=PW):
            if k >= 8:
                rnd, k = rnd + 1, k - 8
            if k % 2 == 0:
                act.wait_ge(landed[k // 2], rnd * 16 + 16)
            act.wait_ge(used, rnd * 8 + k - 3)
            act.activation(w_hi[:, k % 4, 0:width], raw[:, k // 2, (k % 2) * PW:(k % 2) * PW + width],
                           ACT.Copy).then_inc(hi_ready, 1)

        def split_lo(dve, rnd, k, width=PW):
            if k >= 8:
                rnd, k = rnd + 1, k - 8
            dve.wait_ge(hi_ready, rnd * 8 + k + 1)
            dve.tensor_tensor(w_lo[:, k % 4, 0:width], raw[:, k // 2, (k % 2) * PW:(k % 2) * PW + width],
                              w_hi[:, k % 4, 0:width].bitcast(F32), ALU.subtract).then_inc(lo_ready, 1)

        def products(pe, rnd, k, tiles, bank, act_hi, act_lo, first, last, turn=None):
            if turn is not None:
                pe.wait_ge(free[bank], turn)
            pe.wait_ge(lo_ready, rnd * 8 + k + 1)
            for n, (s, t) in enumerate(tiles):
                hi = w_hi[:, k % 4, s * P:s * P + P]
                lo = w_lo[:, k % 4, s * P:s * P + P]
                end = last and n == len(tiles) - 1
                pe.matmul(po[bank][:, 0:T], lo, act_hi[:, t, :], start=first and n == 0, stop=False)
                pe.matmul(po[bank][:, 0:T], hi, act_lo[:, t, :], start=False, stop=False)
                mm = pe.matmul(po[bank][:, 0:T], hi, act_hi[:, t, :], start=False, stop=end)
            return mm

        def project(pe, phase, rounds, act_hi, act_lo, k_tiles, r_off=0, t_off=0):
            per = 8 if k_tiles == 8 else 4
            with pe.Fori(0, rounds) as i:
                rnd = i + (ROUND0[phase] + r_off)
                for k in range(8):
                    o = k if k_tiles == 8 else k // 2
                    half = 0 if k_tiles == 8 else k % 2
                    turn = None
                    if half == 0:
                        turn = i * (per // 4) + (TURN0[phase] + t_off + o // 4)
                    products(pe, rnd, k, [(s, half * 8 + s) for s in range(8)], o % 4, act_hi, act_lo,
                             half == 0, half == 1 or k_tiles == 8, turn).then_inc(used, 1)

        def project_down(pe, phase):
            with pe.Fori(0, 4) as i:
                for q in range(24):
                    rnd, k, o, s = i * 3 + (ROUND0[phase] + q // 8), q % 8, q // 6, q % 6
                    tiles = [(t, s * 8 + t) for t in range(8 if s < 5 else 4)]
                    products(pe, rnd, k, tiles, o, f_hi, f_lo, s == 0, s == 5,
                             i + TURN0[phase] if s == 0 else None).then_inc(used, 1)

        def down_width(q):
            return PW // 2 if q % 6 == 5 else PW

        def norm_act(act, n, x=x):
            for q in range(4):
                act.activation(hf[:, 4 * q:4 * q + 4, :], x[:, 4 * q:4 * q + 4, :], ACT.Square)\
                   .then_inc(na.did(f"sq{q}"), 1)
            act.wait_ge(*nv.at(n, "var"))
            act.activation(rstd[:], var[:], ACT.Sqrt).then_inc(na.did("sqrt"), 1)

        def norm_pe(pe, n):
            for q in range(4):
                pe.wait_ge(*na.at(n, f"sq{q}"))
                for t in range(4 * q, 4 * q + 4):
                    mm = pe.matmul(pa[0][:, 0:T], ones[:], hf[:, t, :], start=t == 0, stop=t == KD - 1)
            mm.then_inc(np_.did("sum"), 1)

        def norm_dve(dve, n, w, out, shift=None, x=x):
            dve.wait_ge(*np_.at(n, "sum"))
            dve.tensor_scalar(var[:], pa[0][:, 0:T], 1.0 / D, EPS, ALU.mult, ALU.add)\
               .then_inc(nv.did("var"), 1)
            dve.wait_ge(*na.at(n, "sqrt"))
            dve.reciprocal(rstd[:], rstd[:]).then_inc(nv.did("rec"), 1)
            dve.wait_ge(*nv.at(n, "rec"))
            for t in range(KD):
                last = dve.scalar_tensor_tensor(out[:, t, :], x[:, t, :], w(t), rstd[:], ALU.mult, ALU.mult)
                if shift is not None:
                    last.then_inc(dv, 1)
            if shift is not None:
                cc[0] += KD
                dve.wait_ge(dv, cc[0])
                for t in range(KD):
                    last = dve.tensor_scalar(out[:, t, :], out[:, t, :], shift(t), None, ALU.add)
            last.then_inc(nv.did("h"), 1)

        def split_act(act, m, out_hi, src, tiles=4):
            for q in range(4):
                act.activation(out_hi[:, tiles * q:tiles * (q + 1), :], src[:, tiles * q:tiles * (q + 1), :],
                               ACT.Copy).then_inc(sa.did(f"hi{q}"), 1)

        def split_dve(dve, m, out_lo, out_hi, src, tiles=4):
            for q in range(4):
                s = slice(tiles * q, tiles * (q + 1))
                dve.wait_ge(*sa.at(m, f"hi{q}"))
                dve.tensor_tensor(out_lo[:, s, :], src[:, s, :], out_hi[:, s, :].bitcast(F32), ALU.subtract)\
                   .then_inc(sv.did(f"lo{q}"), 1)

        def freed(phase, i, per, o, r_off=0):
            return free[o % 4], i * (per // 4) + (TURN0[phase] + r_off + o // 4 + 1)

        def all_freed(eng, phase):
            for n in range(4):
                eng.wait_ge(free[n], TURN0[phase])

        def settle(eng):
            eng.sem_inc(settled, 1)

        def b4(n):
            return pa[n][:].rearrange("p (m s) -> p m s", m=4)

        q_names = " ".join
        s5_in, s5_ct_in, io_in, mask_in = sem("s5_in"), sem("s5_ct_in"), sem("io_in"), sem("mask_in")
        s5ca = steps("s5_coef_act", "dt mag sin half")
        s5cv = steps("s5_coef_dve", "p1 p2 done")
        s5v = steps("s5_v", q_names(
            ["f0_0 f1_0 f2_0"] + [(f"f0_{q + 1} f1_{q + 1} f2_{q + 1} " if q < 3 else "")
             + f"c0_{q} c1_{q} c2_{q} c3_{q} v0_{q} v1_{q} v2_{q} zr_{q} zi_{q} x0_{q} x1_{q} x2_{q}"
             for q in range(4)] + ["y"]))
        s5a = steps("s5_a", q_names(["u"] + [f"sp_{q} sn_{q} hs_{q} sq_{q} cos_{q}" for q in range(4)] + ["gelu"]))
        s5p = steps("s5_p", q_names([f"bu_{q}" if q == 0 else f"bu_{q} y_{q - 1}" for q in range(4)] + ["y_3"]))
        l2a = steps("l2_a", "sq sqrt")
        l2v = steps("l2_v", "eps rec mul")
        l2p = steps("l2_p", "sum")
        rwa = steps("rows_act", "beta exp ln ea egc kdec cols")
        rwv = steps("rows_dve", "neg g gc kdec")
        rwp = steps("rows_pe", "cols")
        dna = steps("dn_a", q_names(["k v q e1 bv"] + [f"vn{c}" for c in range(NCH)] + ["sq sqrt"]))
        dnv = steps("dn_v", q_names(
            ["sel df kb el qg kg kd em at aqm aq init"] + [f"ur{c} st{c}" for c in range(NCH)]
            + ["var rec o1 o2"]))
        dnp = steps("dn_p", q_names(
            ["gc eg be kt kk kq vt"] + [f"ks{c} vn{c} o{c} st{c}" for c in range(NCH)] + ["sum"]))
        inv_p = steps("inv_p", "p d dt")
        inv_v = steps("inv_v", "p t tt")
        inv, ibuf = (inv_p, inv_v), (i_a, i_t, i_tt, i_p)
        branch_done = sem("branch_done")
        glu_v = steps("glu_v", "out")
        mrg_v, mrg_a, mrg_lo = steps("mrg_v", "sum"), sem("mrg_hi"), sem("mrg_lo")
        branch_lo, ones_set = sem("branch_lo"), sem("ones_set")
        conv_sum = sem("conv_sum")
        CONV0 = 72
        ff_silu, ff_prod, ff_hi, ff_lo = sem("ff_silu"), sem("ff_prod"), sem("ff_hi"), sem("ff_lo")

        def bc4(ap):
            return ap.broadcast_to([P, 4, P])

        def s5_coef_act(act):
            act.activation(s_w[:, 0, :], pcol("log_dt", 0, 32), ACT.Exp).then_inc(s5ca.did("dt"), 1)
            act.wait_ge(*s5cv.at(0, "p1"))
            act.activation(s_w[:, 2, :], s_w[:, 1, :], ACT.Exp).then_inc(s5ca.did("mag"), 1)
            act.wait_ge(*s5cv.at(0, "p2"))
            act.activation(s_w[:, 6, :], s_w[:, 3, :], ACT.Sin).then_inc(s5ca.did("sin"), 1)
            act.activation(s_w[:, 7, :], s_w[:, 3, :], ACT.Sin, scale=0.5).then_inc(s5ca.did("half"), 1)

        def s5_coef_dve(dve, link):
            w = lambda n: s_w[:, n, :]
            lr, li = pcol("a_re", 0, 32), pcol("a_im", 0, 32)
            link(dve.memset(s_cp[:].bitcast(U32), 0))
            dve.wait_ge(*s5ca.at(0, "dt"))
            link(dve.tensor_tensor(w(3), li, w(0), ALU.mult))
            dve.tensor_tensor(w(1), lr, w(0), ALU.mult).then_inc(s5cv.did("p1"), 1)
            link(dve.tensor_scalar(w(4), w(3), 1 / TWO_PI, MAGIC, ALU.mult, ALU.add))
            link(dve.tensor_scalar(w(4), w(4), MAGIC, None, ALU.subtract))
            for part in (6.28125, 0.0019350051879882812, 3.0199159819567e-07):
                link(dve.scalar_tensor_tensor(w(3), w(4), -part, w(3), ALU.mult, ALU.add))
            link(dve.tensor_scalar(w(5), w(3), 1 / TWO_PI, None, ALU.mult))
            dve.tensor_scalar(w(3), w(3), PI_IN, -PI_IN, ALU.min, ALU.max).then_inc(s5cv.did("p2"), 1)
            dve.wait_ge(*s5ca.at(0, "half"))
            link(dve.tensor_tensor(w(7), w(7), w(7), ALU.mult))
            link(dve.tensor_scalar(w(7), w(7), -2.0, 1.0, ALU.mult, ALU.add))
            link(dve.tensor_tensor(w(8), w(7), w(2), ALU.mult))
            link(dve.tensor_scalar(w(8), w(8), 1.0, None, ALU.subtract))
            link(dve.tensor_tensor(w(9), w(6), w(2), ALU.mult))
            link(dve.tensor_tensor(w(10), lr, lr, ALU.mult))
            link(dve.tensor_tensor(w(11), li, li, ALU.mult))
            link(dve.tensor_tensor(w(10), w(10), w(11), ALU.add))
            link(dve.reciprocal(w(10), w(10)))
            link(dve.tensor_tensor(w(11), w(8), lr, ALU.mult))
            link(dve.tensor_tensor(w(6), w(9), li, ALU.mult))
            link(dve.tensor_tensor(w(11), w(11), w(6), ALU.add))
            link(dve.tensor_tensor(w(11), w(11), w(10), ALU.mult))
            link(dve.tensor_tensor(w(6), w(9), lr, ALU.mult))
            link(dve.tensor_tensor(w(7), w(8), li, ALU.mult))
            link(dve.tensor_tensor(w(6), w(6), w(7), ALU.subtract))
            link(dve.tensor_tensor(w(6), w(6), w(10), ALU.mult))
            dve.tensor_scalar(w(7), w(6), -1.0, None, ALU.mult).then_inc(s5cv.did("done"), 1)

        def s5_pool(pool):
            with pool.Fori(0, 8) as i:
                pool.wait_ge(*s5p.before(i))
                settle(pool)
                pool.dma_start(s_bt[:], d["s5_b"][ds(i, 1)].rearrange("a p r n -> p (a r) n")).then_inc(s5_in, 16)
                pool.wait_ge(*s5v.before(i))
                settle(pool)
                pool.dma_start(s_ct[:], d["s5_c"][ds(i, 1)].rearrange("a p q r n -> p (a q) r n")).then_inc(s5_ct_in, 16)

        def s5_act(act):
            with act.Fori(0, 8) as i:
                act.wait_ge(*s5v.before(i))
                act.wait_ge(*s5p.before(i))
                settle(act)
                act.activation(s_u[:], u[:, ds(i, 1), :], ACT.Copy).then_inc(s5a.did("u"), 1)
                for q in range(4):
                    b = q % 2
                    act.wait_ge(*s5v.at(i, f"f2_{q}"))
                    act.wait_ge(*(s5v.at(i, f"x1_{q - 2}") if q >= 2 else s5v.before(i)))
                    act.activation(s_sin[:, b, 0, :], s_fr[:, b, :], ACT.Sin, scale=2 * PI_IN)\
                       .then_inc(s5a.did(f"sp_{q}"), 1)
                    act.activation(s_sin[:, b, 1, :], s_fr[:, b, :], ACT.Sin, scale=-2 * PI_IN)\
                       .then_inc(s5a.did(f"sn_{q}"), 1)
                    act.wait_ge(*(s5a.at(i, f"cos_{q - 1}") if q else s5a.before(i)))
                    act.activation(s_hs[:], s_fr[:, b, :], ACT.Sin, scale=PI_IN).then_inc(s5a.did(f"hs_{q}"), 1)
                    act.wait_ge(*s5a.at(i, f"hs_{q}"))
                    act.activation(s_hs[:], s_hs[:], ACT.Square).then_inc(s5a.did(f"sq_{q}"), 1)
                    act.wait_ge(*s5a.at(i, f"sq_{q}"))
                    act.activation(s_cos[:, b, :], s_hs[:], ACT.Copy, scale=-2.0, bias=1.0)\
                       .then_inc(s5a.did(f"cos_{q}"), 1)
                act.wait_ge(*s5v.at(i, "y"))
                settle(act)
                act.activation(u[:, ds(i, 1), :], s_y[:], ACT.Gelu).then_inc(s5a.did("gelu"), 1)

        def s5_dve(dve):
            def turns(i, q):
                th = s_w[:, 5, ds(i * 4 + q, 1)]
                dve.wait_ge(*(s5v.at(i, f"f2_{q - 1}") if q else s5v.before(i)))
                dve.tensor_scalar(s_rd[:], s_io[:], th, MAGIC, ALU.mult, ALU.add).then_inc(s5v.did(f"f0_{q}"), 1)
                dve.wait_ge(*s5v.at(i, f"f0_{q}"))
                dve.tensor_scalar(s_rd[:], s_rd[:], MAGIC, None, ALU.subtract).then_inc(s5v.did(f"f1_{q}"), 1)
                dve.wait_ge(*s5v.at(i, f"f1_{q}"))
                dve.wait_ge(*(s5a.at(i, f"hs_{q - 2}") if q >= 2 else s5a.before(i)))
                dve.scalar_tensor_tensor(s_fr[:, q % 2, :], s_io[:], th, s_rd[:], ALU.mult, ALU.subtract)\
                   .then_inc(s5v.did(f"f2_{q}"), 1)

            with dve.Fori(0, 8) as i:
                turns(i, 0)
                dve.wait_ge(s5_ct_in, i * 16 + 16)
                for q in range(4):
                    b = q % 2
                    if q < 3:
                        turns(i, q + 1)
                    cr, ci, nci = (s_w[:, n, ds(i * 4 + q, 1)] for n in (11, 6, 7))
                    re, im = s_ct[:, q, 0, :], s_ct[:, q, 1, :]
                    dve.tensor_scalar(s_c1[:, q, 0, :], im, ci, None, ALU.mult).then_inc(s5v.did(f"c0_{q}"), 1)
                    dve.tensor_scalar(s_c1[:, q, 1, :], im, cr, None, ALU.mult).then_inc(s5v.did(f"c1_{q}"), 1)
                    dve.wait_ge(*s5v.at(i, f"c1_{q}"))
                    dve.wait_ge(*s5p.before(i))
                    dve.scalar_tensor_tensor(s_cp[:, 0, q, 32 * q:32 * q + 32], re, cr, s_c1[:, q, 0, :],
                                             ALU.mult, ALU.subtract).then_inc(s5v.did(f"c2_{q}"), 1)
                    dve.scalar_tensor_tensor(s_cp[:, 1, q, 32 * q:32 * q + 32], re, nci, s_c1[:, q, 1, :],
                                             ALU.mult, ALU.subtract).then_inc(s5v.did(f"c3_{q}"), 1)
                    pq = pa[b][:].rearrange("p (r t) -> p r t", r=2)
                    cos = s_cos[:, b:b + 1, :].broadcast_to([P, 2, T])
                    sin = s_sin[:, b, :, :]
                    rho = s_w[:, 2, ds(i * 4 + q, 1)].broadcast_to([P, T])
                    dve.wait_ge(*s5a.at(i, f"cos_{q}"))
                    dve.wait_ge(*s5p.at(i, f"bu_{q}"))
                    if q:
                        dve.wait_ge(*s5v.at(i, f"x2_{q - 1}"))
                    dve.tensor_tensor(s_v[:], pq, cos, ALU.mult).then_inc(s5v.did(f"v0_{q}"), 1)
                    dve.tensor_tensor(s_p[:], pq[:, ::-1, :], sin, ALU.mult).then_inc(s5v.did(f"v1_{q}"), 1)
                    dve.wait_ge(*s5v.at(i, f"v1_{q}"))
                    dve.tensor_tensor(s_v[:], s_v[:], s_p[:], ALU.add).then_inc(s5v.did(f"v2_{q}"), 1)
                    dve.wait_ge(*s5v.at(i, f"v2_{q}"))
                    dve.tensor_tensor_scan(s_z[:, 0, :], rho, s_v[:, 0, :], 0.0, ALU.mult, ALU.add)\
                       .then_inc(s5v.did(f"zr_{q}"), 1)
                    dve.tensor_tensor_scan(s_z[:, 1, :], rho, s_v[:, 1, :], 0.0, ALU.mult, ALU.add)\
                       .then_inc(s5v.did(f"zi_{q}"), 1)
                    dve.wait_ge(*s5v.at(i, f"zi_{q}"))
                    dve.wait_ge(*(s5p.at(i, f"y_{q - 2}") if q >= 2 else s5p.before(i)))
                    dve.tensor_tensor(s_x[:, b, :, :], s_z[:], cos, ALU.mult).then_inc(s5v.did(f"x0_{q}"), 1)
                    dve.tensor_tensor(s_p[:], s_z[:, ::-1, :], sin, ALU.mult).then_inc(s5v.did(f"x1_{q}"), 1)
                    dve.wait_ge(*s5v.at(i, f"x1_{q}"))
                    dve.tensor_tensor(s_x[:, b, :, :], s_x[:, b, :, :], s_p[:], ALU.subtract)\
                       .then_inc(s5v.did(f"x2_{q}"), 1)
                dve.wait_ge(*s5p.at(i, "y_3"))
                dve.wait_ge(*s5a.before(i))
                dve.scalar_tensor_tensor(s_y[:], s_u[:], par[:, ds(i + COL["s5_d"], 1)], pa[2][:, 0:T],
                                         ALU.mult, ALU.add).then_inc(s5v.did("y"), 1)

        def s5_pe(pe):
            def readout(i, q):
                pe.wait_ge(*s5v.at(i, f"x2_{q}"))
                if q == 0:
                    pe.wait_ge(*s5v.before(i))
                pe.matmul(pa[2][:, 0:T], s_cp[:, 0, q, :], s_x[:, q % 2, 0, :], start=q == 0, stop=False)
                pe.matmul(pa[2][:, 0:T], s_cp[:, 1, q, :], s_x[:, q % 2, 1, :], start=False, stop=q == 3)\
                  .then_inc(s5p.did(f"y_{q}"), 1)

            with pe.Fori(0, 8) as i:
                pe.wait_ge(*s5a.at(i, "u"))
                pe.wait_ge(s5_in, i * 16 + 16)
                for q in range(4):
                    r = slice(32 * q, 32 * q + 32)
                    pe.wait_ge(*(s5v.at(i, f"v1_{q - 2}") if q >= 2 else s5v.before(i)))
                    for n in range(2):
                        mm = pe.matmul(pa[q % 2][:, n * T:n * T + T], s_bt[r, n, :], s_u[r, :], start=True, stop=True)
                    mm.then_inc(s5p.did(f"bu_{q}"), 1)
                    if q:
                        readout(i, q - 1)
                readout(i, 3)

        def unit_act(act, n, base_t):
            with act.Fori(0, 4) as i:
                act.wait_ge(*l2v.before(i + 4 * n))
                settle(act)
                act.activation(d_sq[:], qkv[:, ds(i * 2 + base_t, 2), :], ACT.Square).then_inc(l2a.did("sq"), 1)
                act.wait_ge(*l2v.at(i + 4 * n, "eps"))
                act.activation(d_rn[:], d_rn[:], ACT.Sqrt).then_inc(l2a.did("sqrt"), 1)

        def unit_pe(pe, n):
            with pe.Fori(0, 4) as i:
                pe.wait_ge(*l2a.at(i + 4 * n, "sq"))
                pe.wait_ge(*l2v.before(i + 4 * n))
                pe.matmul(pa[0][:], ones[:], d_sq[:], start=True, stop=True).then_inc(l2p.did("sum"), 1)

        def unit_dve(dve, n, base_t, scale):
            with dve.Fori(0, 4) as i:
                j = i + 4 * n
                dve.wait_ge(*l2p.at(j, "sum"))
                dve.tensor_scalar(d_rn[:], pa[0][:].rearrange("p (a t) -> p a t", a=2), EPS, scale,
                                  ALU.add, ALU.mult).then_inc(l2v.did("eps"), 1)
                dve.wait_ge(*l2a.at(j, "sqrt"))
                dve.reciprocal(d_rn[:], d_rn[:]).then_inc(l2v.did("rec"), 1)
                dve.wait_ge(*l2v.at(j, "rec"))
                tile = qkv[:, ds(i * 2 + base_t, 2), :]
                dve.tensor_tensor(tile, tile, d_rn[:], ALU.mult).then_inc(l2v.did("mul"), 1)

        H8 = slice(0, HEADS)

        def rows_act(act):
            act.activation(d_rows[H8, 2, :], graw[H8, 0, :], ACT.Sigmoid).then_inc(rwa.did("beta"), 1)
            act.wait_ge(*rwv.at(0, "neg"))
            act.activation(d_g[H8, 1, :], d_g[H8, 1, :], ACT.Exp).then_inc(rwa.did("exp"), 1)
            act.wait_ge(*rwa.at(0, "exp"))
            act.activation(d_g[H8, 1, :], d_g[H8, 1, :], ACT.Ln, bias=1.0).then_inc(rwa.did("ln"), 1)
            act.activation(d_el[H8, 0, 0:1], pcol("a_log")[H8], ACT.Exp).then_inc(rwa.did("ea"), 1)
            act.wait_ge(*rwv.at(0, "gc"))
            act.activation(d_rows[H8, 1, :], d_rows[H8, 0, :], ACT.Exp).then_inc(rwa.did("egc"), 1)
            act.wait_ge(*rwv.at(0, "kdec"))
            act.activation(d_g[H8, 0, :], d_g[H8, 0, :], ACT.Exp).then_inc(rwa.did("kdec"), 1)
            act.wait_ge(*rwp.at(0, "cols"))
            act.activation(d_cols[:], pa[0][:, 0:48].rearrange("p (a b c) -> p a b c", a=2, b=3), ACT.Copy)\
               .then_inc(rwa.did("cols"), 1)

        def rows_dve(dve, link):
            g0, g1 = d_g[H8, 0, :], d_g[H8, 1, :]
            link(dve.tensor_scalar(g0, graw[H8, 1, :], pcol("dt_bias")[H8], None, ALU.add))
            link(dve.tensor_scalar(g1, g0, -1.0, None, ALU.mult))
            dve.tensor_tensor(g1, g1, g0, ALU.min).then_inc(rwv.did("neg"), 1)
            dve.wait_ge(*rwa.at(0, "ea"))
            link(dve.scalar_tensor_tensor(g1, g0, 0.0, g1, ALU.max, ALU.add))
            dve.tensor_scalar(g1, g1, d_el[H8, 0, 0:1], -1.0, ALU.mult, ALU.mult).then_inc(rwv.did("g"), 1)
            dve.wait_ge(*rwv.at(0, "g"))
            for c in range(NCH):
                last = dve.tensor_tensor_scan(d_rows[H8, 0, c * C:c * C + C], ones[H8, 0:C],
                                              g1[:, c * C:c * C + C], 0.0, ALU.mult, ALU.add)
            last.then_inc(rwv.did("gc"), 1)
            dve.wait_ge(*rwv.at(0, "gc"))
            gcc = d_rows[H8, 0, :].rearrange("p (c t) -> p c t", t=C)
            dve.tensor_tensor(g0.rearrange("p (c t) -> p c t", t=C), gcc[:, :, C - 1:C].broadcast_to([HEADS, NCH, C]),
                              gcc, ALU.subtract).then_inc(rwv.did("kdec"), 1)

        def rows_pe(pe):
            pe.wait_ge(*rwa.at(0, "kdec"))
            for t in range(2):
                for n, r in enumerate((d_rows[H8, 0, :], d_rows[H8, 2, :], d_g[H8, 0, :])):
                    o = (t * 3 + n) * 8
                    mm = pe.transpose(pa[0][:, o:o + 8], r[:, t * P:t * P + P], ident[H8, H8])
            mm.then_inc(rwp.did("cols"), 1)

        def invert_pe(pe, j, signals, bufs):
            (inv_p, inv_v), (i_a, i_t, i_tt, i_p) = signals, bufs
            with pe.Fori(0, 6) as l:
                n = j * 6 + l
                pe.wait_ge(*inv_v.before(n))
                for m in range(4):
                    mm = pe.matmul(pa[0][:, m * P:m * P + P], i_a[:, m, :], i_t[:, m, :], start=True, stop=True)
                mm.then_inc(inv_p.did("p"), 1)
                pe.wait_ge(*inv_v.at(n, "p"))
                for m in range(4):
                    mm = pe.matmul(pa[1][:, m * P:m * P + P], i_tt[:, m, :], i_p[:, m, :], start=True, stop=True)
                mm.then_inc(inv_p.did("d"), 1)
                for m in range(4):
                    mm = pe.matmul(pa[2][:, m * P:m * P + P], i_p[:, m, :], i_tt[:, m, :], start=True, stop=True)
                mm.then_inc(inv_p.did("dt"), 1)

        def invert_dve(dve, j, signals, bufs, masks):
            (inv_p, inv_v), (i_a, i_t, i_tt, i_p) = signals, bufs
            with dve.Fori(0, 6) as l:
                n = j * 6 + l
                dve.wait_ge(*inv_p.at(n, "p"))
                dve.tensor_tensor(i_p[:], b4(0), masks[:, ds(l, 1), :].broadcast_to([P, 4, P]), ALU.mult)\
                   .then_inc(inv_v.did("p"), 1)
                dve.wait_ge(*inv_p.at(n, "d"))
                dve.tensor_tensor(i_t[:], b4(1), i_t[:], ALU.add).then_inc(inv_v.did("t"), 1)
                dve.wait_ge(*inv_p.at(n, "dt"))
                dve.tensor_tensor(i_tt[:], b4(2), i_tt[:], ALU.add).then_inc(inv_v.did("tt"), 1)

        def tok(c):
            return c // 2, slice(C * (c % 2), C * (c % 2) + C)

        def dn_act(act):
            with act.Fori(0, 4) as i:
                act.wait_ge(*dnv.before(i))
                settle(act)
                act.activation(d_k[:], qkv[:, ds(i * 2 + 8, 2), :], ACT.Copy).then_inc(dna.did("k"), 1)
                act.activation(d_v[:], qkv[:, ds(i * 2 + 16, 2), :], ACT.Copy).then_inc(dna.did("v"), 1)
                act.activation(d_q[:], qkv[:, ds(i * 2, 2), :], ACT.Copy).then_inc(dna.did("q"), 1)
                act.wait_ge(*dnv.at(i, "df"))
                act.activation(d_e1[:], d_e1[:], ACT.Exp).then_inc(dna.did("e1"), 1)
                act.wait_ge(*dnp.at(i, "vt"))
                settle(act)
                for a in range(2):
                    for t in range(2):
                        m = a * 2 + t
                        last = act.activation(d_bv[:, m, :], pa[3][:, m * P:m * P + P], ACT.Copy,
                                              scale=d_cols[:, t, 1, ds(i * 2 + a, 1)])
                last.then_inc(dna.did("bv"), 1)
                for c in range(NCH):
                    _, r = tok(c)
                    act.wait_ge(*dnp.at(i, f"vn{c}"))
                    act.activation(d_vn[r], pa[1][r, 0:2 * P].rearrange("p (a n) -> p a n", a=2), ACT.Copy)\
                       .then_inc(dna.did(f"vn{c}"), 1)
                act.wait_ge(*dnp.at(i, f"st{NCH - 1}"))
                act.activation(d_qg[:], pa[2][:].rearrange("p (a t) -> p a t", a=2), ACT.Square)\
                   .then_inc(dna.did("sq"), 1)
                act.wait_ge(*dnv.at(i, "var"))
                act.activation(d_kg[:], d_kg[:], ACT.Sqrt).then_inc(dna.did("sqrt"), 1)

        def dn_dve(dve):
            def b2(n):
                return pa[n][:].rearrange("p (a t) -> p a t", a=2)

            with dve.Fori(0, 4) as i:
                dve.wait_ge(*dnv.before(i))
                for a in range(2):
                    last = dve.tensor_scalar(d_sel[H8, a], d_rows[H8], ident[H8, ds(i * 2 + a, 1)], None, ALU.mult)
                last.then_inc(dnv.did("sel"), 1)
                dve.wait_ge(*dnp.at(i, "gc"))
                for a in range(2):
                    for t in range(2):
                        last = dve.tensor_scalar(d_e1[:, 2 * a + t, :], pa[0][:, a * T + t * P:a * T + t * P + P],
                                                 d_cols[:, t, 0, ds(i * 2 + a, 1)], 0.0, ALU.subtract, ALU.min)
                last.then_inc(dnv.did("df"), 1)
                dve.wait_ge(*dnp.at(i, "be"))
                dve.wait_ge(*dna.at(i, "k"))
                dve.tensor_tensor(d_kb[:], b2(2), d_k[:], ALU.mult).then_inc(dnv.did("kb"), 1)
                dve.wait_ge(*dnp.at(i, "eg"))
                dve.tensor_copy(d_el[:], b2(1)[:, :, C - 1::C]).then_inc(dnv.did("el"), 1)
                dve.wait_ge(*dna.at(i, "q"))
                dve.tensor_tensor(d_qg[:], b2(1), d_q[:], ALU.mult).then_inc(dnv.did("qg"), 1)
                dve.wait_ge(*dnv.at(i, "kb"))
                dve.tensor_tensor(d_kg[:], b2(1), d_kb[:], ALU.mult).then_inc(dnv.did("kg"), 1)
                dve.wait_ge(*dnp.at(i, "kt"))
                for a in range(2):
                    for t in range(2):
                        m = a * 2 + t
                        last = dve.tensor_scalar(d_kd[:, m, :], pa[3][:, m * P:m * P + P],
                                                 d_cols[:, t, 2, ds(i * 2 + a, 1)], None, ALU.mult)
                last.then_inc(dnv.did("kd"), 1)
                dve.wait_ge(*dna.at(i, "e1"))
                dve.tensor_tensor(i_a[:], d_e1[:], bc4(masks[:, 6:7, :]), ALU.mult).then_inc(dnv.did("em"), 1)
                dve.wait_ge(*dnv.at(i, "em"))
                dve.wait_ge(*dnp.at(i, "kk"))
                dve.tensor_tensor(i_a[:], b4(0), i_a[:], ALU.mult).then_inc(dnv.did("at"), 1)
                dve.tensor_tensor(d_at[:], d_e1[:], bc4(masks[:, 7:8, :]), ALU.mult).then_inc(dnv.did("aqm"), 1)
                dve.wait_ge(*dnv.at(i, "aqm"))
                dve.wait_ge(*dnp.at(i, "kq"))
                dve.tensor_tensor(d_at[:], b4(2), d_at[:], ALU.mult).then_inc(dnv.did("aq"), 1)
                dve.tensor_copy(i_t[:], bc4(ident[:].unsqueeze(1)))
                dve.tensor_copy(i_tt[:], bc4(ident[:].unsqueeze(1)))
                dve.memset(d_s[:], 0.0).then_inc(dnv.did("init"), 1)
                dve.wait_ge(*dnv.at(i, "init"))
                settle(dve)
                invert_dve(dve, i, inv, ibuf, masks)
                for c in range(NCH):
                    t, r = tok(c)
                    dve.wait_ge(*dnp.at(i, f"ks{c}"))
                    dve.wait_ge(*dna.at(i, "bv"))
                    bv = d_bv[r].rearrange("p (a t) n -> p a t n", a=2)[:, :, t, :]
                    dve.tensor_tensor(d_ur[r], bv, pa[0][r, 0:2 * P].rearrange("p (a n) -> p a n", a=2),
                                      ALU.subtract).then_inc(dnv.did(f"ur{c}"), 1)
                    dve.wait_ge(*dnp.at(i, f"st{c}"))
                    for a in range(2):
                        last = dve.scalar_tensor_tensor(d_s[:, a, :], d_s[:, a, :], d_el[:, a, c:c + 1],
                                                        pa[3][:, a * P:a * P + P], ALU.mult, ALU.add)
                    last.then_inc(dnv.did(f"st{c}"), 1)
                dve.wait_ge(*dnp.at(i, "sum"))
                dve.tensor_scalar(d_kg[:], b2(0), 1.0 / P, EPS, ALU.mult, ALU.add).then_inc(dnv.did("var"), 1)
                dve.wait_ge(*dna.at(i, "sqrt"))
                dve.reciprocal(d_kg[:], d_kg[:]).then_inc(dnv.did("rec"), 1)
                dve.wait_ge(*dnv.at(i, "rec"))
                dve.scalar_tensor_tensor(d_kb[:], b2(2), pcol("dn_norm"), d_kg[:], ALU.mult, ALU.mult)\
                   .then_inc(dnv.did("o1"), 1)
                dve.wait_ge(*dnv.at(i, "o1"))
                zt = z[:, ds(i * 2, 2), :]
                dve.tensor_tensor(zt, zt, d_kb[:], ALU.mult).then_inc(dnv.did("o2"), 1)

        def dn_pe(pe):
            def each(fn, name):
                for a in range(2):
                    for t in range(2):
                        mm = fn(a, t, slice((2 * a + t) * P, (2 * a + t + 1) * P), slice(t * P, t * P + P))
                mm.then_inc(dnp.did(name), 1)

            with pe.Fori(0, 4) as i:
                pe.wait_ge(*dnv.at(i, "sel"))
                for n, name in enumerate(("gc", "eg", "be")):
                    for a in range(2):
                        mm = pe.matmul(pa[n][:, a * T:a * T + T], ones[H8, :], d_sel[H8, a, n, :], start=True, stop=True)
                    mm.then_inc(dnp.did(name), 1)
                pe.wait_ge(*dna.at(i, "v"))
                each(lambda a, t, m, s: pe.transpose(pa[3][:, m], d_k[:, a, s], ident[:]), "kt")
                pe.wait_ge(*dnv.at(i, "kb"))
                each(lambda a, t, m, s: pe.matmul(pa[0][:, m], d_k[:, a, s], d_kb[:, a, s], start=True, stop=True), "kk")
                pe.wait_ge(*dna.at(i, "q"))
                each(lambda a, t, m, s: pe.matmul(pa[2][:, m], d_k[:, a, s], d_q[:, a, s], start=True, stop=True), "kq")
                pe.wait_ge(*dnv.at(i, "kd"))
                each(lambda a, t, m, s: pe.transpose(pa[3][:, m], d_v[:, a, s], ident[:]), "vt")
                pe.wait_ge(*dnv.at(i, "init"))
                settle(pe)
                invert_pe(pe, i, inv, ibuf)
                pe.wait_ge(*inv_v.at(i * 6 + 5, "tt"))
                pe.wait_ge(*dna.at(i, "bv"))
                for c in range(NCH):
                    t, r = tok(c)
                    cols = slice(c * C, c * C + C)
                    if c:
                        pe.wait_ge(*dnv.at(i, f"st{c - 1}"))
                    for a in range(2):
                        mm = pe.matmul(pa[0][r, a * P:a * P + P], d_kg[:, a, cols], d_s[:, a, :], start=True, stop=True)
                    mm.then_inc(dnp.did(f"ks{c}"), 1)
                    pe.wait_ge(*dnv.at(i, f"ur{c}"))
                    settle(pe)
                    for a in range(2):
                        mm = pe.matmul(pa[1][r, a * P:a * P + P], i_tt[r, 2 * a + t, r], d_ur[r, a, :], start=True, stop=True)
                    mm.then_inc(dnp.did(f"vn{c}"), 1)
                    pe.wait_ge(*dna.at(i, f"vn{c}"))
                    for a in range(2):
                        o = slice(a * T + c * C, a * T + c * C + C)
                        pe.matmul(pa[2][:, o], d_s[:, a, :], d_qg[:, a, cols], start=True, stop=False)
                        mm = pe.matmul(pa[2][:, o], d_vn[r, a, :], d_at[r, 2 * a + t, r], start=False, stop=True)
                    mm.then_inc(dnp.did(f"o{c}"), 1)
                    for a in range(2):
                        mm = pe.matmul(pa[3][:, a * P:a * P + P], d_kd[r, 2 * a + t, :], d_vn[r, a, :], start=True, stop=True)
                    mm.then_inc(dnp.did(f"st{c}"), 1)
                pe.wait_ge(*dna.at(i, "sq"))
                pe.matmul(pa[0][:], ones[:], d_qg[:], start=True, stop=True).then_inc(dnp.did("sum"), 1)

        xc = sb("xc", [KD, T], A0 + 32)
        hc_hi = sb("hc_hi", [KD, T], A0, F32R)
        hc_lo = sb("hc_lo", [KD, T], A0 + 16, F32R)
        T2 = 2 * T
        zk = sb("zk", [8, T2], A0 + 32)
        zv = sb("zv", [8, T2], A0 + 48)
        zl = sb("zl", [2, T2], A0 + 64)
        kv = sb("kv", [4, T2], A0 + 68)
        zg = sb("zg", [2, T], A0 + 76)
        zr = sb("zr", [8, T], A0)
        q = sb("q", [8, T], A0 + 8)
        ts0 = sb("ts0", [28], A0 + 78)
        t_cos = sb("t_cos", [T], H0)
        t_sin = sb("t_sin", [T], H0 + 1)
        t_perm = sb("t_perm", [P], H0 + 2)
        t_rot = sb("t_rot", [T], H0 + 2.5)
        t_q = sb("t_q", [T], H0 + 3.5)
        t_s = sb("t_s", [2, T2], H0 + 4.5)
        t_pt = sb("t_pt", [4, P], H0 + 8.5)
        t_v = sb("t_v", [4, T], H0 + 10.5)
        t_band = sb("t_band", [2, T2], H0 + 14.5)
        t_st = sb("t_st", [4, 4], H0 + 18.5)
        R2, R3, R4 = A0 + 18, A0 + 68, A0 + 78
        k_kk = sb("k_kk", [T2], H0)
        k_kd = sb("k_kd", [T2], H0 + 2)
        k_a = sb("k_a", [T2], H0 + 4)
        k_s = sb("k_s", [T2], H0 + 6)
        k_cs = sb("k_cs", [T2], H0 + 8)
        k_g = sb("k_g", [T2], H0 + 10)
        k_gi = sb("k_gi", [T2], H0 + 12)
        k_gp = sb("k_gp", [T2], H0 + 14)
        k_bh = sb("k_bh", [T2], H0 + 16)
        k_kh = sb("k_kh", [T2], H0 + 18)
        k_ah = sb("k_ah", [T2], H0 + 20)
        k_vt = sb("k_vt", [4, P], H0 + 22)
        k_bt = sb("k_bt", [4, P], H0 + 24)
        k_kt = sb("k_kt", [4, P], H0 + 26)
        k_nt = sb("k_nt", [4, P], H0 + 28)
        k_rh = sb("k_rh", [T], H0 + 30)
        k_bo = sb("k_bo", [T], H0 + 31)
        j_a = sb("j_a", [4, P], R2)
        j_t = sb("j_t", [4, P], R2 + 2)
        j_tt = sb("j_tt", [4, P], R2 + 4)
        j_p = sb("j_p", [4, P], R2 + 6)
        k_ab = sb("k_ab", [4, P], R2 + 8)
        k_ak = sb("k_ak", [4, P], R2 + 10)
        k_nv = sb("k_nv", [2, P], R2 + 12)
        k_ur = sb("k_ur", [P], R2 + 13)
        k_u = sb("k_u", [P], R2 + 13.5)
        k_masks = sb("k_masks", [10, P], R3)
        k_bd = sb("k_bd", [P], R3 + 5)
        k_S = sb("k_S", [P], R3 + 5.5)
        k_st = sb("k_st", [P], R3 + 6)
        k_y = sb("k_y", [T], R3 + 6.5)
        k_w = sb("k_w", [4, P], R4 + 0.25)
        k_rst = sb("k_rst", [T2], R4 + 2.25)
        k_ln = sb("k_ln", [T], R4 + 4.25)
        k_gt = sb("k_gt", [T], R4 + 5.25)
        k_x = sb("k_x", [T], R4 + 6.25)
        o_hi = sb("o_hi", [KD, T], H0, F32R)
        o_lo = sb("o_lo", [KD, T], H0 + 16, F32R)

        def order(e):
            return range(NCH) if e == 0 else range(NCH - 1, -1, -1)

        ada_landed = [sem(f"ada_landed{n}") for n in range(4)]
        ada_used, ada_set, cv_in, xc_in = sem("ada_used"), sem("ada_set"), sem("cv_in"), sem("xc_in")
        cva = steps("cva", "silu")
        mix_set = sem("mix_set")
        att_in, rwk_in, k_w_in = sem("att_in"), sem("rwk_in"), sem("k_w_in")
        rop = steps("rope_pe", "rot")
        rov = steps("rope_dve", "sin cos add")
        vtp, vta = sem("att_v_pe"), sem("att_v_act")
        ata = steps("att_act", q_names(["q"] + [f"p{n} e{n} t{n}" for n in range(4)] + ["o"]))
        atv = steps("att_dve", q_names([f"s{n} m{n} c{n} n{n} d{n} r{n} p{n}" for n in range(4)]))
        atp = steps("att_pe", q_names([f"s{n} t{n} o{n}" for n in range(4)]))
        low_a = sem("low_act")
        rka = steps("rk_a", q_names(["vs sq sqrt vt"] + [
            f"s{e} a{e} g{e} gi{e} gp{e} bt{e} kt{e} " + " ".join(
                f"nv{e}{x} " + " ".join(f"u{e}{x}{c}" for c in order(e)) for x in "cl") + (f" y{e}" if e == 0 else "")
            for e in range(2)] + ["sq2 sqrt2"]))
        rkv = steps("rk_v", q_names(["kq eps rec kk"] + [
            f"cs{e} sm{e} t{e} kd{e} b0{e} b1{e} kh{e} ah{e} rh{e} bo{e} " + (f"bo2{e} " if e else "") + " ".join(
                f"im{e}{x} nt{e}{x} " + (f"ab{e}{x} ak{e}{x} " if x == "l" else "") + f"init{e}{x} "
                + " ".join(f"ur{e}{x}{c} sa{e}{x}{c} sb{e}{x}{c}" for c in order(e)) for x in "cl")
            + (f" y{e}" if e == 1 else "")
            for e in range(2)] + ["yc eps2 rec2 n1 n2 bv add out"]))
        rkp = steps("rk_p", q_names(["sum vt"] + [
            f"s{e} a{e} bt{e} kt{e} " + " ".join(
                f"head{e}{x} im{e}{x} nt{e}{x} " + (f"ab{e}{x} ak{e}{x} " if x == "l" else "") + f"nv{e}{x} "
                + " ".join(f"ks{e}{x}{c} u{e}{x}{c} " + (f"y{e}{x}{c} " if x == "l" else "") + f"st{e}{x}{c}"
                           for c in order(e)) for x in "cl")
            for e in range(2)] + ["mean gate bonus var"]))
        jnv_p = steps("jnv_p", "p d dt")
        jnv_v = steps("jnv_v", "p t tt")

        def load_ada(sp):
            for c in range(4):
                sp.dma_start(raw[:, c, :], chunk_rows("ada")(0, c)).then_inc(ada_landed[c], 16)
            with sp.Fori(1, 24) as i:
                for c in range(4):
                    sp.wait_ge(ada_used, i * 4 + (c - 3))
                    sp.dma_start(raw[:, c, :], chunk_rows("ada")(i * 4, c)).then_inc(ada_landed[c], 16)
            for c in range(4):
                sp.wait_ge(ada_used, 93 + c)

        def ada_pe(pe):
            pe.wait_ge(*cva.at(0, "silu"))
            with pe.Fori(0, 24) as i:
                for c in range(4):
                    pe.wait_ge(ada_landed[c], i * 16 + 16)
                    for t in range(KD):
                        mm = pe.matmul(pa[3][:, ds(i * 8 + 2 * c, 2)], raw[:, c, t * P:t * P + P], cve[:, t, :],
                                       start=t == 0, stop=t == KD - 1)
                    mm.then_inc(ada_used, 1)

        def ada_dve(dve):
            dve.wait_ge(ada_used, 96)
            m = pa[3][:, 0:192].rearrange("p (n s) -> p n s", s=2)
            dve.tensor_tensor(mod[:], m[:, :, 0], pcol("ada_b", 0, 96), ALU.add)
            dve.tensor_tensor(modc[:], m[:, 0:32, 1], pcol("ada_b", 0, 32), ALU.add).then_inc(ada_set, 1)

        def mix_scales(dve, link, row, scale, g):
            link(dve.scalar_tensor_tensor(nscale[:, row, :], scale, 1.0, pcol(g, 0, KD), ALU.add, ALU.mult))

        def project2(pe):
            def piece(rnd, k, o, half, wide, turn):
                tiles = [(s, half * 8 + s) for s in range(8)]
                if not wide:
                    return products(pe, rnd, k, tiles, o % 4, h_hi, h_lo, half == 0, half == 1, turn)
                if turn is not None:
                    pe.wait_ge(free[o % 4], turn)
                pe.wait_ge(lo_ready, rnd * 8 + k + 1)
                for n, (s, t) in enumerate(tiles):
                    hi, lo = (w[:, k % 4, s * P:s * P + P] for w in (w_hi, w_lo))
                    for w, ctx_in, lat_in, last in ((lo, hc_hi, h_hi, False), (hi, hc_lo, h_lo, False),
                                                    (hi, hc_hi, h_hi, True)):
                        first = half == 0 and n == 0 and w is lo
                        end = half == 1 and n == 7 and last
                        pe.matmul(po[o % 4][:, 0:T], w, ctx_in[:, t, :], start=first, stop=False,
                                  skip_group_check=True)
                        mm = pe.matmul(po[o % 4][:, T:T2], w, lat_in[:, t, :], start=False, stop=end,
                                       skip_group_check=True)
                return mm

            def part(rounds, r_off, wide):
                with pe.Fori(0, rounds) as i:
                    for k in range(8):
                        turn = i + (TURN0["w_in2"] + r_off) if k % 2 == 0 else None
                        piece(i + (ROUND0["w_in2"] + r_off), k, k // 2, k % 2, wide(k // 2), turn).then_inc(used, 1)

            part(5, 0, lambda o: True)
            part(1, 5, lambda o: o < 2)
            part(4, 6, lambda o: False)

        def shifted(dve, out, src, n, wide, at, inc):
            if wide:
                out, src = (v.rearrange("p (s t) -> p s t", s=2) for v in (out, src))
                a, b = (slice(None), slice(1, T)), (slice(None), slice(0, T - 1))
            else:
                a, b = (slice(1, T),), (slice(0, T - 1),)
            P0 = (slice(None),)
            dve.tensor_scalar(out, src, ts0[:, n], None, ALU.mult).then_inc(shift_sum, 1)
            dve.wait_ge(shift_sum, at + 1)
            dve.scalar_tensor_tensor(out[P0 + a], src[P0 + b], par[:, ds_of(COL["ts_prev"], n)], out[P0 + a],
                                     ALU.mult, ALU.add).then_inc(shift_sum, 1)
            dve.wait_ge(shift_sum, at + 2)
            dve.scalar_tensor_tensor(out[P0 + b], src[P0 + a], par[:, ds_of(COL["ts_next"], n)], out[P0 + b],
                                     ALU.mult, ALU.add).then_inc(inc, 1)

        shift_sum = sem("shift_sum")

        def ds_of(col, n):
            return ds(n.start + col, 1) if not isinstance(n, slice) else slice(col + n.start, col + n.start + 1)

        def rope_pe(pe, n0, tile, count):
            for j in range(count):
                pe.wait_ge(*rov.before(n0 + j))
                pe.matmul(pa[0][:, 0:T], t_perm[:], tile(j), start=True, stop=True).then_inc(rop.did("rot"), 1)

        def rope_dve(dve, n0, tile, count):
            for j in range(count):
                n = n0 + j
                dve.wait_ge(*rop.at(n, "rot"))
                dve.tensor_tensor(t_rot[:], pa[0][:, 0:T], t_sin[:], ALU.mult).then_inc(rov.did("sin"), 1)
                dve.tensor_tensor(tile(j), tile(j), t_cos[:], ALU.mult).then_inc(rov.did("cos"), 1)
                dve.wait_ge(*rov.at(n, "cos"))
                dve.tensor_tensor(tile(j), tile(j), t_rot[:], ALU.add).then_inc(rov.did("add"), 1)
                dve.wait_ge(*rov.at(n, "add"))

        def att_v_pe(pe):
            for j in range(2):
                if j:
                    pe.wait_ge(vta, j)
                for n in range(4):
                    mm = pe.transpose(pa[1][:, n * P:n * P + P], kv[:, 2 + j, n * P:n * P + P], ident[:])
                mm.then_inc(vtp, 1)

        def att_v_act(act):
            for j in range(2):
                act.wait_ge(vtp, j + 1)
                act.activation(t_v[:, :, j * P:j * P + P], pa[1][:].rearrange("p (n c) -> p n c", n=4), ACT.Copy)\
                   .then_inc(vta, 1)

        def att_pe(pe, g):
            with pe.Fori(0, 4) as i:
                b = i + 4 * g
                pe.wait_ge(*ata.at(b, "q"))
                for n in range(4):
                    a, blk = n // 2, n % 2
                    r = slice(64 * a, 64 * a + 64)
                    pe.wait_ge(*(atv.at(b, f"s{n - 1}") if n else atv.before(b)))
                    settle(pe)
                    pe.matmul(pa[0][:], t_q[r, blk * P:blk * P + P], kv[r, g, :], start=True, stop=True)\
                      .then_inc(atp.did(f"s{n}"), 1)
                    pe.wait_ge(*atv.at(b, f"p{n}"))
                    for kb in range(4):
                        mm = pe.transpose(pa[1][:, kb * P:kb * P + P], t_s[:, n % 2, kb * P:kb * P + P], ident[:])
                    mm.then_inc(atp.did(f"t{n}"), 1)
                    pe.wait_ge(*ata.at(b, f"t{n}"))
                    vcol = slice((2 * g + a) * 64, (2 * g + a) * 64 + 64)
                    for kb in range(4):
                        mm = pe.matmul(pa[2][r, blk * P:blk * P + P], t_v[:, kb, vcol], t_pt[:, kb, :],
                                       start=kb == 0, stop=kb == 3)
                    mm.then_inc(atp.did(f"o{n}"), 1)

        def att_act(act, g):
            with act.Fori(0, 4) as i:
                b = i + 4 * g
                act.wait_ge(*ata.before(b))
                settle(act)
                act.activation(t_q[:], q[:, ds(b, 1), :], ACT.Copy).then_inc(ata.did("q"), 1)
                for n in range(4):
                    sink = par[:, ds(b * 2 + (COL["sink"] + n // 2), 1)]
                    act.wait_ge(*atv.at(b, f"n{n}"))
                    settle(act)
                    act.activation(t_s[:, n % 2, :], t_s[:, n % 2, :], ACT.Exp, bias=t_st[:, n, 1:2], scale=0.125,
                                   accum_out=t_st[:, n, 2:3]).then_inc(ata.did(f"p{n}"), 1)
                    act.activation(t_st[:, n, 3:4], t_st[:, n, 1:2], ACT.Exp, bias=sink).then_inc(ata.did(f"e{n}"), 1)
                    act.wait_ge(*atp.at(b, f"t{n}"))
                    act.activation(t_pt[:], pa[1][:].rearrange("p (n c) -> p n c", n=4), ACT.Copy)\
                       .then_inc(ata.did(f"t{n}"), 1)
                act.wait_ge(*atp.at(b, "o3"))
                settle(act)
                act.activation(q[:, ds(b, 1), :], pa[2][:, 0:T], ACT.Copy).then_inc(ata.did("o"), 1)

        def att_dve(dve, g):
            with dve.Fori(0, 4) as i:
                b = i + 4 * g
                dve.wait_ge(*ata.before(b))
                for n in range(4):
                    sink = par[:, ds(b * 2 + (COL["sink"] + n // 2), 1)]
                    s = t_s[:, n % 2, :]
                    dve.wait_ge(*atp.at(b, f"s{n}"))
                    if n >= 2:
                        dve.wait_ge(*atp.at(b, f"t{n - 2}"))
                    elif n == 0:
                        dve.wait_ge(*atp.before(b))
                    dve.tensor_tensor(s, pa[0][:], t_band[:, n % 2, :], ALU.add).then_inc(atv.did(f"s{n}"), 1)
                    dve.wait_ge(*atv.at(b, f"s{n}"))
                    dve.tensor_reduce(t_st[:, n, 0:1], s, AX.X, ALU.max).then_inc(atv.did(f"m{n}"), 1)
                    dve.wait_ge(*atv.at(b, f"m{n}"))
                    dve.tensor_scalar(t_st[:, n, 0:1], t_st[:, n, 0:1], 0.125, sink, ALU.mult, ALU.max)\
                       .then_inc(atv.did(f"c{n}"), 1)
                    dve.wait_ge(*atv.at(b, f"c{n}"))
                    dve.tensor_scalar(t_st[:, n, 1:2], t_st[:, n, 0:1], -1.0, None, ALU.mult)\
                       .then_inc(atv.did(f"n{n}"), 1)
                    dve.wait_ge(*ata.at(b, f"e{n}"))
                    dve.tensor_tensor(t_st[:, n, 2:3], t_st[:, n, 2:3], t_st[:, n, 3:4], ALU.add)\
                       .then_inc(atv.did(f"d{n}"), 1)
                    dve.wait_ge(*atv.at(b, f"d{n}"))
                    dve.reciprocal(t_st[:, n, 2:3], t_st[:, n, 2:3]).then_inc(atv.did(f"r{n}"), 1)
                    dve.wait_ge(*atv.at(b, f"r{n}"))
                    dve.tensor_scalar(s, s, t_st[:, n, 2:3], None, ALU.mult).then_inc(atv.did(f"p{n}"), 1)

        def ffn_up_act(act, phase, f, round_act):
            def body(i, rnd, k):
                j = i * 2 + k // 4
                if k % 4 == 1 and f == 0:
                    act.wait_ge(*freed(phase, i, 4, k // 2))
                    act.activation(conv_a[:], conv_a[:], ACT.Silu).then_inc(ff_silu, 1)
                if k % 4 == 1 and f == 1:
                    act.wait_ge(used, rnd * 8 + k + 1)
                    act.wait_ge(ff_prod, j + KF)
                    act.activation(conv_a[:], po[k // 2][:, 0:T], ACT.Silu).then_inc(free[k // 2], 1)
                if k % 4 == 3:
                    act.wait_ge(ff_prod, j + (KF * f + 1))
                    settle(act)
                    act.activation(f_hi[:, ds(j, 1), :], conv_v[:], ACT.Copy).then_inc(ff_hi, 1)
            round_act(act, phase, 22, body)

        def ffn_up_dve(dve, phase, f, round_dve, conv):
            def body(i, rnd, k):
                o, j = k // 2, i * 2 + k // 4
                w = lambda n: par[:, ds(i * 4 + (COL["ffn_conv"] + 88 * n + o), 1)]
                at = i * 8 + (CONV0 + 2 * o)
                if k % 4 == 1 and f == 0:
                    dve.wait_ge(used, rnd * 8 + k + 1)
                    conv(dve, conv_a[:], o, w, 3, at).then_inc(free[o], 1)
                if k % 4 == 3:
                    dve.wait_ge(used, rnd * 8 + k + 1)
                    if f == 0:
                        conv(dve, conv_v[:], o, w, 3, at).then_inc(free[o], 1)
                        dve.wait_ge(*freed(phase, i, 4, o))
                        dve.wait_ge(ff_silu, j + 1)
                        dve.tensor_tensor(conv_v[:], conv_v[:], conv_a[:], ALU.mult).then_inc(ff_prod, 1)
                        dve.wait_ge(ff_prod, j + 1)
                    else:
                        dve.wait_ge(*freed(phase, i, 4, o - 1))
                        dve.tensor_tensor(conv_v[:], po[o][:, 0:T], conv_a[:], ALU.mult).then_inc(free[o], 1)
                        dve.wait_ge(*freed(phase, i, 4, o))
                        dve.sem_inc(ff_prod, 1)
                    dve.wait_ge(ff_hi, j + (KF * f + 1))
                    dve.tensor_tensor(f_lo[:, ds(j, 1), :], conv_v[:], f_hi[:, ds(j, 1), :].bitcast(F32),
                                      ALU.subtract).then_inc(ff_lo, 1)
            round_dve(dve, phase, 22, body)

        def ffn_down_act(act, phase, final=False):
            def body(i, final):
                for q in range(24):
                    if not final or q + LOOK < 24:
                        split_hi(act, i * 3 + (ROUND0[phase] + q // 8), q % 8 + LOOK, down_width(q + LOOK))
            with act.Fori(0, 3 if final else 4) as i:
                body(i, False)
            if final:
                body(3, True)

        def ffn_down_dve(dve, phase, f, final=False):
            def body(i, final):
                for q in range(24):
                    rnd = i * 3 + (ROUND0[phase] + q // 8)
                    if q % 6 == 5:
                        o = q // 6
                        xt = x[:, ds(i * 4 + o, 1), :]
                        dve.wait_ge(used, rnd * 8 + q % 8 + 1)
                        if f:
                            dve.scalar_tensor_tensor(xt, po[o][:, 0:T], mod[:, ds(i * 4 + (80 + o), 1)], xt,
                                                     ALU.mult, ALU.add).then_inc(free[o], 1)
                        else:
                            dve.tensor_tensor(xt, po[o][:, 0:T], xt, ALU.add).then_inc(free[o], 1)
                    if not final or q + LOOK < 24:
                        split_lo(dve, rnd, q % 8 + LOOK, down_width(q + LOOK))
            with dve.Fori(0, 3 if final else 4) as i:
                body(i, False)
            if final:
                body(3, True)


        jnv, jbuf = (jnv_p, jnv_v), (j_a, j_t, j_tt, j_p)

        def half(a):
            return slice(64 * a, 64 * a + 64)

        def off(x):
            return 0 if x == "c" else T

        def rk_pool(pool):
            with pool.Fori(0, 8) as j:
                pool.wait_ge(*rkp.before(j))
                settle(pool)
                pool.dma_start(k_w[:], d["rk_w"][ds(j, 1)].rearrange("a p n c -> p (a n) c")).then_inc(k_w_in, 16)

        def rk_act(act):
            with act.Fori(0, 8) as j:
                def then(ins, name):
                    ins.then_inc(rka.did(name), 1)
                    act.wait_ge(*rka.at(j, name))

                act.wait_ge(*rkv.before(j))
                settle(act)
                then(act.activation(k_s[:], zv[:, ds(j, 1), :], ACT.Copy), "vs")
                act.wait_ge(*rkv.at(j, "kq"))
                then(act.activation(k_cs[:], k_kk[:], ACT.Square), "sq")
                act.wait_ge(*rkv.at(j, "eps"))
                then(act.activation(k_cs[:], k_cs[:], ACT.Sqrt), "sqrt")
                act.wait_ge(*rkp.at(j, "vt"))
                then(act.activation(k_vt[:], b4(1), ACT.Copy), "vt")
                for e in range(2):
                    act.wait_ge(*rkp.at(j, f"s{e}"))
                    settle(act)
                    then(act.activation(k_s[:], pa[0][:], ACT.Sigmoid, bias=par[:, ds(j + (COL["w0"] + 8 * e), 1)]), f"s{e}")
                    act.wait_ge(*rkp.at(j, f"a{e}"))
                    settle(act)
                    then(act.activation(k_a[:], pa[1][:], ACT.Sigmoid, bias=par[:, ds(j + (COL["a0"] + 8 * e), 1)]), f"a{e}")
                    act.wait_ge(*rkv.at(j, f"sm{e}"))
                    then(act.activation(k_g[:], k_cs[:], ACT.Exp, scale=-DECAY), f"g{e}")
                    then(act.activation(k_gi[:], k_cs[:], ACT.Exp, scale=DECAY), f"gi{e}")
                    then(act.activation(k_gp[:], k_gp[:], ACT.Exp, scale=-DECAY), f"gp{e}")
                    act.wait_ge(*rkp.at(j, f"bt{e}"))
                    then(act.activation(k_bt[:], b4(2), ACT.Copy), f"bt{e}")
                    act.wait_ge(*rkp.at(j, f"kt{e}"))
                    then(act.activation(k_kt[:], b4(3), ACT.Copy), f"kt{e}")
                    for x in "cl":
                        act.wait_ge(*rkp.at(j, f"nv{e}{x}"))
                        then(act.activation(k_nv[:], pa[1][:, 0:T].rearrange("p (n c) -> p n c", n=2), ACT.Copy), f"nv{e}{x}")
                        for c in order(e):
                            r = half(c % 2)
                            act.wait_ge(*rkp.at(j, f"u{e}{x}{c}"))
                            then(act.activation(k_u[r], pa[1][r, 0:P], ACT.Copy), f"u{e}{x}{c}")
                    if e == 0:
                        act.wait_ge(*rkp.at(j, f"st{e}l{NCH - 1}"))
                        then(act.activation(k_y[:], pa[2][:, 0:T], ACT.Copy), "y0")
                act.wait_ge(*rkv.at(j, "yc"))
                then(act.activation(k_ln[:], k_y[:], ACT.Square), "sq2")
                act.wait_ge(*rkv.at(j, "eps2"))
                then(act.activation(k_ln[:], k_ln[:], ACT.Sqrt), "sqrt2")

        def rk_dve(dve):
            with dve.Fori(0, 8) as j:
                def then(ins, name):
                    ins.then_inc(rkv.did(name), 1)
                    dve.wait_ge(*rkv.at(j, name))

                def scale(name, e=0):
                    return par[:, ds(j + (COL[name] + 8 * e), 1)]

                def tile(v, lat=False):
                    w = v[:, ds(j, 1), T:T2] if lat else v[:, ds(j, 1), :]
                    return w.rearrange("p a t -> p (a t)")

                dve.wait_ge(*rkp.before(j))
                then(dve.tensor_scalar(k_kk[:], tile(zk), scale("k_k"), None, ALU.mult), "kq")
                dve.wait_ge(*rkp.at(j, "sum"))
                then(dve.tensor_scalar(k_cs[:], pa[0][:], 1e-12, None, ALU.max), "eps")
                dve.wait_ge(*rka.at(j, "sqrt"))
                then(dve.reciprocal(k_cs[:], k_cs[:]), "rec")
                then(dve.tensor_tensor(k_kk[:], k_kk[:], k_cs[:], ALU.mult), "kk")
                for e in range(2):
                    dve.wait_ge(*rka.at(j, f"s{e}"))
                    sc = (k_cs[:], k_s[:]) if e == 0 else (k_cs[:, ::-1], k_s[:, ::-1])
                    then(dve.tensor_tensor_scan(sc[0], k_rst[:], sc[1], 0.0, ALU.mult, ALU.add), f"cs{e}")
                    then(dve.tensor_tensor(k_gp[:], k_cs[:], k_s[:], ALU.subtract), f"sm{e}")
                    dve.wait_ge(*rka.at(j, f"a{e}"))
                    then(dve.tensor_scalar(k_kd[:], k_a[:], 1.0, scale("k_a"), ALU.subtract, ALU.mult), f"t{e}")
                    then(dve.scalar_tensor_tensor(k_kd[:], k_kd[:], 1.0, tile(zk), ALU.add, ALU.mult), f"kd{e}")
                    then(dve.tensor_tensor(k_bh[:], k_kk[:], k_a[:], ALU.mult), f"b0{e}")
                    dve.wait_ge(*rka.at(j, f"gp{e}"))
                    then(dve.tensor_tensor(k_bh[:], k_bh[:], k_gi[:], ALU.mult), f"b1{e}")
                    then(dve.tensor_tensor(k_kh[:], k_kd[:], k_gi[:], ALU.mult), f"kh{e}")
                    then(dve.tensor_tensor(k_ah[:], k_kk[:], k_gp[:], ALU.mult), f"ah{e}")
                    then(dve.tensor_tensor(k_rh[:], tile(zr), k_g[:, T:T2], ALU.mult), f"rh{e}")
                    bo = k_bo if e == 0 else k_x
                    then(dve.scalar_tensor_tensor(bo[:], k_kd[:, T:T2], scale("r_k"), tile(zr), ALU.mult, ALU.mult), f"bo{e}")
                    if e:
                        then(dve.tensor_tensor(k_bo[:], k_bo[:], k_x[:], ALU.add), f"bo2{e}")
                    for x in "cl":
                        dve.wait_ge(*rkp.at(j, f"im{e}{x}"))
                        then(dve.tensor_tensor(j_a[:], b4(0), bc4(k_masks[:, 6:7, :]), ALU.mult), f"im{e}{x}")
                        dve.wait_ge(*rkp.at(j, f"nt{e}{x}"))
                        m = 6 + 2 * e
                        then(dve.tensor_tensor(k_nt[:], b4(1), bc4(k_masks[:, m:m + 1, :]), ALU.mult), f"nt{e}{x}")
                        if x == "l":
                            m = bc4(k_masks[:, 7 + 2 * e:8 + 2 * e, :])
                            dve.wait_ge(*rkp.at(j, f"ab{e}{x}"))
                            then(dve.tensor_tensor(k_ab[:], b4(2), m, ALU.mult), f"ab{e}{x}")
                            dve.wait_ge(*rkp.at(j, f"ak{e}{x}"))
                            then(dve.tensor_tensor(k_ak[:], b4(3), m, ALU.mult), f"ak{e}{x}")
                        dve.tensor_copy(j_t[:], bc4(ident[:].unsqueeze(1)))
                        if x == "c":
                            dve.memset(k_S[:], 0.0)
                        dve.tensor_copy(j_tt[:], bc4(ident[:].unsqueeze(1))).then_inc(rkv.did(f"init{e}{x}"), 1)
                        dve.wait_ge(*rkv.at(j, f"init{e}{x}"))
                        settle(dve)
                        invert_dve(dve, j * 4 + (2 * e + (x == "l")), jnv, jbuf, k_masks)
                        for c in order(e):
                            r, n = half(c % 2), c // 2
                            dve.wait_ge(*rkp.at(j, f"ks{e}{x}{c}"))
                            dve.wait_ge(*rka.at(j, f"nv{e}{x}"))
                            then(dve.tensor_tensor(k_ur[r], k_nv[r, n, :], pa[0][r, 0:P], ALU.subtract), f"ur{e}{x}{c}")
                            end = off(x) + c * C + (C - 1 if e == 0 else 0)
                            g = k_g[:, end:end + 1]
                            dve.wait_ge(*rkp.at(j, f"st{e}{x}{c}"))
                            then(dve.scalar_tensor_tensor(k_st[:], pa[3][:, 0:P], g, k_bd[:], ALU.mult, ALU.mult), f"sa{e}{x}{c}")
                            then(dve.scalar_tensor_tensor(k_S[:], k_S[:], g, k_st[:], ALU.mult, ALU.add), f"sb{e}{x}{c}")
                    if e == 1:
                        then(dve.tensor_tensor(k_y[:], pa[2][:, 0:T], k_y[:], ALU.add), "y1")
                dve.wait_ge(*rkp.at(j, "mean"))
                then(dve.scalar_tensor_tensor(k_y[:], pa[0][:, 0:T], -1.0 / 64, k_y[:], ALU.mult, ALU.add), "yc")
                dve.wait_ge(*rkp.at(j, "var"))
                then(dve.tensor_scalar(k_ln[:], pa[0][:, 0:T], 1.0 / 64, 64e-5, ALU.mult, ALU.add), "eps2")
                dve.wait_ge(*rka.at(j, "sqrt2"))
                then(dve.reciprocal(k_ln[:], k_ln[:]), "rec2")
                then(dve.tensor_tensor(k_y[:], k_y[:], k_ln[:], ALU.mult), "n1")
                then(dve.tensor_scalar(k_y[:], k_y[:], scale("lnx_g"), scale("lnx_b"), ALU.mult, ALU.add), "n2")
                dve.wait_ge(*rkp.at(j, "bonus"))
                then(dve.tensor_tensor(k_x[:], pa[2][:, 0:T], tile(zv, True), ALU.mult), "bv")
                then(dve.tensor_tensor(k_y[:], k_y[:], k_x[:], ALU.add), "add")
                then(dve.tensor_tensor(tile(zr), pa[1][:, 0:T], k_y[:], ALU.mult), "out")

        def rk_pe(pe):
            with pe.Fori(0, 8) as j:
                pe.wait_ge(*rka.at(j, "sq"))
                pe.wait_ge(k_w_in, j * 16 + 16)
                pe.matmul(pa[0][:], k_bd[:], k_cs[:], start=True, stop=True).then_inc(rkp.did("sum"), 1)
                for n in range(4):
                    mm = pe.transpose(pa[1][:, n * P:n * P + P], k_s[:, n * P:n * P + P], ident[:])
                mm.then_inc(rkp.did("vt"), 1)
                for e in range(2):
                    pe.wait_ge(*rkv.at(j, "kk"))
                    pe.wait_ge(*rka.at(j, "vt" if e == 0 else "y0"))
                    if e:
                        pe.wait_ge(*rkv.at(j, f"sb0l{NCH - 1}"))
                    settle(pe)
                    for n in range(2):
                        pe.matmul(pa[n][:], k_w[half(e), n, :], zl[half(e), n, :], start=True, stop=True)\
                          .then_inc(rkp.did("sa"[n] + str(e)), 1)
                    pe.wait_ge(*rkv.at(j, f"b1{e}"))
                    for n in range(4):
                        mm = pe.transpose(pa[2][:, n * P:n * P + P], k_bh[:, n * P:n * P + P], ident[:])
                    mm.then_inc(rkp.did(f"bt{e}"), 1)
                    pe.wait_ge(*rkv.at(j, f"kh{e}"))
                    for n in range(4):
                        mm = pe.transpose(pa[3][:, n * P:n * P + P], k_kh[:, n * P:n * P + P], ident[:])
                    mm.then_inc(rkp.did(f"kt{e}"), 1)
                    pe.wait_ge(*rkv.at(j, f"bo{e}"))
                    pe.wait_ge(*rka.at(j, f"kt{e}"))
                    for x in "cl":
                        if x == "l":
                            pe.wait_ge(*rkv.at(j, f"sb{e}c{order(e)[-1]}"))
                        lhs, rhs = (k_bh, k_ah) if e == 0 else (k_ah, k_bh)
                        pairs = [("im", lhs, rhs), ("nt", k_kh, k_ah)]
                        if x == "l":
                            pairs += [("ab", k_bh, k_rh), ("ak", k_kh, k_rh)]
                        for a in range(2):
                            for bank, (name, w, m) in enumerate(pairs):
                                for n in range(2):
                                    at = slice(off(x) + n * P, off(x) + n * P + P)
                                    r_at = slice(n * P, n * P + P) if m is k_rh else at
                                    o = (2 * a + n) * P
                                    mm = pe.matmul(pa[bank][:, o:o + P], w[half(a), at], m[half(a), r_at],
                                                   start=True, stop=True)
                                if a:
                                    mm.then_inc(rkp.did(f"{name}{e}{x}"), 1)
                            if a == 0:
                                mm.then_inc(rkp.did(f"head{e}{x}"), 1)
                                pe.wait_ge(*rkp.at(j, f"head{e}{x}"))
                        pe.wait_ge(*rkv.at(j, f"nt{e}{x}"))
                        for a in range(2):
                            for n in range(2):
                                o = n * P + 64 * a
                                mm = pe.matmul(pa[1][:, o:o + 64], k_nt[:, 2 * a + n, :],
                                               k_vt[:, n + (2 if x == "l" else 0), half(a)], start=True, stop=True)
                        mm.then_inc(rkp.did(f"nv{e}{x}"), 1)
                        pe.wait_ge(*rkv.at(j, f"init{e}{x}"))
                        pe.wait_ge(*rka.at(j, f"nv{e}{x}"))
                        settle(pe)
                        n_inv = j * 4 + (2 * e + (x == "l"))
                        invert_pe(pe, n_inv, jnv, jbuf)
                        inv = j_tt if e == 0 else j_t
                        pe.wait_ge(*jnv[1].before(n_inv + 1, 6))
                        for c in order(e):
                            r, n = half(c % 2), c // 2
                            cols = slice(off(x) + c * C, off(x) + c * C + C)
                            blk = n + (2 if x == "l" else 0)
                            if c != order(e)[0]:
                                pe.wait_ge(*rkv.at(j, f"sb{e}{x}{c - (1 if e == 0 else -1)}"))
                            settle(pe)
                            pe.matmul(pa[0][r, 0:P], k_ah[:, cols], k_S[:], start=True, stop=True)\
                              .then_inc(rkp.did(f"ks{e}{x}{c}"), 1)
                            pe.wait_ge(*rkv.at(j, f"ur{e}{x}{c}"))
                            settle(pe)
                            for a in range(2):
                                mm = pe.matmul(pa[1][r, half(a)], inv[r, 2 * a + n, r], k_ur[r, half(a)],
                                               start=True, stop=True)
                            mm.then_inc(rkp.did(f"u{e}{x}{c}"), 1)
                            pe.wait_ge(*rka.at(j, f"u{e}{x}{c}"))
                            if x == "l":
                                o = slice(c * C, c * C + C)
                                pe.matmul(pa[2][:, o], k_S[:], k_rh[:, o], start=True, stop=False)
                                for a in range(2):
                                    pe.matmul(pa[2][half(a), o], k_u[r, half(a)], k_ab[r, 2 * a + n, r],
                                              start=False, stop=False)
                                    mm = pe.matmul(pa[2][half(a), o], k_vt[r, blk, half(a)], k_ak[r, 2 * a + n, r],
                                                   start=False, stop=True)
                                mm.then_inc(rkp.did(f"y{e}{x}{c}"), 1)
                            pe.matmul(pa[3][:, 0:P], k_bt[r, blk, :], k_u[r], start=True, stop=False)
                            pe.matmul(pa[3][:, 0:P], k_kt[r, blk, :], k_vt[r, blk, :], start=False, stop=True)\
                              .then_inc(rkp.did(f"st{e}{x}{c}"), 1)
                pe.wait_ge(*rkv.at(j, "y1"))
                pe.matmul(pa[0][:, 0:T], k_bd[:], k_y[:], start=True, stop=True).then_inc(rkp.did("mean"), 1)
                pe.matmul(pa[1][:, 0:T], k_w[:, 2, :], zg[:, 0, :], start=True, stop=False)
                pe.matmul(pa[1][:, 0:T], k_w[0:32, 3, :], zg[0:32, 1, :], start=False, stop=True)\
                  .then_inc(rkp.did("gate"), 1)
                pe.matmul(pa[2][:, 0:T], k_bd[:], k_bo[:], start=True, stop=True).then_inc(rkp.did("bonus"), 1)
                pe.wait_ge(*rka.at(j, "sq2"))
                pe.matmul(pa[0][:, 0:T], k_bd[:], k_ln[:], start=True, stop=True).then_inc(rkp.did("var"), 1)

        def block2_sp(sp):
            load_phase(sp, "w_in2", "w_in2", 10)
            load_phase(sp, "w_out2", "w_out2", 4)
            load_phase(sp, "ffn_up2", "ffn_up2", 22)
            load_down(sp, "ffn_down2", "ffn_down2")
            sp.wait_ge(*nv.at(6, "h"))
            sp.dma_start(d["out"], x[:]).then_inc(out_done, 16)
            sp.wait_ge(out_done, 16)

        def block2_pool(pool):
            pool.wait_ge(*nv.at(2, "h"))
            pool.dma_start(xc[:], d["ctx"]).then_inc(xc_in, 16)
            pool.wait_ge(used, 8 * ROUND0["w_out2"])
            for t, n in ((t_cos, "t_cos"), (t_sin, "t_sin"), (t_perm, "t_perm"), (t_band, "t_band")):
                pool.dma_start(t[:], d[n]).then_inc(att_in, 16)
            pool.wait_ge(*ata.before(8))
            pool.wait_ge(*atp.before(8))
            for t, n in ((k_masks, "masks"), (k_bd, "k_bd"), (k_rst, "k_rst")):
                pool.dma_start(t[:], d[n]).then_inc(rwk_in, 16)
            rk_pool(pool)

        def block2_act(act, round_act):
            act.wait_ge(*nv.at(2, "h"))
            norm_act(act, 3)
            act.wait_ge(*nv.at(3, "h"))
            split_act(act, 2, h_hi, hf)
            act.wait_ge(*sv.at(2, "lo3"))
            act.wait_ge(xc_in, 16)
            norm_act(act, 4, xc)
            act.wait_ge(*nv.at(4, "h"))
            split_act(act, 3, hc_hi, hf)

            def on_kv(i, rnd, k):
                if k % 2:
                    act.wait_ge(used, rnd * 8 + k + 1)
                    settle(act)
                    act.activation(kv[:, ds(k // 2, 1), :], po[k // 2][:], ACT.Copy).then_inc(free[k // 2], 1)

            def on_q(i, rnd, k):
                if k % 2:
                    act.wait_ge(used, rnd * 8 + k + 1)
                    settle(act)
                    act.activation(q[:, ds(i * 4 + k // 2, 1), :], po[k // 2][:, 0:T], ACT.Copy)\
                       .then_inc(free[k // 2], 1)
            nothing = lambda i, rnd, k: None
            round_act(act, "w_in2", 4, nothing)
            round_act(act, "w_in2", 1, on_kv, 4)
            round_act(act, "w_in2", 3, nothing, 5)
            round_act(act, "w_in2", 2, on_q, 8)
            act.wait_ge(*rov.before(10))
            att_v_act(act)
            att_act(act, 0)
            att_act(act, 1)
            act.activation(zl[:, 0, :], zl[:, 0, :], ACT.Tanh).then_inc(low_a, 1)
            act.activation(zg[:, 0, :], zg[:, 0, :], ACT.Sigmoid).then_inc(low_a, 1)
            act.activation(zg[:, 1, :], zg[:, 1, :], ACT.Sigmoid).then_inc(low_a, 1)
            rk_act(act)
            act.wait_ge(*rkv.before(8))
            for n, src in enumerate((q, zr)):
                for m in range(2):
                    s = slice(8 * n + 4 * m, 8 * n + 4 * m + 4)
                    act.activation(o_hi[:, s, :], src[:, 4 * m:4 * m + 4, :], ACT.Copy).then_inc(sa.did(f"hi{2 * n + m}"), 1)
            round_act(act, "w_out2", 4, nothing)
            all_freed(act, "ffn_up2")
            norm_act(act, 5)
            act.wait_ge(*nv.at(5, "h"))
            split_act(act, 5, h_hi, hf)
            ffn_up_act(act, "ffn_up2", 1, round_act)
            ffn_down_act(act, "ffn_down2", True)
            all_freed(act, "end")
            norm_act(act, 6)

        def block2_dve(dve, round_dve, conv):
            def link(ins):
                ins.then_inc(dv, 1)
                cc[0] += 1
                dve.wait_ge(dv, cc[0])

            mix_scales(dve, link, 0, mod[:, 16:32], "norm1")
            norm_dve(dve, 3, lambda t: nscale[:, 0, t:t + 1], hf, lambda t: mod[:, t:t + 1])
            dve.wait_ge(*nv.at(3, "h"))
            split_dve(dve, 2, h_lo, h_hi, hf)
            mix_scales(dve, link, 1, modc[:, 16:32], "norm1")
            norm_dve(dve, 4, lambda t: nscale[:, 1, t:t + 1], hf, lambda t: modc[:, t:t + 1], xc)
            dve.wait_ge(*nv.at(4, "h"))
            split_dve(dve, 3, hc_lo, hc_hi, hf)
            dve.wait_ge(*sv.at(3, "lo3"))
            link(dve.tensor_tensor(ts0[:], pcol("ts_prev", 0, 28), pcol("ts_next", 0, 28), ALU.add))
            link(dve.tensor_scalar(ts0[:], ts0[:], -1.0, 1.0, ALU.mult, ALU.add))

            def shift_round(dst, n0, base_n, at0, wide=True):
                def body(i, rnd, k):
                    if k % 2:
                        o = k // 2
                        dve.wait_ge(used, rnd * 8 + k + 1)
                        w = T2 if wide else T
                        out = dst[:, ds(i * 4 + (n0 + o), 1), :].rearrange("p a t -> p (a t)")
                        shifted(dve, out, po[o][:, 0:w], ds(i * 4 + (base_n + o), 1), wide,
                                i * 8 + (at0 + 2 * o), free[o])
                return body

            def low_round(i, rnd, k):
                if k % 2:
                    o = k // 2
                    dve.wait_ge(used, rnd * 8 + k + 1)
                    out = zl[:, o, :] if o < 2 else zg[:, o - 2, :]
                    n = 16 + o if o < 2 else 24 + o
                    shifted(dve, out, po[o][:, 0:T2 if o < 2 else T], slice(n, n + 1), o < 2, i * 8 + (32 + 2 * o), free[o])

            nothing = lambda i, rnd, k: None
            round_dve(dve, "w_in2", 2, shift_round(zk, 0, 0, 0))
            round_dve(dve, "w_in2", 2, shift_round(zv, 0, 8, 16), 2)
            round_dve(dve, "w_in2", 1, nothing, 4)
            round_dve(dve, "w_in2", 1, low_round, 5)
            round_dve(dve, "w_in2", 2, shift_round(zr, 0, 18, 40, False), 6)
            round_dve(dve, "w_in2", 2, nothing, 8)
            dve.wait_ge(att_in, 64)
            all_freed(dve, "w_out2")
            rope_dve(dve, 0, lambda j: kv[:, j, T:T2], 2)
            rope_dve(dve, 2, lambda j: q[:, j, :], 8)
            dve.wait_ge(vta, 2)
            att_dve(dve, 0)
            att_dve(dve, 1)
            dve.wait_ge(rwk_in, 48)
            rk_dve(dve)
            for n, src in enumerate((q, zr)):
                for m in range(2):
                    s = slice(8 * n + 4 * m, 8 * n + 4 * m + 4)
                    dve.wait_ge(*sa.at(4, f"hi{2 * n + m}"))
                    dve.tensor_tensor(o_lo[:, s, :], src[:, 4 * m:4 * m + 4, :], o_hi[:, s, :].bitcast(F32), ALU.subtract)\
                       .then_inc(sv.did(f"lo{2 * n + m}"), 1)

            def on_out(i, rnd, k):
                if k % 2:
                    o = k // 2
                    xt = x[:, ds(i * 4 + o, 1), :]
                    dve.wait_ge(used, rnd * 8 + k + 1)
                    dve.scalar_tensor_tensor(xt, po[o][:, 0:T], mod[:, ds(i * 4 + (32 + o), 1)], xt,
                                             ALU.mult, ALU.add).then_inc(free[o], 1)
            round_dve(dve, "w_out2", 4, on_out)
            mix_scales(dve, link, 0, mod[:, 64:80], "norm2")
            norm_dve(dve, 5, lambda t: nscale[:, 0, t:t + 1], hf, lambda t: mod[:, 48 + t:49 + t])
            dve.wait_ge(*nv.at(5, "h"))
            split_dve(dve, 5, h_lo, h_hi, hf)
            ffn_up_dve(dve, "ffn_up2", 1, round_dve, conv)
            ffn_down_dve(dve, "ffn_down2", 1, True)
            all_freed(dve, "end")
            norm_dve(dve, 6, lambda t: pcol("final2", t), x)

        def block2_pe(pe):
            norm_pe(pe, 3)
            pe.wait_ge(*sv.at(2, "lo3"))
            norm_pe(pe, 4)
            pe.wait_ge(*sv.at(3, "lo3"))
            project2(pe)
            pe.wait_ge(att_in, 64)
            all_freed(pe, "w_out2")
            rope_pe(pe, 0, lambda j: kv[:, j, T:T2], 2)
            rope_pe(pe, 2, lambda j: q[:, j, :], 8)
            att_v_pe(pe)
            pe.wait_ge(vta, 2)
            att_pe(pe, 0)
            att_pe(pe, 1)
            pe.wait_ge(low_a, 3)
            pe.wait_ge(rwk_in, 48)
            rk_pe(pe)
            pe.wait_ge(*sv.at(4, "lo3"))
            project(pe, "w_out2", 4, o_hi, o_lo, 16)
            norm_pe(pe, 5)
            pe.wait_ge(*sv.at(5, "lo3"))
            project(pe, "ffn_up2", 22, h_hi, h_lo, 16)
            pe.wait_ge(ff_lo, 2 * KF)
            project_down(pe, "ffn_down2")
            norm_pe(pe, 6)

        block = ctx.enter_context(nc.Block())

        def chunk_rows(name, per=1):
            return lambda n, c: d[name][ds(n + c, 1)].rearrange("a p w -> p (a w)")

        def down_rows(name):
            return lambda o, s, w: d[name][ds(o, 1), :, s * 2 * PW:s * 2 * PW + w].rearrange("a p w -> p (a w)")

        def load_phase(sp, phase, name, rounds, first=False):
            if first:
                load_round(sp, chunk_rows(name), 0, 0, first=True)
            with sp.Fori(1 if first else 0, rounds) as i:
                load_round(sp, chunk_rows(name), i + ROUND0[phase], i * 4)

        def load_down(sp, phase, name):
            src = down_rows(name)
            with sp.Fori(0, 4) as i:
                for q in range(12):
                    o, s, c = q // 3, q % 3, q % 4
                    rnd = i * 3 + (ROUND0[phase] + q // 4)
                    w = 2 * PW if s < 2 else PW + PW // 2
                    sp.wait_ge(hi_ready, rnd * 8 + (2 * c - 6))
                    sp.wait_ge(lo_ready, rnd * 8 + (2 * c - 6))
                    sp.dma_start(raw[:, c, 0:w], src(i * 4 + o, s, w)).then_inc(landed[c], 16)

        @block.sync
        def _(sp):
            sp.dma_start(cv[:], d["c"]).then_inc(cv_in, 16)
            sp.dma_start(par[:], d["params"]).then_inc(par_in, 16)
            sp.dma_start(ident[:], d["ident"]).then_inc(par_in, 16)
            sp.dma_start(x[:], d["x"]).then_inc(x_in, 16)
            sp.dma_start(w_ab[:], d["w_ab"]).then_inc(ab_in, 16)
            load_ada(sp)
            load_phase(sp, "w_in", "w_in", 18, first=True)
            load_phase(sp, "glu", "glu", 4)
            load_phase(sp, "dn_proj", "dn_proj", 2)
            load_phase(sp, "w_out", "w_out", 4)
            load_phase(sp, "ffn_up", "ffn_up", 22)
            load_down(sp, "ffn_down", "ffn_down")
            block2_sp(sp)

        @block.gpsimd
        def _(pool):
            pool.wait_ge(used, 144)
            pool.dma_start(s_io[:], d["iota"]).then_inc(io_in, 16)
            pool.dma_start(masks[:], d["masks"][:, 0:8, :]).then_inc(mask_in, 16)
            s5_pool(pool)
            block2_pool(pool)

        @block.scalar
        def _(act):
            ac = [0]

            def evacuate(bank):
                return po[bank][:, 0:T]

            def round_act(act, phase, rounds, body, r_off=0):
                with act.Fori(0, rounds) as i:
                    for k in range(8):
                        split_hi(act, i + (ROUND0[phase] + r_off), k + LOOK)
                        body(i, i + (ROUND0[phase] + r_off), k)

            act.wait_ge(cv_in, 16)
            act.activation(cve[:], cv[:], ACT.Silu).then_inc(cva.did("silu"), 1)
            for k in range(LOOK):
                act.wait_ge(landed[k // 2], 16)
                act.activation(w_hi[:, k, :], raw[:, k // 2, (k % 2) * PW:(k % 2) * PW + PW], ACT.Copy)\
                   .then_inc(hi_ready, 1)
            act.wait_ge(x_in, 16)
            norm_act(act, 0)
            act.wait_ge(*nv.at(0, "h"))
            split_act(act, 0, h_hi, hf)
            act.wait_ge(ab_done, 1)
            act.activation(graw[0:HEADS], pa[1][0:HEADS, :].rearrange("p (a t) -> p a t", a=2), ACT.Copy)\
               .then_inc(ab_read, 1)

            def on_u(i, rnd, k):
                if k % 2:
                    act.wait_ge(used, rnd * 8 + k + 1)
                    settle(act)
                    act.activation(u[:, ds(i * 4 + k // 2, 1), :], evacuate(k // 2), ACT.Copy)\
                       .then_inc(free[k // 2], 1)
            round_act(act, "w_in", 2, on_u)

            def on_qkv(i, rnd, k):
                def silu(o):
                    act.wait_ge(*freed("w_in", i, 4, o, 2))
                    settle(act)
                    act.activation(qkv[:, ds(i * 4 + o, 1), :], cacc[:, o, :], ACT.Silu).then_inc(conv_read, 1)
                if k % 2 == 0 and k:
                    silu(k // 2 - 1)
                if k == 7:
                    silu(3)
            round_act(act, "w_in", 6, on_qkv, 2)

            def on_z(i, rnd, k):
                if k % 2:
                    act.wait_ge(used, rnd * 8 + k + 1)
                    settle(act)
                    act.activation(z[:, ds(i * 4 + k // 2, 1), :], evacuate(k // 2), ACT.Silu)\
                       .then_inc(free[k // 2], 1)
            round_act(act, "w_in", 2, on_z, 8)

            def on_gate(i, rnd, k):
                if k % 2:
                    act.wait_ge(used, rnd * 8 + k + 1)
                    settle(act)
                    act.activation(gates[:, ds(i * 4 + k // 2, 1), :], evacuate(k // 2), ACT.Sigmoid)\
                       .then_inc(free[k // 2], 1)
            round_act(act, "w_in", 8, on_gate, 10)

            act.wait_ge(used, 144)
            s5_coef_act(act)
            s5_act(act)
            act.wait_ge(*s5v.before(8))
            act.wait_ge(*s5p.before(8))
            unit_act(act, 0, 0)
            unit_act(act, 1, 8)
            rows_act(act)
            dn_act(act)
            act.wait_ge(*dnv.before(4))
            act.activation(ys_hi[:], u[:], ACT.Copy).then_inc(branch_done, 1)
            act.activation(yd_hi[:], z[:], ACT.Copy).then_inc(branch_done, 1)

            def on_glu(i, rnd, k):
                if k % 2:
                    act.wait_ge(used, rnd * 8 + k + 1)
                    act.wait_ge(*glu_v.before(i * 4 + k // 2))
                    act.activation(sg[:, 0, :], evacuate(k % 4), ACT.Sigmoid).then_inc(free[k % 4], 1)
            round_act(act, "glu", 4, on_glu)

            def on_merge(i, rnd, k):
                act.wait_ge(*mrg_v.at(i * 8 + k, "sum"))
                o = ds(i * 8 + k, 1)
                settle(act)
                act.activation(m_hi[:, o, :], gates[:, o, :], ACT.Copy).then_inc(mrg_a, 1)
            round_act(act, "dn_proj", 2, on_merge)
            round_act(act, "w_out", 4, lambda i, rnd, k: None)
            all_freed(act, "ffn_up")
            norm_act(act, 1)
            act.wait_ge(*nv.at(1, "h"))
            split_act(act, 1, h_hi, hf)
            ffn_up_act(act, "ffn_up", 0, round_act)
            ffn_down_act(act, "ffn_down")
            all_freed(act, "w_in2")
            norm_act(act, 2)
            block2_act(act, round_act)

        @block.vector
        def _(dve):
            def link(ins):
                ins.then_inc(dv, 1)
                cc[0] += 1
                dve.wait_ge(dv, cc[0])

            def round_dve(dve, phase, rounds, body, r_off=0):
                with dve.Fori(0, rounds) as i:
                    for k in range(8):
                        body(i, i + (ROUND0[phase] + r_off), k)
                        split_lo(dve, i + (ROUND0[phase] + r_off), k + LOOK)

            def nothing(i, rnd, k):
                pass

            dve.memset(ones[:], 1.0).then_inc(ones_set, 1)
            dve.wait_ge(par_in, 32)
            ada_dve(dve)
            for k in range(LOOK):
                split_lo(dve, 0, k)
            norm_dve(dve, 0, lambda t: pcol("mix_norm", t), hf)
            dve.wait_ge(*nv.at(0, "h"))
            split_dve(dve, 0, h_lo, h_hi, hf)
            round_dve(dve, "w_in", 2, nothing)

            def conv(dve, out, bank, w, taps, at):
                src = po[bank]
                ins = dve.tensor_scalar(out, src[:, 0:T], w(taps - 1), None, ALU.mult)
                for n, j in enumerate(range(taps - 2, -1, -1)):
                    s = taps - 1 - j
                    ins.then_inc(conv_sum, 1)
                    dve.wait_ge(conv_sum, at + (n + 1))
                    ins = dve.scalar_tensor_tensor(out[:, s:T], src[:, 0:T - s], w(j), out[:, s:T],
                                                   ALU.mult, ALU.add)
                return ins

            def on_qkv(i, rnd, k):
                if k % 2:
                    o = k // 2
                    dve.wait_ge(used, rnd * 8 + k + 1)
                    dve.wait_ge(conv_read, i * 4)
                    w = lambda j: par[:, ds(i * 4 + (COL["conv"] + 24 * j + o), 1)]
                    conv(dve, cacc[:, o, :], o, w, 4, i * 12 + 3 * o).then_inc(free[o], 1)
            dve.wait_ge(*sv.at(0, "lo3"))
            dve.wait_ge(ab_done, 1)
            round_dve(dve, "w_in", 6, on_qkv, 2)
            round_dve(dve, "w_in", 2, nothing, 8)
            round_dve(dve, "w_in", 8, nothing, 10)

            dve.wait_ge(used, 144)
            s5_coef_dve(dve, link)
            dve.wait_ge(io_in, 16)
            dve.wait_ge(*s5cv.at(0, "done"))
            s5_dve(dve)
            unit_dve(dve, 0, 0, float(P))
            unit_dve(dve, 1, 8, 1.0)
            rows_dve(dve, link)
            dve.wait_ge(mask_in, 16)
            dve.wait_ge(*rwa.at(0, "cols"))
            dn_dve(dve)
            dve.wait_ge(branch_done, 2)
            dve.tensor_tensor(ys_lo[:], u[:], ys_hi[:].bitcast(F32), ALU.subtract).then_inc(branch_lo, 1)
            dve.tensor_tensor(yd_lo[:], z[:], yd_hi[:].bitcast(F32), ALU.subtract).then_inc(branch_lo, 1)

            def on_glu(i, rnd, k):
                if k % 2:
                    n = i * 4 + k // 2
                    dve.wait_ge(*freed("glu", i, 8, k))
                    dve.tensor_tensor(sg[:, 1, :], po[(k - 1) % 4][:, 0:T], sg[:, 0, :], ALU.mult)\
                       .then_inc(free[(k - 1) % 4], 1)
                    dve.wait_ge(*freed("glu", i, 8, k - 1))
                    g = gates[:, ds(n, 1), :]
                    dve.tensor_tensor(g, g, sg[:, 1, :], ALU.mult).then_inc(glu_v.did("out"), 1)
                    dve.wait_ge(*glu_v.at(n, "out"))
            round_dve(dve, "glu", 4, on_glu)

            def on_merge(i, rnd, k):
                n = i * 8 + k
                dve.wait_ge(used, rnd * 8 + k + 1)
                dve.wait_ge(*mrg_v.before(n))
                dve.tensor_tensor(sg[:, 1, :], po[k % 4][:, 0:T], gates[:, ds(n + 16, 1), :], ALU.mult)\
                   .then_inc(free[k % 4], 1)
                dve.wait_ge(*freed("dn_proj", i, 8, k))
                g = gates[:, ds(n, 1), :]
                dve.tensor_tensor(g, g, sg[:, 1, :], ALU.add).then_inc(mrg_v.did("sum"), 1)
                dve.wait_ge(mrg_a, n + 1)
                dve.tensor_tensor(m_lo[:, ds(n, 1), :], g, m_hi[:, ds(n, 1), :].bitcast(F32), ALU.subtract)\
                   .then_inc(mrg_lo, 1)
            round_dve(dve, "dn_proj", 2, on_merge)

            def on_out(i, rnd, k):
                if k % 2:
                    o = k // 2
                    xt = x[:, ds(i * 4 + o, 1), :]
                    dve.wait_ge(used, rnd * 8 + k + 1)
                    dve.tensor_tensor(xt, po[o][:, 0:T], xt, ALU.add).then_inc(free[o], 1)
            round_dve(dve, "w_out", 4, on_out)
            norm_dve(dve, 1, lambda t: pcol("ffn_norm", t), hf)
            dve.wait_ge(*nv.at(1, "h"))
            split_dve(dve, 1, h_lo, h_hi, hf)
            ffn_up_dve(dve, "ffn_up", 0, round_dve, conv)
            ffn_down_dve(dve, "ffn_down", 0)
            all_freed(dve, "w_in2")
            norm_dve(dve, 2, lambda t: pcol("final_norm", t), x)
            block2_dve(dve, round_dve, conv)

        @block.tensor
        def _(pe):
            ada_pe(pe)
            pe.wait_ge(ones_set, 1)
            norm_pe(pe, 0)
            pe.wait_ge(*nv.at(0, "h"))
            pe.wait_ge(ab_in, 16)
            for n in range(2):
                for t in range(KD):
                    mm = pe.matmul(pa[1][0:HEADS, n * T:n * T + T], w_ab[:, t, n * HEADS:(n + 1) * HEADS], hf[:, t, :],
                                   start=t == 0, stop=t == KD - 1)
            mm.then_inc(ab_done, 1)
            pe.wait_ge(*sv.at(0, "lo3"))
            project(pe, "w_in", 18, h_hi, h_lo, 16)
            s5_pe(pe)
            pe.wait_ge(*s5v.before(8))
            unit_pe(pe, 0)
            unit_pe(pe, 1)
            pe.wait_ge(*l2v.before(8))
            rows_pe(pe)
            pe.wait_ge(*rwa.at(0, "cols"))
            dn_pe(pe)
            pe.wait_ge(branch_lo, 2)
            project(pe, "glu", 4, ys_hi, ys_lo, 8)
            project(pe, "dn_proj", 2, yd_hi, yd_lo, 8)
            pe.wait_ge(mrg_lo, 16)
            project(pe, "w_out", 4, m_hi, m_lo, 16)
            norm_pe(pe, 1)
            pe.wait_ge(*sv.at(1, "lo3"))
            project(pe, "ffn_up", 22, h_hi, h_lo, 16)
            pe.wait_ge(ff_lo, KF)
            project_down(pe, "ffn_down")
            norm_pe(pe, 2)
            block2_pe(pe)



def tiles(w):
    k, n = w.shape
    return np.ascontiguousarray(w.reshape(k // P, P, n // P, P).transpose(2, 1, 0, 3).reshape(n // P, P, k))


def paired(t, order):
    n, p, w = t.shape
    return np.ascontiguousarray(t[order].reshape(n // 2, 2, p, w).transpose(0, 2, 1, 3).reshape(n // 2, p, 2 * w))


def cols(v):
    return np.asarray(v).reshape(-1, P).T


def constants():
    t = np.arange(P)
    same = (t[:, None] // C) == (t[None, :] // C)
    levels = []
    for b in (1, 2, 4, 8, 16, 32):
        levels.append(((t[:, None] // (2 * b)) == (t[None, :] // (2 * b)))
                      & (t[:, None] % (2 * b) >= b) & (t[None, :] % (2 * b) < b))
    before = same & (t[:, None] < t[None, :])
    upto = same & (t[:, None] <= t[None, :])
    masks = np.stack(levels + [before, upto], 1).astype(np.float32)
    masks[:, 6] *= -1.0
    return {"ident": np.eye(P, dtype=np.float32), "masks": np.ascontiguousarray(masks),
            "iota": np.tile(np.arange(T, dtype=np.float32), (P, 1))}


def layout(i):
    a = {k: np.asarray(v) for k, v in i.items()}
    f32 = np.float32
    w_in = a["w_in"][0]
    main = np.concatenate([w_in[:, :5120], w_in[:, 5136:]], axis=1)
    ab = w_in[:, 5120:5136]
    two = np.arange(16)
    inter = lambda n: np.stack([np.arange(n), np.arange(n) + n], 1).reshape(-1)
    out = {
        "w_in": tiles(main),
        "w_ab": np.ascontiguousarray(ab.reshape(KD, P, 16).transpose(1, 0, 2)),
        "glu": paired(tiles(a["s5_glu_w"][0]), inter(16)),
        "dn_proj": paired(tiles(a["dn_proj_w"][0]), two),
        "w_out": tiles(a["w_out"][0]),
        "ffn_up": tiles(a["ffn_up"][0])[inter(KF)],
        "ffn_down": tiles(a["ffn_down"][0]),
        "x": np.ascontiguousarray(a["x"][0].T.reshape(KD, P, T).transpose(1, 0, 2)),
    }
    b = np.stack([a["s5_b_re"][0], a["s5_b_im"][0]])
    c = np.stack([a["s5_c_re"][0], a["s5_c_im"][0]])
    bt = np.zeros((8, P, 2, P), f32)
    ct = np.zeros((8, P, 4, 2, 32), f32)
    for g in range(64):
        j, e = g // 2, g % 2
        t, q = j // 4, j % 4
        for r in range(2):
            bt[t, 32 * q + 16 * e:32 * q + 16 * e + 16, r, 64 * e:64 * e + 64] = b[r, g].T
            ct[t, 64 * e:64 * e + 64, q, r, 16 * e:16 * e + 16] = c[r, g].T
    out["s5_b"], out["s5_c"] = bt, ct
    one = lambda v: np.pad(np.asarray(v, f32)[:, None], ((0, P - len(v)), (0, 0)))
    inter44 = inter(KF)
    parts = {
        "mix_norm": cols(a["mix_norm_w"][0]), "ffn_norm": cols(a["ffn_norm_w"][0]),
        "final_norm": cols(a["final_norm_w"]),
        "a_re": cols(a["s5_a_re"][0].reshape(-1)), "a_im": cols(a["s5_a_im"][0].reshape(-1)),
        "log_dt": cols(np.repeat(a["s5_log_dt"][0], 64)), "s5_d": cols(a["s5_d"][0]),
        "conv": np.concatenate([cols(a["dn_conv_w"][0, j]) for j in range(4)], 1),
        "dn_norm": cols(a["dn_norm_w"][0]), "a_log": one(a["dn_a_log"][0]), "dt_bias": one(a["dn_dt_bias"][0]),
        "ffn_conv": np.concatenate([cols(a["ffn_conv_w"][0, j])[:, inter44] for j in range(3)], 1),
    }
    block2_layout(a, out, parts)
    out["params"] = np.ascontiguousarray(np.concatenate(
        [parts.get(n, np.zeros((P, w), f32)) for n, w in PARAMS], 1), dtype=f32)
    assert out["params"].shape == (P, NPAR)
    out.update(constants())
    constants2(out)
    return out


def kernel(**inputs):
    import concourse.bacc as bacc
    from concourse.bass_utils import run_bass_kernel_spmd

    nc = bacc.Bacc("TRN2", target_bir_lowering=False, num_devices=1)
    arrays = layout(inputs)
    dram = {n: nc.dram_tensor(n, v.shape, mybir.dt.from_np(v.dtype), kind="ExternalInput").ap()
            for n, v in arrays.items()}
    dram["out"] = nc.dram_tensor("out", (P, KD, T), F32, kind="ExternalOutput").ap()
    program(nc, dram)
    r = run_bass_kernel_spmd(nc, [arrays], core_ids=[0])
    y = np.asarray(r.results[0]["out"])
    return np.ascontiguousarray(y.transpose(2, 1, 0).reshape(1, T, D))


def block2_layout(a, out, parts):
    g = {k[:-2]: v for k, v in a.items() if k.endswith("_2")}
    f32 = np.float32
    fm = lambda v: np.ascontiguousarray(v.T.reshape(KD, P, -1).transpose(1, 0, 2))
    out["c"] = np.ascontiguousarray(np.stack([cols(g["c"][0]), cols(g["c_ctx"])], 2))
    out["ctx"] = fm(g["ctx"][0])
    out["ada"] = tiles(g["ada_w"][0])
    w = g["w_in"][0]
    heads = [h for j in range(8) for h in ((j, 4 + j) if j < 4 else (4 + j, 8 + j))]
    q_cols = np.concatenate([np.arange(64) + 64 * h for h in heads])
    r0 = 1536
    sel = lambda lo, n: w[:, lo:lo + n]
    k0, v0, l0 = r0 + 1024, r0 + 2048, r0 + 3072
    pad = np.zeros((D, 96), f32)
    out["w_in2"] = tiles(np.concatenate([
        sel(k0, 1024), sel(v0, 1024), sel(1024, 512), sel(l0, 416), pad, sel(r0, 1024), w[:, q_cols]], 1))
    w_out = g["w_out"][0]
    out["w_out2"] = tiles(np.concatenate([w_out[q_cols], w_out[1024:]], 0))
    inter = np.stack([np.arange(KF), np.arange(KF) + KF], 1).reshape(-1)
    out["ffn_up2"] = tiles(np.concatenate([g["ffn_w1"][0], g["ffn_w3"][0]], 1))[inter]
    out["ffn_down2"] = tiles(g["ffn_w2"][0])
    rk_w = np.zeros((8, P, 4, P), f32)
    wu, au, gu = (v[0].reshape(-1, 8, P) for v in (g["w_up"], g["a_up"], g["g_up"]))
    rk_w[:, :, 0] = wu.transpose(1, 0, 2)
    rk_w[:, :, 1] = au.transpose(1, 0, 2)
    rk_w[:, :, 2] = gu[:P].transpose(1, 0, 2)
    rk_w[:, :32, 3] = gu[P:].transpose(1, 0, 2)
    out["rk_w"] = rk_w
    ts = lambda v: cols(np.concatenate([v[1024:3072], v[3072:3328], v[:1024], v[3328:3488], np.zeros(96, f32)]))
    parts.update({
        "ada_b": cols(g["ada_b"][0]), "norm1": cols(g["norm1_g"][0]), "norm2": cols(g["norm2_g"][0]),
        "final2": cols(g["final_norm_g"]), "sink": np.tile(g["attn_sink"][0][heads], (P, 1)),
        "ts_prev": ts(g["ts_prev"][0]), "ts_next": ts(g["ts_next"][0]),
        "w0": np.concatenate([cols(g["w0"][0, e]) for e in range(2)], 1),
        "a0": np.concatenate([cols(g["a0"][0, e]) for e in range(2)], 1),
        "k_k": cols(g["k_k"][0]), "k_a": cols(g["k_a"][0]), "r_k": cols(g["r_k"][0]),
        "lnx_g": cols(g["lnx_g"][0]), "lnx_b": cols(g["lnx_b"][0]),
    })


def constants2(out):
    t = np.arange(P)
    same = (t[:, None] // C) == (t[None, :] // C)
    extra = np.stack([-(same & (t[:, None] > t[None, :])).astype(np.float32),
                      (same & (t[:, None] >= t[None, :])).astype(np.float32)], 1)
    out["masks"] = np.ascontiguousarray(np.concatenate([out["masks"], extra], 1), dtype=np.float32)
    out["k_bd"] = np.ascontiguousarray(same.astype(np.float32))
    out["k_rst"] = np.tile((np.arange(2 * T) % C != 0).astype(np.float32), (P, 1))
    freqs = (1.0 / (10000.0 ** (np.arange(16, dtype=np.float32) / 16))).astype(np.float32)
    tok = np.arange(T)
    pos = np.stack([tok // 64, tok % 64]).astype(np.float32)
    p = np.arange(P) % 64
    ang = pos[p // 32] * freqs[p % 16][:, None]
    out["t_cos"], out["t_sin"] = np.cos(ang).astype(np.float32), np.sin(ang).astype(np.float32)
    perm = np.zeros((P, P), np.float32)
    for m in range(P):
        if m % 32 < 16:
            perm[m + 16, m] = -1.0
        else:
            perm[m - 16, m] = 1.0
    out["t_perm"] = perm
    qi = np.arange(T).reshape(2, P).T
    band = np.zeros((P, 2, 2 * T), np.float32)
    far = np.abs(qi[:, :, None] - np.arange(T)[None, None, :]) > 128
    band[:, :, T:][far] = -8e30
    out["t_band"] = band
```

```python
import concourse.bass as bass
from concourse import mybir
from contextlib import ExitStack, contextmanager
import numpy as np

F32 = mybir.dt.float32
F32R = mybir.dt.float32r
U32 = mybir.dt.uint32
ALU = mybir.AluOpType
ACT = mybir.ActivationFunctionType
AX = mybir.AxisListType
ds = bass.ds

P = 128
T = 256
D = 2048
KD = D // P
FFN = 5632
KF = FFN // P
EPS = 1e-6
S5_TILES = 32
HEADS = 8
C = 64
NCH = T // C
PIECE = 8
PW = PIECE * P
LOOK = 3
KB = 1024
MAGIC = 12582912.0
TWO_PI = 6.283185307179586
DECAY = float(np.float32(np.exp(-0.5)))
PI_IN = 3.1415925


class Steps:

    def __init__(self, sem, names):
        self.sem, self.names, self.k = sem, names, 0

    def did(self, name):
        assert self.names[self.k % len(self.names)] == name, (self.names[self.k % len(self.names)], name)
        self.k += 1
        return self.sem

    def at(self, i, name):
        return self.sem, i * len(self.names) + (self.names.index(name) + 1)

    def before(self, i, bodies=1):
        return self.sem, i * (bodies * len(self.names))


PHASES = [("w_in", 18), ("glu", 4), ("dn_proj", 2), ("w_out", 4), ("ffn_up", 22), ("ffn_down", 12),
          ("w_in2", 10), ("w_out2", 4), ("ffn_up2", 22), ("ffn_down2", 12)]
ROUND0, _r = {}, 0
for _n, _c in PHASES:
    ROUND0[_n] = _r
    _r += _c
ROUNDS = _r
OUTS = {"w_in": 72, "glu": 32, "dn_proj": 16, "w_out": 16, "ffn_up": 88, "ffn_down": 16,
        "w_in2": 40, "w_out2": 16, "ffn_up2": 88, "ffn_down2": 16}
TURN0, _t = {}, 0
for _n, _c in PHASES:
    TURN0[_n] = _t
    _t += OUTS[_n] // 4
TURN0["end"] = _t

PARAMS = [("mix_norm", 16), ("ffn_norm", 16), ("final_norm", 16), ("a_re", 32), ("a_im", 32),
          ("log_dt", 32), ("s5_d", 8), ("conv", 96), ("dn_norm", 1), ("a_log", 1), ("dt_bias", 1),
          ("ffn_conv", 264), ("ada_b", 96), ("norm1", 16), ("norm2", 16), ("final2", 16),
          ("sink", 16), ("ts_prev", 28), ("ts_next", 28), ("w0", 16), ("a0", 16), ("k_k", 8),
          ("k_a", 8), ("r_k", 8), ("lnx_g", 8), ("lnx_b", 8)]
COL, _c0 = {}, 0
for _n, _c in PARAMS:
    COL[_n] = _c0
    _c0 += _c
NPAR = _c0


def program(nc, d):
    ctx = ExitStack()
    with ctx:
        base = (nc.sbuf_base + 63) // 64 * 64

        def sb(name, shape, offset, dt=F32):
            return nc.alloc_sbuf_tensor_at(name, [P] + list(shape), dt, offset=base + int(offset * KB))

        def sem(name):
            return ctx.enter_context(nc.semaphore(name))

        def steps(name, names):
            return Steps(sem(name), names.split())

        x = sb("x", [KD, T], 0)
        raw = sb("raw", [4, 2 * PW], 16)
        w_hi = sb("w_hi", [4, PW], 48, F32R)
        w_lo = sb("w_lo", [4, PW], 64, F32R)
        par = sb("par", [NPAR], 80)
        ident = sb("ident", [P], 83.5)
        ones = sb("ones", [P], 84)
        rstd = sb("rstd", [T], 84.5)
        var = sb("var", [T], 85.5)
        conv_a = sb("conv_a", [T], 84.5)
        conv_v = sb("conv_v", [T], 85.5)
        mod = sb("mod", [96], 86.5)
        modc = sb("modc", [32], 86.875)
        cv = sb("cv", [KD, 2], 87)
        cve = sb("cve", [KD, 2], 87.125)
        nscale = sb("nscale", [2, KD], 87.25)
        H0, A0, TMP = 87.75, 119.75, 191.75
        h_hi = sb("h_hi", [KD, T], H0, F32R)
        h_lo = sb("h_lo", [KD, T], H0 + 16, F32R)
        hf = sb("hf", [KD, T], TMP)

        def pcol(name, n=0, width=1):
            return par[:, COL[name] + n:COL[name] + n + width]

        gates = sb("gates", [2 * KD, T], A0)
        w_ab = sb("w_ab", [KD, 16], A0)
        qkv = sb("qkv", [24, T], A0 + 32)
        u = sb("u", [8, T], A0 + 56)
        z = sb("z", [8, T], A0 + 64)
        cacc = sb("cacc", [4, T], TMP)
        ada_buf = sb("ada_buf", [2, 4, 512], TMP)
        ada_row = sb("ada_row", [512], 60)
        graw = sb("graw", [2, T], 84.5)
        sg = sb("sg", [2, T], TMP)
        s_bt = sb("s_bt", [2, P], H0)
        s_ct = sb("s_ct", [4, 2, 32], H0 + 1)
        s_cp = sb("s_cp", [2, 4, P], H0 + 2)
        s_u = sb("s_u", [T], H0 + 6)
        s_cos = sb("s_cos", [2, T], H0 + 7)
        s_sin = sb("s_sin", [2, 2, T], H0 + 9)
        s_hs = sb("s_hs", [T], H0 + 13)
        s_fr = sb("s_fr", [2, T], H0 + 14)
        s_rd = sb("s_rd", [T], H0 + 16)
        s_v = sb("s_v", [2, T], H0 + 17)
        s_p = sb("s_p", [2, T], H0 + 19)
        s_z = sb("s_z", [2, T], H0 + 21)
        s_x = sb("s_x", [2, 2, T], H0 + 23)
        s_y = sb("s_y", [T], H0 + 27)
        s_w = sb("s_w", [12, S5_TILES], H0 + 28)
        s_c1 = sb("s_c1", [4, 2, 32], H0 + 29.5)
        s_io = sb("s_io", [T], H0 + 30.5)
        d_sq = sb("d_sq", [2, T], H0)
        d_rn = sb("d_rn", [2, T], H0 + 2)
        d_rows = sb("d_rows", [3, T], H0 + 4)
        d_g = sb("d_g", [2, T], H0 + 7)
        d_cols = sb("d_cols", [2, 3, 8], H0 + 9)
        d_sel = sb("d_sel", [2, 3, T], H0 + 9.25)
        d_k = sb("d_k", [2, T], H0 + 15.25)
        d_q = sb("d_q", [2, T], H0 + 17.25)
        d_v = sb("d_v", [2, T], H0 + 19.25)
        d_kg = sb("d_kg", [2, T], H0 + 21.25)
        d_qg = sb("d_qg", [2, T], H0 + 23.25)
        d_kd = sb("d_kd", [4, P], H0 + 25.25)
        d_bv = sb("d_bv", [4, P], H0 + 27.25)
        d_at = sb("d_at", [4, P], H0 + 29.25)
        d_el = sb("d_el", [2, NCH], H0 + 31.25)
        i_a = sb("i_a", [4, P], TMP)
        i_t = sb("i_t", [4, P], TMP + 2)
        i_tt = sb("i_tt", [4, P], TMP + 4)
        i_p = sb("i_p", [4, P], TMP + 6)
        d_s = sb("d_s", [2, P], TMP + 8)
        d_ur = sb("d_ur", [2, P], TMP + 9)
        d_vn = sb("d_vn", [2, P], TMP + 10)
        masks = sb("masks", [8, P], TMP + 11)
        d_e1 = sb("d_e1", [4, P], H0)
        d_kb = sb("d_kb", [2, T], H0 + 2)
        ys_hi = sb("ys_hi", [8, T], H0, F32R)
        ys_lo = sb("ys_lo", [8, T], H0 + 8, F32R)
        yd_hi = sb("yd_hi", [8, T], H0 + 16, F32R)
        yd_lo = sb("yd_lo", [8, T], H0 + 24, F32R)
        m_hi = sb("m_hi", [KD, T], A0 + 32, F32R)
        m_lo = sb("m_lo", [KD, T], A0 + 48, F32R)
        f_hi = sb("f_hi", [KF, T], A0, F32R)
        f_lo = sb("f_lo", [KF, T], A0 + 44, F32R)

        po = [ctx.enter_context(nc.psum_tensor(f"po{n}", [P, 512], F32)) for n in range(4)]
        pa = [ctx.enter_context(nc.psum_tensor(f"pa{n}", [P, 512], F32)) for n in range(4)]

        par_in = sem("par_in")
        settled = sem("settled")
        x_in = sem("x_in")
        landed = [sem(f"landed{n}") for n in range(4)]
        hi_ready, lo_ready, used = sem("hi_ready"), sem("lo_ready"), sem("used")
        free = [sem(f"free{n}") for n in range(4)]
        out_done = sem("out_done")
        na = steps("na", "sq0 sq1 sq2 sq3 sqrt")
        nv = steps("nv", "var rec h")
        np_ = steps("np_", "sum")
        sa = steps("split_act", "hi0 hi1 hi2 hi3")
        sv = steps("split_dve", "lo0 lo1 lo2 lo3")
        ab_in, ab_done, ab_read = sem("ab_in"), sem("ab_done"), sem("ab_read")
        conv_read = sem("conv_read")
        dv = sem("dve_chain")
        cc = [0]

        def load_round(sp, src, rnd, n, first=False, chunks=range(4)):
            for c in chunks:
                if not first:
                    sp.wait_ge(hi_ready, rnd * 8 + (2 * c + 2 - 8))
                    sp.wait_ge(lo_ready, rnd * 8 + (2 * c + 2 - 8))
                sp.dma_start(raw[:, c, :], src(n, c)).then_inc(landed[c], 16)

        def split_hi(act, rnd, k, width=PW):
            if k >= 8:
                rnd, k = rnd + 1, k - 8
            if k % 2 == 0:
                act.wait_ge(landed[k // 2], rnd * 16 + 16)
            act.wait_ge(used, rnd * 8 + k - 3)
            act.activation(w_hi[:, k % 4, 0:width], raw[:, k // 2, (k % 2) * PW:(k % 2) * PW + width],
                           ACT.Copy).then_inc(hi_ready, 1)

        def split_lo(dve, rnd, k, width=PW):
            if k >= 8:
                rnd, k = rnd + 1, k - 8
            dve.wait_ge(hi_ready, rnd * 8 + k + 1)
            dve.tensor_tensor(w_lo[:, k % 4, 0:width], raw[:, k // 2, (k % 2) * PW:(k % 2) * PW + width],
                              w_hi[:, k % 4, 0:width].bitcast(F32), ALU.subtract).then_inc(lo_ready, 1)

        def products(pe, rnd, k, tiles, bank, act_hi, act_lo, first, last, turn=None):
            if turn is not None:
                pe.wait_ge(free[bank], turn)
            pe.wait_ge(lo_ready, rnd * 8 + k + 1)
            for n, (s, t) in enumerate(tiles):
                hi = w_hi[:, k % 4, s * P:s * P + P]
                lo = w_lo[:, k % 4, s * P:s * P + P]
                end = last and n == len(tiles) - 1
                pe.matmul(po[bank][:, 0:T], lo, act_hi[:, t, :], start=first and n == 0, stop=False)
                pe.matmul(po[bank][:, 0:T], hi, act_lo[:, t, :], start=False, stop=False)
                mm = pe.matmul(po[bank][:, 0:T], hi, act_hi[:, t, :], start=False, stop=end)
            return mm

        def project(pe, phase, rounds, act_hi, act_lo, k_tiles, r_off=0, t_off=0):
            per = 8 if k_tiles == 8 else 4
            with pe.Fori(0, rounds) as i:
                rnd = i + (ROUND0[phase] + r_off)
                for k in range(8):
                    o = k if k_tiles == 8 else k // 2
                    half = 0 if k_tiles == 8 else k % 2
                    turn = None
                    if half == 0:
                        turn = i * (per // 4) + (TURN0[phase] + t_off + o // 4)
                    products(pe, rnd, k, [(s, half * 8 + s) for s in range(8)], o % 4, act_hi, act_lo,
                             half == 0, half == 1 or k_tiles == 8, turn).then_inc(used, 1)

        def project_down(pe, phase):
            with pe.Fori(0, 4) as i:
                for q in range(24):
                    rnd, k, o, s = i * 3 + (ROUND0[phase] + q // 8), q % 8, q // 6, q % 6
                    tiles = [(t, s * 8 + t) for t in range(8 if s < 5 else 4)]
                    products(pe, rnd, k, tiles, o, f_hi, f_lo, s == 0, s == 5,
                             i + TURN0[phase] if s == 0 else None).then_inc(used, 1)

        def down_width(q):
            return PW // 2 if q % 6 == 5 else PW

        def norm_act(act, n, x=x):
            for q in range(4):
                act.activation(hf[:, 4 * q:4 * q + 4, :], x[:, 4 * q:4 * q + 4, :], ACT.Square)\
                   .then_inc(na.did(f"sq{q}"), 1)
            act.wait_ge(*nv.at(n, "var"))
            act.activation(rstd[:], var[:], ACT.Sqrt).then_inc(na.did("sqrt"), 1)

        def norm_pe(pe, n):
            for q in range(4):
                pe.wait_ge(*na.at(n, f"sq{q}"))
                for t in range(4 * q, 4 * q + 4):
                    mm = pe.matmul(pa[0][:, 0:T], ones[:], hf[:, t, :], start=t == 0, stop=t == KD - 1)
            mm.then_inc(np_.did("sum"), 1)

        def norm_dve(dve, n, w, out, shift=None, x=x):
            dve.wait_ge(*np_.at(n, "sum"))
            dve.tensor_scalar(var[:], pa[0][:, 0:T], 1.0 / D, EPS, ALU.mult, ALU.add)\
               .then_inc(nv.did("var"), 1)
            dve.wait_ge(*na.at(n, "sqrt"))
            dve.reciprocal(rstd[:], rstd[:]).then_inc(nv.did("rec"), 1)
            dve.wait_ge(*nv.at(n, "rec"))
            for t in range(KD):
                last = dve.scalar_tensor_tensor(out[:, t, :], x[:, t, :], w(t), rstd[:], ALU.mult, ALU.mult)
                if shift is not None:
                    last.then_inc(dv, 1)
            if shift is not None:
                cc[0] += KD
                dve.wait_ge(dv, cc[0])
                for t in range(KD):
                    last = dve.tensor_scalar(out[:, t, :], out[:, t, :], shift(t), None, ALU.add)
            last.then_inc(nv.did("h"), 1)

        def split_act(act, m, out_hi, src, tiles=4):
            for q in range(4):
                act.activation(out_hi[:, tiles * q:tiles * (q + 1), :], src[:, tiles * q:tiles * (q + 1), :],
                               ACT.Copy).then_inc(sa.did(f"hi{q}"), 1)

        def split_dve(dve, m, out_lo, out_hi, src, tiles=4):
            for q in range(4):
                s = slice(tiles * q, tiles * (q + 1))
                dve.wait_ge(*sa.at(m, f"hi{q}"))
                dve.tensor_tensor(out_lo[:, s, :], src[:, s, :], out_hi[:, s, :].bitcast(F32), ALU.subtract)\
                   .then_inc(sv.did(f"lo{q}"), 1)

        def freed(phase, i, per, o, r_off=0):
            return free[o % 4], i * (per // 4) + (TURN0[phase] + r_off + o // 4 + 1)

        def all_freed(eng, phase):
            for n in range(4):
                eng.wait_ge(free[n], TURN0[phase])

        def settle(eng):
            eng.sem_inc(settled, 1)

        def quarters(bank):
            return bank[:].rearrange("p (m s) -> p m s", m=4)

        def b4(n):
            return quarters(pa[n])

        ada_landed = [sem(f"ada_landed{n}") for n in range(4)]
        ada_used, ada_copied, ada_cols, cv_in = sem("ada_used"), sem("ada_copied"), sem("ada_cols"), sem("cv_in")
        cva = steps("cva", "silu")

        q_names = " ".join
        s5_in, s5_ct_in, io_in, mask_in = sem("s5_in"), sem("s5_ct_in"), sem("io_in"), sem("mask_in")
        s5ca = steps("s5_coef_act", "dt mag sin half")
        s5cv = steps("s5_coef_dve", "p1 p2 done")
        s5v = steps("s5_v", q_names(
            ["f0_0 f1_0 f2_0"] + [(f"f0_{q + 1} f1_{q + 1} f2_{q + 1} " if q < 3 else "")
             + f"c0_{q} c1_{q} c2_{q} c3_{q} v0_{q} v1_{q} v2_{q} zr_{q} zi_{q} x0_{q} x1_{q} x2_{q}"
             for q in range(4)] + ["y"]))
        s5a = steps("s5_a", q_names(["u"] + [f"sp_{q} sn_{q} hs_{q} sq_{q} cos_{q}" for q in range(4)] + ["gelu"]))
        s5p = steps("s5_p", q_names([f"bu_{q}" if q == 0 else f"bu_{q} y_{q - 1}" for q in range(4)] + ["y_3"]))
        l2a = steps("l2_a", "sq sqrt")
        l2v = steps("l2_v", "eps rec mul")
        l2p = steps("l2_p", "sum")
        rwa = steps("rows_act", "beta exp ln ea egc kdec cols")
        rwv = steps("rows_dve", "neg g gc kdec")
        rwp = steps("rows_pe", "cols")
        dna = steps("dn_a", q_names(["k v q e1 bv"] + [f"vn{c}" for c in range(NCH)] + ["sq sqrt"]))
        dnv = steps("dn_v", q_names(
            ["sel df kb el qg kg kd em at aqm aq init"] + [f"ur{c} st{c}" for c in range(NCH)]
            + ["var rec o1 o2"]))
        dnp = steps("dn_p", q_names(
            ["gc eg be kt kk kq vt"] + [f"ks{c} vn{c} o{c} st{c}" for c in range(NCH)] + ["sum"]))
        inv = (sem("inv_pe"), sem("inv_dve"), (i_a, i_t, i_tt, i_p), pa, "tt")
        branch_done = sem("branch_done")
        glu_v = steps("glu_v", "out")
        mrg_v, mrg_a, mrg_lo = steps("mrg_v", "sum"), sem("mrg_hi"), sem("mrg_lo")
        branch_lo, ones_set = sem("branch_lo"), sem("ones_set")
        conv_sum = sem("conv_sum")
        CONV0 = 72
        ff_silu, ff_prod, ff_hi, ff_lo = sem("ff_silu"), sem("ff_prod"), sem("ff_hi"), sem("ff_lo")

        def bc4(ap):
            return ap.broadcast_to([P, 4, P])

        ada_slots = [raw[:, 2, :], raw[:, 3, :]] + [ada_buf[:, n].rearrange("p a n -> p (a n)") for n in range(2)]

        def load_ada(sp):
            def load(block, c):
                sp.dma_start(ada_slots[c], d["ada"][ds(block * 4 + c, 1)].rearrange("a p w -> p (a w)"))\
                  .then_inc(ada_landed[c], 16)
            for c in (2, 3):
                sp.wait_ge(hi_ready, ROUND0["glu"] * 8 + (2 * c - 6))
                sp.wait_ge(lo_ready, ROUND0["glu"] * 8 + (2 * c - 6))
            sp.wait_ge(conv_read, 24)
            for c in range(4):
                load(0, c)
            with sp.Fori(1, 24) as n:
                for c in range(4):
                    sp.wait_ge(ada_used, n * 4 + (c - 3))
                    load(n, c)
            sp.wait_ge(ada_used, 96)

        def ada_chunk(pe, block, m, c):
            pe.wait_ge(ada_landed[c], block * 16 + 16)
            for t in range(4):
                mm = pe.matmul(po[m][0:2, :], cve[:, 4 * c + t, :], ada_slots[c][:, t * 512:t * 512 + 512],
                               start=c == 0 and t == 0, stop=c == 3 and t == 3)
            mm.then_inc(ada_used, 1)

        def ada_columns(pe, block):
            pe.wait_ge(ada_copied, block + 1)
            settle(pe)
            for s in range(4):
                mm = pe.matmul(po[3][:, ds(block * 8 + 2 * s, 2)], ada_row[0:2, s * P:s * P + P], ident[0:2, 0:2],
                               start=True, stop=True)
            mm.then_inc(ada_cols, 1)

        def ada_act(act, block, m):
            act.wait_ge(ada_used, block * 4 + 4)
            act.wait_ge(ada_cols, block)
            act.activation(ada_row[0:2], po[m][0:2, :], ACT.Copy).then_inc(ada_copied, 1)

        def ada_dve(dve):
            dve.wait_ge(ada_cols, 24)
            m = po[3][:, 0:192].rearrange("p (n s) -> p n s", s=2)
            dve.tensor_tensor(mod[:], m[:, :, 0], pcol("ada_b", 0, 96), ALU.add)
            dve.tensor_tensor(modc[:], m[:, 0:32, 1], pcol("ada_b", 0, 32), ALU.add)

        def s5_coef_act(act):
            act.activation(s_w[:, 0, :], pcol("log_dt", 0, 32), ACT.Exp).then_inc(s5ca.did("dt"), 1)
            act.wait_ge(*s5cv.at(0, "p1"))
            act.activation(s_w[:, 2, :], s_w[:, 1, :], ACT.Exp).then_inc(s5ca.did("mag"), 1)
            act.wait_ge(*s5cv.at(0, "p2"))
            act.activation(s_w[:, 6, :], s_w[:, 3, :], ACT.Sin).then_inc(s5ca.did("sin"), 1)
            act.activation(s_w[:, 7, :], s_w[:, 3, :], ACT.Sin, scale=0.5).then_inc(s5ca.did("half"), 1)

        def s5_coef_dve(dve, link):
            w = lambda n: s_w[:, n, :]
            lr, li = pcol("a_re", 0, 32), pcol("a_im", 0, 32)
            link(dve.memset(s_cp[:].bitcast(U32), 0))
            dve.wait_ge(*s5ca.at(0, "dt"))
            link(dve.tensor_tensor(w(3), li, w(0), ALU.mult))
            dve.tensor_tensor(w(1), lr, w(0), ALU.mult).then_inc(s5cv.did("p1"), 1)
            link(dve.tensor_scalar(w(4), w(3), 1 / TWO_PI, MAGIC, ALU.mult, ALU.add))
            link(dve.tensor_scalar(w(4), w(4), MAGIC, None, ALU.subtract))
            for part in (6.28125, 0.0019350051879882812, 3.0199159819567e-07):
                link(dve.scalar_tensor_tensor(w(3), w(4), -part, w(3), ALU.mult, ALU.add))
            link(dve.tensor_scalar(w(5), w(3), 1 / TWO_PI, None, ALU.mult))
            dve.tensor_scalar(w(3), w(3), PI_IN, -PI_IN, ALU.min, ALU.max).then_inc(s5cv.did("p2"), 1)
            dve.wait_ge(*s5ca.at(0, "half"))
            link(dve.tensor_tensor(w(7), w(7), w(7), ALU.mult))
            link(dve.tensor_scalar(w(7), w(7), -2.0, 1.0, ALU.mult, ALU.add))
            link(dve.tensor_tensor(w(8), w(7), w(2), ALU.mult))
            link(dve.tensor_scalar(w(8), w(8), 1.0, None, ALU.subtract))
            link(dve.tensor_tensor(w(9), w(6), w(2), ALU.mult))
            link(dve.tensor_tensor(w(10), lr, lr, ALU.mult))
            link(dve.tensor_tensor(w(11), li, li, ALU.mult))
            link(dve.tensor_tensor(w(10), w(10), w(11), ALU.add))
            link(dve.reciprocal(w(10), w(10)))
            link(dve.tensor_tensor(w(11), w(8), lr, ALU.mult))
            link(dve.tensor_tensor(w(6), w(9), li, ALU.mult))
            link(dve.tensor_tensor(w(11), w(11), w(6), ALU.add))
            link(dve.tensor_tensor(w(11), w(11), w(10), ALU.mult))
            link(dve.tensor_tensor(w(6), w(9), lr, ALU.mult))
            link(dve.tensor_tensor(w(7), w(8), li, ALU.mult))
            link(dve.tensor_tensor(w(6), w(6), w(7), ALU.subtract))
            link(dve.tensor_tensor(w(6), w(6), w(10), ALU.mult))
            dve.tensor_scalar(w(7), w(6), -1.0, None, ALU.mult).then_inc(s5cv.did("done"), 1)

        def s5_pool(pool):
            with pool.Fori(0, 8) as i:
                pool.wait_ge(*s5p.before(i))
                settle(pool)
                pool.dma_start(s_bt[:], d["s5_b"][ds(i, 1)].rearrange("a p r n -> p (a r) n")).then_inc(s5_in, 16)
                pool.wait_ge(*s5v.before(i))
                settle(pool)
                pool.dma_start(s_ct[:], d["s5_c"][ds(i, 1)].rearrange("a p q r n -> p (a q) r n")).then_inc(s5_ct_in, 16)

        def s5_act(act):
            with act.Fori(0, 8) as i:
                act.wait_ge(*s5v.before(i))
                act.wait_ge(*s5p.before(i))
                settle(act)
                act.activation(s_u[:], u[:, ds(i, 1), :], ACT.Copy).then_inc(s5a.did("u"), 1)
                for q in range(4):
                    b = q % 2
                    act.wait_ge(*s5v.at(i, f"f2_{q}"))
                    act.wait_ge(*(s5v.at(i, f"x1_{q - 2}") if q >= 2 else s5v.before(i)))
                    act.activation(s_sin[:, b, 0, :], s_fr[:, b, :], ACT.Sin, scale=2 * PI_IN)\
                       .then_inc(s5a.did(f"sp_{q}"), 1)
                    act.activation(s_sin[:, b, 1, :], s_fr[:, b, :], ACT.Sin, scale=-2 * PI_IN)\
                       .then_inc(s5a.did(f"sn_{q}"), 1)
                    act.wait_ge(*(s5a.at(i, f"cos_{q - 1}") if q else s5a.before(i)))
                    act.activation(s_hs[:], s_fr[:, b, :], ACT.Sin, scale=PI_IN).then_inc(s5a.did(f"hs_{q}"), 1)
                    act.wait_ge(*s5a.at(i, f"hs_{q}"))
                    act.activation(s_hs[:], s_hs[:], ACT.Square).then_inc(s5a.did(f"sq_{q}"), 1)
                    act.wait_ge(*s5a.at(i, f"sq_{q}"))
                    act.activation(s_cos[:, b, :], s_hs[:], ACT.Copy, scale=-2.0, bias=1.0)\
                       .then_inc(s5a.did(f"cos_{q}"), 1)
                    if q == 2:
                        ada_act(act, i * 2, 0)
                act.wait_ge(*s5v.at(i, "y"))
                settle(act)
                act.activation(u[:, ds(i, 1), :], s_y[:], ACT.Gelu).then_inc(s5a.did("gelu"), 1)
                ada_act(act, i * 2 + 1, 1)

        def s5_dve(dve):
            def turns(i, q):
                th = s_w[:, 5, ds(i * 4 + q, 1)]
                dve.wait_ge(*(s5v.at(i, f"f2_{q - 1}") if q else s5v.before(i)))
                dve.tensor_scalar(s_rd[:], s_io[:], th, MAGIC, ALU.mult, ALU.add).then_inc(s5v.did(f"f0_{q}"), 1)
                dve.wait_ge(*s5v.at(i, f"f0_{q}"))
                dve.tensor_scalar(s_rd[:], s_rd[:], MAGIC, None, ALU.subtract).then_inc(s5v.did(f"f1_{q}"), 1)
                dve.wait_ge(*s5v.at(i, f"f1_{q}"))
                dve.wait_ge(*(s5a.at(i, f"hs_{q - 2}") if q >= 2 else s5a.before(i)))
                dve.scalar_tensor_tensor(s_fr[:, q % 2, :], s_io[:], th, s_rd[:], ALU.mult, ALU.subtract)\
                   .then_inc(s5v.did(f"f2_{q}"), 1)

            with dve.Fori(0, 8) as i:
                turns(i, 0)
                dve.wait_ge(s5_ct_in, i * 16 + 16)
                for q in range(4):
                    b = q % 2
                    if q < 3:
                        turns(i, q + 1)
                    cr, ci, nci = (s_w[:, n, ds(i * 4 + q, 1)] for n in (11, 6, 7))
                    re, im = s_ct[:, q, 0, :], s_ct[:, q, 1, :]
                    dve.tensor_scalar(s_c1[:, q, 0, :], im, ci, None, ALU.mult).then_inc(s5v.did(f"c0_{q}"), 1)
                    dve.tensor_scalar(s_c1[:, q, 1, :], im, cr, None, ALU.mult).then_inc(s5v.did(f"c1_{q}"), 1)
                    dve.wait_ge(*s5v.at(i, f"c1_{q}"))
                    dve.wait_ge(*s5p.before(i))
                    dve.scalar_tensor_tensor(s_cp[:, 0, q, 32 * q:32 * q + 32], re, cr, s_c1[:, q, 0, :],
                                             ALU.mult, ALU.subtract).then_inc(s5v.did(f"c2_{q}"), 1)
                    dve.scalar_tensor_tensor(s_cp[:, 1, q, 32 * q:32 * q + 32], re, nci, s_c1[:, q, 1, :],
                                             ALU.mult, ALU.subtract).then_inc(s5v.did(f"c3_{q}"), 1)
                    pq = pa[b][:].rearrange("p (r t) -> p r t", r=2)
                    cos = s_cos[:, b:b + 1, :].broadcast_to([P, 2, T])
                    sin = s_sin[:, b, :, :]
                    rho = s_w[:, 2, ds(i * 4 + q, 1)].broadcast_to([P, T])
                    dve.wait_ge(*s5a.at(i, f"cos_{q}"))
                    dve.wait_ge(*s5p.at(i, f"bu_{q}"))
                    if q:
                        dve.wait_ge(*s5v.at(i, f"x2_{q - 1}"))
                    dve.tensor_tensor(s_v[:], pq, cos, ALU.mult).then_inc(s5v.did(f"v0_{q}"), 1)
                    dve.tensor_tensor(s_p[:], pq[:, ::-1, :], sin, ALU.mult).then_inc(s5v.did(f"v1_{q}"), 1)
                    dve.wait_ge(*s5v.at(i, f"v1_{q}"))
                    dve.tensor_tensor(s_v[:], s_v[:], s_p[:], ALU.add).then_inc(s5v.did(f"v2_{q}"), 1)
                    dve.wait_ge(*s5v.at(i, f"v2_{q}"))
                    dve.tensor_tensor_scan(s_z[:, 0, :], rho, s_v[:, 0, :], 0.0, ALU.mult, ALU.add)\
                       .then_inc(s5v.did(f"zr_{q}"), 1)
                    dve.tensor_tensor_scan(s_z[:, 1, :], rho, s_v[:, 1, :], 0.0, ALU.mult, ALU.add)\
                       .then_inc(s5v.did(f"zi_{q}"), 1)
                    dve.wait_ge(*s5v.at(i, f"zi_{q}"))
                    dve.wait_ge(*(s5p.at(i, f"y_{q - 2}") if q >= 2 else s5p.before(i)))
                    dve.tensor_tensor(s_x[:, b, :, :], s_z[:], cos, ALU.mult).then_inc(s5v.did(f"x0_{q}"), 1)
                    dve.tensor_tensor(s_p[:], s_z[:, ::-1, :], sin, ALU.mult).then_inc(s5v.did(f"x1_{q}"), 1)
                    dve.wait_ge(*s5v.at(i, f"x1_{q}"))
                    dve.tensor_tensor(s_x[:, b, :, :], s_x[:, b, :, :], s_p[:], ALU.subtract)\
                       .then_inc(s5v.did(f"x2_{q}"), 1)
                dve.wait_ge(*s5p.at(i, "y_3"))
                dve.wait_ge(*s5a.before(i))
                dve.scalar_tensor_tensor(s_y[:], s_u[:], par[:, ds(i + COL["s5_d"], 1)], pa[2][:, 0:T],
                                         ALU.mult, ALU.add).then_inc(s5v.did("y"), 1)

        def s5_pe(pe):
            def readout(i, q):
                pe.wait_ge(*s5v.at(i, f"x2_{q}"))
                if q == 0:
                    pe.wait_ge(*s5v.before(i))
                pe.matmul(pa[2][:, 0:T], s_cp[:, 0, q, :], s_x[:, q % 2, 0, :], start=q == 0, stop=False)
                pe.matmul(pa[2][:, 0:T], s_cp[:, 1, q, :], s_x[:, q % 2, 1, :], start=False, stop=q == 3)\
                  .then_inc(s5p.did(f"y_{q}"), 1)

            with pe.Fori(0, 8) as i:
                pe.wait_ge(*s5a.at(i, "u"))
                pe.wait_ge(s5_in, i * 16 + 16)
                for q in range(4):
                    r = slice(32 * q, 32 * q + 32)
                    pe.wait_ge(*(s5v.at(i, f"v1_{q - 2}") if q >= 2 else s5v.before(i)))
                    for n in range(2):
                        mm = pe.matmul(pa[q % 2][:, n * T:n * T + T], s_bt[r, n, :], s_u[r, :], start=True, stop=True)
                    mm.then_inc(s5p.did(f"bu_{q}"), 1)
                    if q:
                        readout(i, q - 1)
                    if q == 3:
                        ada_columns(pe, i * 2)
                    for n in range(2 * q, 2 * q + 2):
                        ada_chunk(pe, i * 2 + n // 4, n // 4, n % 4)
                readout(i, 3)
                ada_columns(pe, i * 2 + 1)

        def unit_act(act, n, base_t):
            with act.Fori(0, 4) as i:
                act.wait_ge(*l2v.before(i + 4 * n))
                settle(act)
                act.activation(d_sq[:], qkv[:, ds(i * 2 + base_t, 2), :], ACT.Square).then_inc(l2a.did("sq"), 1)
                act.wait_ge(*l2v.at(i + 4 * n, "eps"))
                act.activation(d_rn[:], d_rn[:], ACT.Sqrt).then_inc(l2a.did("sqrt"), 1)
                ada_act(act, i + (16 + 4 * n), 0)

        def unit_pe(pe, n):
            with pe.Fori(0, 4) as i:
                pe.wait_ge(*l2a.at(i + 4 * n, "sq"))
                pe.wait_ge(*l2v.before(i + 4 * n))
                pe.matmul(pa[0][:], ones[:], d_sq[:], start=True, stop=True).then_inc(l2p.did("sum"), 1)
                for c in range(4):
                    ada_chunk(pe, i + (16 + 4 * n), 0, c)
                ada_columns(pe, i + (16 + 4 * n))

        def unit_dve(dve, n, base_t, scale):
            with dve.Fori(0, 4) as i:
                j = i + 4 * n
                dve.wait_ge(*l2p.at(j, "sum"))
                dve.tensor_scalar(d_rn[:], pa[0][:].rearrange("p (a t) -> p a t", a=2), EPS, scale,
                                  ALU.add, ALU.mult).then_inc(l2v.did("eps"), 1)
                dve.wait_ge(*l2a.at(j, "sqrt"))
                dve.reciprocal(d_rn[:], d_rn[:]).then_inc(l2v.did("rec"), 1)
                dve.wait_ge(*l2v.at(j, "rec"))
                tile = qkv[:, ds(i * 2 + base_t, 2), :]
                dve.tensor_tensor(tile, tile, d_rn[:], ALU.mult).then_inc(l2v.did("mul"), 1)

        H8 = slice(0, HEADS)

        def rows_act(act):
            act.activation(d_rows[H8, 2, :], graw[H8, 0, :], ACT.Sigmoid).then_inc(rwa.did("beta"), 1)
            act.wait_ge(*rwv.at(0, "neg"))
            act.activation(d_g[H8, 1, :], d_g[H8, 1, :], ACT.Exp).then_inc(rwa.did("exp"), 1)
            act.wait_ge(*rwa.at(0, "exp"))
            act.activation(d_g[H8, 1, :], d_g[H8, 1, :], ACT.Ln, bias=1.0).then_inc(rwa.did("ln"), 1)
            act.activation(d_el[H8, 0, 0:1], pcol("a_log")[H8], ACT.Exp).then_inc(rwa.did("ea"), 1)
            act.wait_ge(*rwv.at(0, "gc"))
            act.activation(d_rows[H8, 1, :], d_rows[H8, 0, :], ACT.Exp).then_inc(rwa.did("egc"), 1)
            act.wait_ge(*rwv.at(0, "kdec"))
            act.activation(d_g[H8, 0, :], d_g[H8, 0, :], ACT.Exp).then_inc(rwa.did("kdec"), 1)
            act.wait_ge(*rwp.at(0, "cols"))
            act.activation(d_cols[:], pa[0][:, 0:48].rearrange("p (a b c) -> p a b c", a=2, b=3), ACT.Copy)\
               .then_inc(rwa.did("cols"), 1)

        def rows_dve(dve, link):
            g0, g1 = d_g[H8, 0, :], d_g[H8, 1, :]
            link(dve.tensor_scalar(g0, graw[H8, 1, :], pcol("dt_bias")[H8], None, ALU.add))
            link(dve.tensor_scalar(g1, g0, -1.0, None, ALU.mult))
            dve.tensor_tensor(g1, g1, g0, ALU.min).then_inc(rwv.did("neg"), 1)
            dve.wait_ge(*rwa.at(0, "ea"))
            link(dve.scalar_tensor_tensor(g1, g0, 0.0, g1, ALU.max, ALU.add))
            dve.tensor_scalar(g1, g1, d_el[H8, 0, 0:1], -1.0, ALU.mult, ALU.mult).then_inc(rwv.did("g"), 1)
            dve.wait_ge(*rwv.at(0, "g"))
            for c in range(NCH):
                last = dve.tensor_tensor_scan(d_rows[H8, 0, c * C:c * C + C], ones[H8, 0:C],
                                              g1[:, c * C:c * C + C], 0.0, ALU.mult, ALU.add)
            last.then_inc(rwv.did("gc"), 1)
            dve.wait_ge(*rwv.at(0, "gc"))
            gcc = d_rows[H8, 0, :].rearrange("p (c t) -> p c t", t=C)
            dve.tensor_tensor(g0.rearrange("p (c t) -> p c t", t=C), gcc[:, :, C - 1:C].broadcast_to([HEADS, NCH, C]),
                              gcc, ALU.subtract).then_inc(rwv.did("kdec"), 1)

        def rows_pe(pe):
            pe.wait_ge(*rwa.at(0, "kdec"))
            for t in range(2):
                for n, r in enumerate((d_rows[H8, 0, :], d_rows[H8, 2, :], d_g[H8, 0, :])):
                    o = (t * 3 + n) * 8
                    mm = pe.transpose(pa[0][:, o:o + 8], r[:, t * P:t * P + P], ident[H8, H8])
            mm.then_inc(rwp.did("cols"), 1)

        def four(pe, out, lhs, rhs):
            for m in range(4):
                mm = pe.matmul(out[:, m * P:m * P + P], lhs[:, m, :],
                               ident[:] if rhs is None else rhs[:, m, :], start=True, stop=True)
            return mm

        def invert_pe(pe, n, sets):
            for by_pe, by_dve, (i_a, i_t, i_tt, i_p), b, want in sets:
                four(pe, b[0], i_a, None).then_inc(by_pe, 1)
            for by_pe, by_dve, (i_a, i_t, i_tt, i_p), b, want in sets:
                pe.wait_ge(by_dve, n * 17 + 1)
                four(pe, b[2], i_p, None).then_inc(by_pe, 1)
            with pe.Fori(1, 5) as l:
                for by_pe, by_dve, (i_a, i_t, i_tt, i_p), b, want in sets:
                    pe.wait_ge(by_dve, n * 17 + l * 3)
                    four(pe, b[0], i_a, i_t).then_inc(by_pe, 1)
                for by_pe, by_dve, (i_a, i_t, i_tt, i_p), b, want in sets:
                    pe.wait_ge(by_dve, n * 17 + l * 3 + 1)
                    four(pe, b[1], i_tt, i_p).then_inc(by_pe, 1)
                    four(pe, b[2], i_p, i_tt).then_inc(by_pe, 1)
            for by_pe, by_dve, (i_a, i_t, i_tt, i_p), b, want in sets:
                pe.wait_ge(by_dve, n * 17 + 15)
                four(pe, b[0], i_a, i_t).then_inc(by_pe, 1)
            for by_pe, by_dve, (i_a, i_t, i_tt, i_p), b, want in sets:
                pe.wait_ge(by_dve, n * 17 + 16)
                (four(pe, b[1], i_tt, i_p) if want == "t" else four(pe, b[2], i_p, i_tt)).then_inc(by_pe, 1)

        def invert_dve(dve, n, sets, masks):
            for by_pe, by_dve, (i_a, i_t, i_tt, i_p), b, want in sets:
                dve.wait_ge(by_pe, n * 16 + 1)
                dve.tensor_tensor(i_p[:], quarters(b[0]), bc4(masks[:, 0:1, :]), ALU.mult).then_inc(by_dve, 1)
            for by_pe, by_dve, (i_a, i_t, i_tt, i_p), b, want in sets:
                dve.wait_ge(by_dve, n * 17 + 1)
                dve.tensor_tensor(i_t[:], i_p[:], bc4(ident[:].unsqueeze(1)), ALU.add).then_inc(by_dve, 1)
                dve.wait_ge(by_pe, n * 16 + 2)
                dve.tensor_tensor(i_tt[:], quarters(b[2]), bc4(ident[:].unsqueeze(1)), ALU.add).then_inc(by_dve, 1)
            with dve.Fori(1, 5) as l:
                for by_pe, by_dve, (i_a, i_t, i_tt, i_p), b, want in sets:
                    dve.wait_ge(by_pe, n * 16 + l * 3)
                    dve.tensor_tensor(i_p[:], quarters(b[0]), bc4(masks[:, ds(l, 1), :]), ALU.mult).then_inc(by_dve, 1)
                for by_pe, by_dve, (i_a, i_t, i_tt, i_p), b, want in sets:
                    dve.wait_ge(by_pe, n * 16 + l * 3 + 1)
                    dve.tensor_tensor(i_t[:], quarters(b[1]), i_t[:], ALU.add).then_inc(by_dve, 1)
                    dve.wait_ge(by_pe, n * 16 + l * 3 + 2)
                    dve.tensor_tensor(i_tt[:], quarters(b[2]), i_tt[:], ALU.add).then_inc(by_dve, 1)
            for by_pe, by_dve, (i_a, i_t, i_tt, i_p), b, want in sets:
                dve.wait_ge(by_pe, n * 16 + 15)
                dve.tensor_tensor(i_p[:], quarters(b[0]), bc4(masks[:, 5:6, :]), ALU.mult).then_inc(by_dve, 1)
            for by_pe, by_dve, (i_a, i_t, i_tt, i_p), b, want in sets:
                dve.wait_ge(by_pe, n * 16 + 16)
                out, product = (i_t, b[1]) if want == "t" else (i_tt, b[2])
                dve.tensor_tensor(out[:], quarters(product), out[:], ALU.add).then_inc(by_dve, 1)

        def tok(c):
            return c // 2, slice(C * (c % 2), C * (c % 2) + C)

        def dn_act(act):
            with act.Fori(0, 4) as i:
                act.wait_ge(*dnv.before(i))
                settle(act)
                act.activation(d_k[:], qkv[:, ds(i * 2 + 8, 2), :], ACT.Copy).then_inc(dna.did("k"), 1)
                act.activation(d_v[:], qkv[:, ds(i * 2 + 16, 2), :], ACT.Copy).then_inc(dna.did("v"), 1)
                act.activation(d_q[:], qkv[:, ds(i * 2, 2), :], ACT.Copy).then_inc(dna.did("q"), 1)
                act.wait_ge(*dnv.at(i, "df"))
                act.activation(d_e1[:], d_e1[:], ACT.Exp).then_inc(dna.did("e1"), 1)
                act.wait_ge(*dnp.at(i, "vt"))
                settle(act)
                for a in range(2):
                    for t in range(2):
                        m = a * 2 + t
                        last = act.activation(d_bv[:, m, :], pa[3][:, m * P:m * P + P], ACT.Copy,
                                              scale=d_cols[:, t, 1, ds(i * 2 + a, 1)])
                last.then_inc(dna.did("bv"), 1)
                for c in range(NCH):
                    _, r = tok(c)
                    act.wait_ge(*dnp.at(i, f"vn{c}"))
                    act.activation(d_vn[r], pa[1][r, 0:2 * P].rearrange("p (a n) -> p a n", a=2), ACT.Copy)\
                       .then_inc(dna.did(f"vn{c}"), 1)
                act.wait_ge(*dnp.at(i, f"st{NCH - 1}"))
                act.activation(d_qg[:], pa[2][:].rearrange("p (a t) -> p a t", a=2), ACT.Square)\
                   .then_inc(dna.did("sq"), 1)
                act.wait_ge(*dnv.at(i, "var"))
                act.activation(d_kg[:], d_kg[:], ACT.Sqrt).then_inc(dna.did("sqrt"), 1)

        def dn_dve(dve):
            def b2(n):
                return pa[n][:].rearrange("p (a t) -> p a t", a=2)

            with dve.Fori(0, 4) as i:
                dve.wait_ge(*dnv.before(i))
                for a in range(2):
                    last = dve.tensor_scalar(d_sel[H8, a], d_rows[H8], ident[H8, ds(i * 2 + a, 1)], None, ALU.mult)
                last.then_inc(dnv.did("sel"), 1)
                dve.wait_ge(*dnp.at(i, "gc"))
                for a in range(2):
                    for t in range(2):
                        last = dve.tensor_scalar(d_e1[:, 2 * a + t, :], pa[0][:, a * T + t * P:a * T + t * P + P],
                                                 d_cols[:, t, 0, ds(i * 2 + a, 1)], 0.0, ALU.subtract, ALU.min)
                last.then_inc(dnv.did("df"), 1)
                dve.wait_ge(*dnp.at(i, "be"))
                dve.wait_ge(*dna.at(i, "k"))
                dve.tensor_tensor(d_kb[:], b2(2), d_k[:], ALU.mult).then_inc(dnv.did("kb"), 1)
                dve.wait_ge(*dnp.at(i, "eg"))
                dve.tensor_copy(d_el[:], b2(1)[:, :, C - 1::C]).then_inc(dnv.did("el"), 1)
                dve.wait_ge(*dna.at(i, "q"))
                dve.tensor_tensor(d_qg[:], b2(1), d_q[:], ALU.mult).then_inc(dnv.did("qg"), 1)
                dve.wait_ge(*dnv.at(i, "kb"))
                dve.tensor_tensor(d_kg[:], b2(1), d_kb[:], ALU.mult).then_inc(dnv.did("kg"), 1)
                dve.wait_ge(*dnp.at(i, "kt"))
                for a in range(2):
                    for t in range(2):
                        m = a * 2 + t
                        last = dve.tensor_scalar(d_kd[:, m, :], pa[3][:, m * P:m * P + P],
                                                 d_cols[:, t, 2, ds(i * 2 + a, 1)], None, ALU.mult)
                last.then_inc(dnv.did("kd"), 1)
                dve.wait_ge(*dna.at(i, "e1"))
                dve.tensor_tensor(i_a[:], d_e1[:], bc4(masks[:, 6:7, :]), ALU.mult).then_inc(dnv.did("em"), 1)
                dve.wait_ge(*dnv.at(i, "em"))
                dve.wait_ge(*dnp.at(i, "kk"))
                dve.tensor_tensor(i_a[:], b4(0), i_a[:], ALU.mult).then_inc(dnv.did("at"), 1)
                dve.tensor_tensor(d_at[:], d_e1[:], bc4(masks[:, 7:8, :]), ALU.mult).then_inc(dnv.did("aqm"), 1)
                dve.wait_ge(*dnv.at(i, "aqm"))
                dve.wait_ge(*dnp.at(i, "kq"))
                dve.tensor_tensor(d_at[:], b4(2), d_at[:], ALU.mult).then_inc(dnv.did("aq"), 1)
                dve.memset(d_s[:], 0.0).then_inc(dnv.did("init"), 1)
                dve.wait_ge(*dnv.at(i, "init"))
                settle(dve)
                invert_dve(dve, i, [inv], masks)
                for c in range(NCH):
                    t, r = tok(c)
                    dve.wait_ge(*dnp.at(i, f"ks{c}"))
                    dve.wait_ge(*dna.at(i, "bv"))
                    bv = d_bv[r].rearrange("p (a t) n -> p a t n", a=2)[:, :, t, :]
                    dve.tensor_tensor(d_ur[r], bv, pa[0][r, 0:2 * P].rearrange("p (a n) -> p a n", a=2),
                                      ALU.subtract).then_inc(dnv.did(f"ur{c}"), 1)
                    dve.wait_ge(*dnp.at(i, f"st{c}"))
                    for a in range(2):
                        last = dve.scalar_tensor_tensor(d_s[:, a, :], d_s[:, a, :], d_el[:, a, c:c + 1],
                                                        pa[3][:, a * P:a * P + P], ALU.mult, ALU.add)
                    last.then_inc(dnv.did(f"st{c}"), 1)
                dve.wait_ge(*dnp.at(i, "sum"))
                dve.tensor_scalar(d_kg[:], b2(0), 1.0 / P, EPS, ALU.mult, ALU.add).then_inc(dnv.did("var"), 1)
                dve.wait_ge(*dna.at(i, "sqrt"))
                dve.reciprocal(d_kg[:], d_kg[:]).then_inc(dnv.did("rec"), 1)
                dve.wait_ge(*dnv.at(i, "rec"))
                dve.scalar_tensor_tensor(d_kb[:], b2(2), pcol("dn_norm"), d_kg[:], ALU.mult, ALU.mult)\
                   .then_inc(dnv.did("o1"), 1)
                dve.wait_ge(*dnv.at(i, "o1"))
                zt = z[:, ds(i * 2, 2), :]
                dve.tensor_tensor(zt, zt, d_kb[:], ALU.mult).then_inc(dnv.did("o2"), 1)

        def dn_pe(pe):
            def each(fn, name):
                for a in range(2):
                    for t in range(2):
                        mm = fn(a, t, slice((2 * a + t) * P, (2 * a + t + 1) * P), slice(t * P, t * P + P))
                mm.then_inc(dnp.did(name), 1)

            with pe.Fori(0, 4) as i:
                pe.wait_ge(*dnv.at(i, "sel"))
                for n, name in enumerate(("gc", "eg", "be")):
                    for a in range(2):
                        mm = pe.matmul(pa[n][:, a * T:a * T + T], ones[H8, :], d_sel[H8, a, n, :], start=True, stop=True)
                    mm.then_inc(dnp.did(name), 1)
                pe.wait_ge(*dna.at(i, "v"))
                each(lambda a, t, m, s: pe.transpose(pa[3][:, m], d_k[:, a, s], ident[:]), "kt")
                pe.wait_ge(*dnv.at(i, "kb"))
                each(lambda a, t, m, s: pe.matmul(pa[0][:, m], d_k[:, a, s], d_kb[:, a, s], start=True, stop=True), "kk")
                pe.wait_ge(*dna.at(i, "q"))
                each(lambda a, t, m, s: pe.matmul(pa[2][:, m], d_k[:, a, s], d_q[:, a, s], start=True, stop=True), "kq")
                pe.wait_ge(*dnv.at(i, "kd"))
                each(lambda a, t, m, s: pe.transpose(pa[3][:, m], d_v[:, a, s], ident[:]), "vt")
                pe.wait_ge(*dnv.at(i, "init"))
                settle(pe)
                invert_pe(pe, i, [inv])
                pe.wait_ge(inv[1], i * 17 + 17)
                pe.wait_ge(*dna.at(i, "bv"))
                for c in range(NCH):
                    t, r = tok(c)
                    cols = slice(c * C, c * C + C)
                    if c:
                        pe.wait_ge(*dnv.at(i, f"st{c - 1}"))
                    for a in range(2):
                        mm = pe.matmul(pa[0][r, a * P:a * P + P], d_kg[:, a, cols], d_s[:, a, :], start=True, stop=True)
                    mm.then_inc(dnp.did(f"ks{c}"), 1)
                    pe.wait_ge(*dnv.at(i, f"ur{c}"))
                    settle(pe)
                    for a in range(2):
                        mm = pe.matmul(pa[1][r, a * P:a * P + P], i_tt[r, 2 * a + t, r], d_ur[r, a, :], start=True, stop=True)
                    mm.then_inc(dnp.did(f"vn{c}"), 1)
                    pe.wait_ge(*dna.at(i, f"vn{c}"))
                    for a in range(2):
                        o = slice(a * T + c * C, a * T + c * C + C)
                        pe.matmul(pa[2][:, o], d_s[:, a, :], d_qg[:, a, cols], start=True, stop=False)
                        mm = pe.matmul(pa[2][:, o], d_vn[r, a, :], d_at[r, 2 * a + t, r], start=False, stop=True)
                    mm.then_inc(dnp.did(f"o{c}"), 1)
                    for a in range(2):
                        mm = pe.matmul(pa[3][:, a * P:a * P + P], d_kd[r, 2 * a + t, :], d_vn[r, a, :], start=True, stop=True)
                    mm.then_inc(dnp.did(f"st{c}"), 1)
                pe.wait_ge(*dna.at(i, "sq"))
                pe.matmul(pa[0][:], ones[:], d_qg[:], start=True, stop=True).then_inc(dnp.did("sum"), 1)

        xc = sb("xc", [KD, T], A0 + 32)
        hc_hi = sb("hc_hi", [KD, T], A0, F32R)
        hc_lo = sb("hc_lo", [KD, T], A0 + 16, F32R)
        T2 = 2 * T
        zk = sb("zk", [8, T2], A0 + 32)
        zv = sb("zv", [8, T2], A0 + 48)
        zl = sb("zl", [2, T2], A0 + 64)
        kv = sb("kv", [4, T2], A0 + 68)
        zg = sb("zg", [2, T], A0 + 76)
        zr = sb("zr", [8, T], A0)
        q = sb("q", [8, T], A0 + 8)
        ts0 = sb("ts0", [28], A0 + 78)
        t_cos = sb("t_cos", [T], H0)
        t_sin = sb("t_sin", [T], H0 + 1)
        t_perm = sb("t_perm", [P], H0 + 2)
        t_rot = sb("t_rot", [T], H0 + 2.5)
        t_q = sb("t_q", [T], H0 + 3.5)
        t_s = sb("t_s", [4, T2], H0 + 4.5)
        t_v = sb("t_v", [4, T], H0 + 12.5)
        t_band = sb("t_band", [2, T2], H0 + 16.5)
        t_pt = sb("t_pt", [4, 4, P], H0 + 20.5)
        t_dg = sb("t_dg", [4, P], H0 + 28.5)
        t_st = sb("t_st", [4, 4], H0 + 30.5)
        def pair(name, shape, offset, size):
            return [sb(f"{name}{e}", shape, offset + e * size) for e in range(2)]
        k_s, k_a = pair("k_s", [T2], H0, 2), pair("k_a", [T2], H0 + 4, 2)
        k_kd = sb("k_kd", [T2], H0 + 8)
        k_cs = sb("k_cs", [T2], H0 + 10)
        k_gi = sb("k_gi", [T2], H0 + 12)
        k_gp = sb("k_gp", [T2], H0 + 14)
        j_a, j_t = pair("j_a", [4, P], H0, 2), pair("j_t", [4, P], H0 + 4, 2)
        j_tt, j_p = pair("j_tt", [4, P], H0 + 8, 2), pair("j_p", [4, P], H0 + 12, 2)
        k_kk = sb("k_kk", [T2], H0 + 16)
        k_vt = sb("k_vt", [4, P], H0 + 18)
        k_g, k_bh, k_kh = (pair(n, [T2], H0 + o, 2) for n, o in (("k_g", 20), ("k_bh", 24), ("k_kh", 28)))
        R2, R3, R4, RAW = A0 + 16, A0 + 68, A0 + 78.25, 32
        k_ah = pair("k_ah", [T2], R2, 2)
        k_rh = pair("k_rh", [T], R2 + 4, 1)
        k_nv = pair("k_nv", [2, P], R2 + 6, 1)
        k_ur, k_u, k_S, k_st = (pair(n, [P], R2 + o, 0.5)
                                for n, o in (("k_ur", 8), ("k_u", 9), ("k_S", 10), ("k_st", 11)))
        k_y = sb("k_y", [T], R2 + 12)
        k_x = sb("k_x", [T], R2 + 13)
        k_bo = sb("k_bo", [T], R2 + 14)
        k_ln = sb("k_ln", [T], R2 + 15)
        k_masks = sb("k_masks", [10, P], R3)
        k_bd = sb("k_bd", [P], R3 + 5)
        k_w = sb("k_w", [4, P], R3 + 5.5)
        k_rst = sb("k_rst", [T2], R4)
        k_nt = pair("k_nt", [4, P], R4 + 2.75, 2)
        k_bt, k_kt, k_ab, k_ak = (pair(n, [4, P], RAW + o, 2)
                                  for n, o in (("k_bt", 0), ("k_kt", 4), ("k_ab", 8), ("k_ak", 12)))
        o_hi = sb("o_hi", [KD, T], H0, F32R)
        o_lo = sb("o_lo", [KD, T], H0 + 16, F32R)

        def order(e):
            return range(NCH) if e == 0 else range(NCH - 1, -1, -1)

        xc_in = sem("xc_in")
        mix_set = sem("mix_set")
        att_in, rwk_in = sem("att_in"), sem("rwk_in")
        k_up_in, k_gate_in = sem("k_up_in"), sem("k_gate_in")
        rop = steps("rope_pe", "rot")
        rov = steps("rope_dve", "sin cos add")
        vtp, vta = sem("att_v_pe"), sem("att_v_act")
        ata = steps("att_act", "q p0 p1 p2 p3 e t0 t1 t2 t3 o")
        atv = steps("att_dve", "s0 s1 s2 s3 m0 m1 m2 m3 c n d den r g0 g1 g2 g3")
        atp = steps("att_pe", "s0 s1 s2 s3 t0 t1 t2 t3 o")
        low_a = sem("low_act")
        def turns_of(x, names):
            return " ".join(n.format(e=e, x=x, c=order(e)[s]) for s in range(NCH) for group in names
                            for e in range(2) for n in group)

        rka = steps("rk_a", "sqrt s0 a0 s1 a1 vt "
                    + " ".join(f"g{e} gi{e} gp{e} bt{e} kt{e}" for e in range(2)) + " "
                    + " ".join(f"nv0{x} nv1{x} " + turns_of(x, [["u{e}{x}{c}"]]) for x in "cl")
                    + " y0 sq2 sqrt2")
        rkv = steps("rk_v", "kq sq vs eps rec kk "
                    + " ".join(f"cs{e} sm{e} t{e} kd{e} b0{e} b1{e} kh{e} ah{e} rh{e} bo{e}" for e in range(2))
                    + " bo2 "
                    + " ".join((" ".join(f"im{e}{x} nt{e}{x}" + (f" ab{e}{x} ak{e}{x}" if x == "l" else "")
                                         for e in range(2))) + (" init " if x == "c" else " ")
                               + turns_of(x, [["ur{e}{x}{c}"], ["sa{e}{x}{c}", "sb{e}{x}{c}"]]) for x in "cl")
                    + " y1 yc eps2 rec2 n1 n2 bv add out")
        rkp = steps("rk_p", "sum s0 a0 s1 a1 vt bt0 kt0 bt1 kt1 "
                    + " ".join(f"head0{x} head1{x} "
                               + " ".join(f"im{e}{x} nt{e}{x}" + (f" ab{e}{x} ak{e}{x}" if x == "l" else "")
                                          for e in range(2)) + f" nv0{x} nv1{x} "
                               + turns_of(x, [["ks{e}{x}{c}"], ["u{e}{x}{c}"],
                                              (["y{e}{x}{c}"] if x == "l" else []) + ["st{e}{x}{c}"]])
                               for x in "cl")
                    + " mean gate bonus var")
        bank = (pa, po)
        jinv = [(sem(f"jinv_pe{e}"), sem(f"jinv_dve{e}"), (j_a[e], j_t[e], j_tt[e], j_p[e]), bank[e],
                 "tt" if e == 0 else "t") for e in range(2)]

        def mix_scales(dve, link, row, scale, g):
            link(dve.scalar_tensor_tensor(nscale[:, row, :], scale, 1.0, pcol(g, 0, KD), ALU.add, ALU.mult))

        def project2(pe):
            def piece(rnd, k, o, half, wide, turn):
                tiles = [(s, half * 8 + s) for s in range(8)]
                if not wide:
                    return products(pe, rnd, k, tiles, o % 4, h_hi, h_lo, half == 0, half == 1, turn)
                if turn is not None:
                    pe.wait_ge(free[o % 4], turn)
                pe.wait_ge(lo_ready, rnd * 8 + k + 1)
                for n, (s, t) in enumerate(tiles):
                    hi, lo = (w[:, k % 4, s * P:s * P + P] for w in (w_hi, w_lo))
                    for w, ctx_in, lat_in, last in ((lo, hc_hi, h_hi, False), (hi, hc_lo, h_lo, False),
                                                    (hi, hc_hi, h_hi, True)):
                        first = half == 0 and n == 0 and w is lo
                        end = half == 1 and n == 7 and last
                        pe.matmul(po[o % 4][:, 0:T], w, ctx_in[:, t, :], start=first, stop=False,
                                  skip_group_check=True)
                        mm = pe.matmul(po[o % 4][:, T:T2], w, lat_in[:, t, :], start=False, stop=end,
                                       skip_group_check=True)
                return mm

            def part(rounds, r_off, wide):
                with pe.Fori(0, rounds) as i:
                    for k in range(8):
                        turn = i + (TURN0["w_in2"] + r_off) if k % 2 == 0 else None
                        piece(i + (ROUND0["w_in2"] + r_off), k, k // 2, k % 2, wide(k // 2), turn).then_inc(used, 1)

            part(5, 0, lambda o: True)
            part(1, 5, lambda o: o < 2)
            part(4, 6, lambda o: False)

        def shifted(dve, out, src, n, wide, at, inc):
            if wide:
                out, src = (v.rearrange("p (s t) -> p s t", s=2) for v in (out, src))
                a, b = (slice(None), slice(1, T)), (slice(None), slice(0, T - 1))
            else:
                a, b = (slice(1, T),), (slice(0, T - 1),)
            P0 = (slice(None),)
            dve.tensor_scalar(out, src, ts0[:, n], None, ALU.mult).then_inc(shift_sum, 1)
            dve.wait_ge(shift_sum, at + 1)
            dve.scalar_tensor_tensor(out[P0 + a], src[P0 + b], par[:, ds_of(COL["ts_prev"], n)], out[P0 + a],
                                     ALU.mult, ALU.add).then_inc(shift_sum, 1)
            dve.wait_ge(shift_sum, at + 2)
            dve.scalar_tensor_tensor(out[P0 + b], src[P0 + a], par[:, ds_of(COL["ts_next"], n)], out[P0 + b],
                                     ALU.mult, ALU.add).then_inc(inc, 1)

        shift_sum = sem("shift_sum")

        def ds_of(col, n):
            return ds(n.start + col, 1) if not isinstance(n, slice) else slice(col + n.start, col + n.start + 1)

        def rope_pe(pe, n0, tile, count):
            for j in range(count):
                pe.wait_ge(*rov.before(n0 + j))
                pe.matmul(pa[0][:, 0:T], t_perm[:], tile(j), start=True, stop=True).then_inc(rop.did("rot"), 1)

        def rope_dve(dve, n0, tile, count):
            for j in range(count):
                n = n0 + j
                dve.wait_ge(*rop.at(n, "rot"))
                dve.tensor_tensor(t_rot[:], pa[0][:, 0:T], t_sin[:], ALU.mult).then_inc(rov.did("sin"), 1)
                dve.tensor_tensor(tile(j), tile(j), t_cos[:], ALU.mult).then_inc(rov.did("cos"), 1)
                dve.wait_ge(*rov.at(n, "cos"))
                dve.tensor_tensor(tile(j), tile(j), t_rot[:], ALU.add).then_inc(rov.did("add"), 1)
                dve.wait_ge(*rov.at(n, "add"))

        def att_v_pe(pe):
            for j in range(2):
                if j:
                    pe.wait_ge(vta, j)
                for n in range(4):
                    mm = pe.transpose(pa[1][:, n * P:n * P + P], kv[:, 2 + j, n * P:n * P + P], ident[:])
                mm.then_inc(vtp, 1)

        def att_v_act(act):
            for j in range(2):
                act.wait_ge(vtp, j + 1)
                act.activation(t_v[:, :, j * P:j * P + P], pa[1][:].rearrange("p (n c) -> p n c", n=4), ACT.Copy)\
                   .then_inc(vta, 1)

        def att_pe(pe, g):
            with pe.Fori(0, 4) as i:
                b = i + 4 * g
                pe.wait_ge(*ata.at(b, "q"))
                pe.wait_ge(*atv.before(b))
                settle(pe)
                for n in range(4):
                    r, q0 = slice(64 * (n // 2), 64 * (n // 2) + 64), n % 2 * P
                    pe.matmul(pa[n][:], t_q[r, q0:q0 + P], kv[r, g, :], start=True, stop=True)\
                      .then_inc(atp.did(f"s{n}"), 1)
                for n in range(4):
                    pe.wait_ge(*atv.at(b, f"g{n}"))
                    for kb in range(4):
                        mm = pe.matmul(po[n][:, kb * P:kb * P + P], t_s[:, n, kb * P:kb * P + P], t_dg[:, n, :],
                                       start=True, stop=True)
                    mm.then_inc(atp.did(f"t{n}"), 1)
                for n in range(4):
                    r, q0 = slice(64 * (n // 2), 64 * (n // 2) + 64), n % 2 * P
                    pe.wait_ge(*ata.at(b, f"t{n}"))
                    vcol = slice((2 * g + n // 2) * 64, (2 * g + n // 2) * 64 + 64)
                    for kb in range(4):
                        mm = pe.matmul(po[0][r, q0:q0 + P], t_v[:, kb, vcol], t_pt[:, n, kb, :],
                                       start=kb == 0, stop=kb == 3)
                mm.then_inc(atp.did("o"), 1)

        def att_act(act, g):
            with act.Fori(0, 4) as i:
                b = i + 4 * g
                act.wait_ge(*ata.before(b))
                settle(act)
                act.activation(t_q[:], q[:, ds(b, 1), :], ACT.Copy).then_inc(ata.did("q"), 1)
                act.wait_ge(*atv.at(b, "n"))
                for n in range(4):
                    act.activation(t_s[:, n, :], t_s[:, n, :], ACT.Exp, bias=t_st[:, 1, n:n + 1], scale=0.125,
                                   accum_out=t_st[:, 2, n:n + 1]).then_inc(ata.did(f"p{n}"), 1)
                act.wait_ge(*atv.at(b, "d"))
                act.activation(t_st[:, 3, :], t_st[:, 3, :], ACT.Exp).then_inc(ata.did("e"), 1)
                for n in range(4):
                    act.wait_ge(*atp.at(b, f"t{n}"))
                    act.activation(t_pt[:, n], quarters(po[n]), ACT.Copy).then_inc(ata.did(f"t{n}"), 1)
                act.wait_ge(*atp.at(b, "o"))
                settle(act)
                act.activation(q[:, ds(b, 1), :], po[0][:, 0:T], ACT.Copy).then_inc(ata.did("o"), 1)

        def att_dve(dve, g):
            with dve.Fori(0, 4) as i:
                b = i + 4 * g
                sink = par[:, ds(b * 2 + COL["sink"], 2)].unsqueeze(2).broadcast_to([P, 2, 2])
                st = [t_st[:, k, :].rearrange("p (a n) -> p a n", a=2) for k in range(4)]
                dve.wait_ge(*ata.before(b))
                for n in range(4):
                    dve.wait_ge(*atp.at(b, f"s{n}"))
                    dve.tensor_tensor(t_s[:, n, :], pa[n][:], t_band[:, n % 2, :], ALU.add).then_inc(atv.did(f"s{n}"), 1)
                for n in range(4):
                    dve.wait_ge(*atv.at(b, f"s{n}"))
                    dve.tensor_reduce(t_st[:, 0, n:n + 1], t_s[:, n, :], AX.X, ALU.max).then_inc(atv.did(f"m{n}"), 1)
                dve.wait_ge(*atv.at(b, "m3"))
                dve.scalar_tensor_tensor(st[0], st[0], 0.125, sink, ALU.mult, ALU.max).then_inc(atv.did("c"), 1)
                dve.wait_ge(*atv.at(b, "c"))
                dve.tensor_scalar(st[1], st[0], -1.0, None, ALU.mult).then_inc(atv.did("n"), 1)
                dve.tensor_tensor(st[3], sink, st[0], ALU.subtract).then_inc(atv.did("d"), 1)
                dve.wait_ge(*ata.at(b, "e"))
                dve.tensor_tensor(st[2], st[2], st[3], ALU.add).then_inc(atv.did("den"), 1)
                dve.wait_ge(*atv.at(b, "den"))
                dve.reciprocal(st[2], st[2]).then_inc(atv.did("r"), 1)
                dve.wait_ge(*atv.at(b, "r"))
                for n in range(4):
                    dve.tensor_scalar(t_dg[:, n, :], ident[:], t_st[:, 2, n:n + 1], None, ALU.mult)\
                       .then_inc(atv.did(f"g{n}"), 1)

        def ffn_up_act(act, phase, f, round_act):
            def body(i, rnd, k):
                j = i * 2 + k // 4
                if k % 4 == 1 and f == 0:
                    act.wait_ge(*freed(phase, i, 4, k // 2))
                    act.activation(conv_a[:], conv_a[:], ACT.Silu).then_inc(ff_silu, 1)
                if k % 4 == 1 and f == 1:
                    act.wait_ge(used, rnd * 8 + k + 1)
                    act.wait_ge(ff_prod, j + KF)
                    act.activation(conv_a[:], po[k // 2][:, 0:T], ACT.Silu).then_inc(free[k // 2], 1)
                if k % 4 == 3:
                    act.wait_ge(ff_prod, j + (KF * f + 1))
                    settle(act)
                    act.activation(f_hi[:, ds(j, 1), :], conv_v[:], ACT.Copy).then_inc(ff_hi, 1)
            round_act(act, phase, 22, body)

        def ffn_up_dve(dve, phase, f, round_dve, conv):
            def body(i, rnd, k):
                o, j = k // 2, i * 2 + k // 4
                w = lambda n: par[:, ds(i * 4 + (COL["ffn_conv"] + 88 * n + o), 1)]
                at = i * 8 + (CONV0 + 2 * o)
                if k % 4 == 1 and f == 0:
                    dve.wait_ge(used, rnd * 8 + k + 1)
                    conv(dve, conv_a[:], o, w, 3, at).then_inc(free[o], 1)
                if k % 4 == 3:
                    dve.wait_ge(used, rnd * 8 + k + 1)
                    if f == 0:
                        conv(dve, conv_v[:], o, w, 3, at).then_inc(free[o], 1)
                        dve.wait_ge(*freed(phase, i, 4, o))
                        dve.wait_ge(ff_silu, j + 1)
                        dve.tensor_tensor(conv_v[:], conv_v[:], conv_a[:], ALU.mult).then_inc(ff_prod, 1)
                        dve.wait_ge(ff_prod, j + 1)
                    else:
                        dve.wait_ge(*freed(phase, i, 4, o - 1))
                        dve.tensor_tensor(conv_v[:], po[o][:, 0:T], conv_a[:], ALU.mult).then_inc(free[o], 1)
                        dve.wait_ge(*freed(phase, i, 4, o))
                        dve.sem_inc(ff_prod, 1)
                    dve.wait_ge(ff_hi, j + (KF * f + 1))
                    dve.tensor_tensor(f_lo[:, ds(j, 1), :], conv_v[:], f_hi[:, ds(j, 1), :].bitcast(F32),
                                      ALU.subtract).then_inc(ff_lo, 1)
            round_dve(dve, phase, 22, body)

        def ffn_down_act(act, phase, final=False):
            def body(i, final):
                for q in range(24):
                    if not final or q + LOOK < 24:
                        split_hi(act, i * 3 + (ROUND0[phase] + q // 8), q % 8 + LOOK, down_width(q + LOOK))
            with act.Fori(0, 3 if final else 4) as i:
                body(i, False)
            if final:
                body(3, True)

        def ffn_down_dve(dve, phase, f, final=False):
            def body(i, final):
                for q in range(24):
                    rnd = i * 3 + (ROUND0[phase] + q // 8)
                    if q % 6 == 5:
                        o = q // 6
                        xt = x[:, ds(i * 4 + o, 1), :]
                        dve.wait_ge(used, rnd * 8 + q % 8 + 1)
                        if f:
                            dve.scalar_tensor_tensor(xt, po[o][:, 0:T], mod[:, ds(i * 4 + (80 + o), 1)], xt,
                                                     ALU.mult, ALU.add).then_inc(free[o], 1)
                        else:
                            dve.tensor_tensor(xt, po[o][:, 0:T], xt, ALU.add).then_inc(free[o], 1)
                    if not final or q + LOOK < 24:
                        split_lo(dve, rnd, q % 8 + LOOK, down_width(q + LOOK))
            with dve.Fori(0, 3 if final else 4) as i:
                body(i, False)
            if final:
                body(3, True)


        def half(a):
            return slice(64 * a, 64 * a + 64)

        def off(x):
            return 0 if x == "c" else T

        def rk_pool(pool):
            def load(j, n, landed):
                pool.dma_start(k_w[:, n:n + 2], d["rk_w"][ds(j, 1), :, n:n + 2, :].rearrange("a p n c -> p (a n) c"))\
                    .then_inc(landed, 16)
            load(0, 0, k_up_in)
            load(0, 2, k_gate_in)
            with pool.Fori(1, 8) as j:
                pool.wait_ge(*rkp.at(j - 1, "a1"))
                settle(pool)
                load(j, 0, k_up_in)
                pool.wait_ge(*rkp.before(j))
                settle(pool)
                load(j, 2, k_gate_in)

        def rk_act(act):
            with act.Fori(0, 8) as j:
                def then(ins, name):
                    ins.then_inc(rka.did(name), 1)
                    act.wait_ge(*rka.at(j, name))

                act.wait_ge(*rkv.at(j, "eps"))
                then(act.activation(k_gi[:], k_gi[:], ACT.Sqrt), "sqrt")
                for e in range(2):
                    act.wait_ge(*rkp.at(j, f"s{e}"))
                    settle(act)
                    then(act.activation(k_s[e][:], bank[e][0][:], ACT.Sigmoid, bias=par[:, ds(j + (COL["w0"] + 8 * e), 1)]),
                         f"s{e}")
                    act.wait_ge(*rkp.at(j, f"a{e}"))
                    settle(act)
                    then(act.activation(k_a[e][:], bank[e][1][:], ACT.Sigmoid, bias=par[:, ds(j + (COL["a0"] + 8 * e), 1)]),
                         f"a{e}")
                act.wait_ge(*rkp.at(j, "vt"))
                then(act.activation(k_vt[:], b4(3), ACT.Copy), "vt")
                for e in range(2):
                    act.wait_ge(*rkv.at(j, f"sm{e}"))
                    then(act.activation(k_g[e][:], k_cs[:], ACT.Exp, scale=-DECAY), f"g{e}")
                    then(act.activation(k_gi[:], k_cs[:], ACT.Exp, scale=DECAY), f"gi{e}")
                    then(act.activation(k_gp[:], k_gp[:], ACT.Exp, scale=-DECAY), f"gp{e}")
                    act.wait_ge(*rkp.at(j, f"bt{e}"))
                    then(act.activation(k_bt[e][:], quarters(bank[e][2]), ACT.Copy), f"bt{e}")
                    act.wait_ge(*rkp.at(j, f"kt{e}"))
                    then(act.activation(k_kt[e][:], quarters(bank[e][3]), ACT.Copy), f"kt{e}")
                for x in "cl":
                    for e in range(2):
                        act.wait_ge(*rkp.at(j, f"nv{e}{x}"))
                        act.activation(k_nv[e][:], bank[e][1][:, 0:T].rearrange("p (n c) -> p n c", n=2), ACT.Copy)\
                           .then_inc(rka.did(f"nv{e}{x}"), 1)
                    for s in range(NCH):
                        for e in range(2):
                            c = order(e)[s]
                            r = half(c % 2)
                            act.wait_ge(*rkp.at(j, f"u{e}{x}{c}"))
                            act.activation(k_u[e][r], bank[e][1][r, 0:P], ACT.Copy).then_inc(rka.did(f"u{e}{x}{c}"), 1)
                act.wait_ge(*rkp.at(j, f"y0l{NCH - 1}"))
                then(act.activation(k_y[:], pa[2][:, 0:T], ACT.Copy), "y0")
                act.wait_ge(*rkv.at(j, "yc"))
                then(act.activation(k_ln[:], k_y[:], ACT.Square), "sq2")
                act.wait_ge(*rkv.at(j, "eps2"))
                then(act.activation(k_ln[:], k_ln[:], ACT.Sqrt), "sqrt2")

        def rk_dve(dve):
            with dve.Fori(0, 8) as j:
                def then(ins, name):
                    ins.then_inc(rkv.did(name), 1)
                    dve.wait_ge(*rkv.at(j, name))

                def signal(ins, name):
                    ins.then_inc(rkv.did(name), 1)

                def scale(name, e=0):
                    return par[:, ds(j + (COL[name] + 8 * e), 1)]

                def tile(v, lat=False):
                    w = v[:, ds(j, 1), T:T2] if lat else v[:, ds(j, 1), :]
                    return w.rearrange("p a t -> p (a t)")

                dve.wait_ge(*rkp.before(j))
                then(dve.tensor_scalar(k_kk[:], tile(zk), scale("k_k"), None, ALU.mult), "kq")
                signal(dve.tensor_tensor(k_gi[:], k_kk[:], k_kk[:], ALU.mult), "sq")
                signal(dve.tensor_copy(k_bh[1][:], tile(zv)), "vs")
                dve.wait_ge(*rkp.at(j, "sum"))
                then(dve.tensor_scalar(k_gi[:], pa[2][:], 1e-12, None, ALU.max), "eps")
                dve.wait_ge(*rka.at(j, "sqrt"))
                then(dve.reciprocal(k_gi[:], k_gi[:]), "rec")
                then(dve.tensor_tensor(k_kk[:], k_kk[:], k_gi[:], ALU.mult), "kk")
                for e in range(2):
                    dve.wait_ge(*rka.at(j, f"s{e}"))
                    if e:
                        dve.wait_ge(*rka.at(j, "gi0"))
                    s, b = (k_s[e][:], k_cs[:]) if e == 0 else (k_s[e][:, ::-1], k_cs[:, ::-1])
                    then(dve.tensor_tensor_scan(b, k_rst[:], s, 0.0, ALU.mult, ALU.add), f"cs{e}")
                    signal(dve.tensor_tensor(k_gp[:], k_cs[:], k_s[e][:], ALU.subtract), f"sm{e}")
                    dve.wait_ge(*rka.at(j, f"a{e}"))
                    then(dve.tensor_scalar(k_kd[:], k_a[e][:], 1.0, scale("k_a"), ALU.subtract, ALU.mult), f"t{e}")
                    then(dve.scalar_tensor_tensor(k_kd[:], k_kd[:], 1.0, tile(zk), ALU.add, ALU.mult), f"kd{e}")
                    then(dve.tensor_tensor(k_bh[e][:], k_kk[:], k_a[e][:], ALU.mult), f"b0{e}")
                    dve.wait_ge(*rka.at(j, f"gp{e}"))
                    signal(dve.tensor_tensor(k_bh[e][:], k_bh[e][:], k_gi[:], ALU.mult), f"b1{e}")
                    signal(dve.tensor_tensor(k_kh[e][:], k_kd[:], k_gi[:], ALU.mult), f"kh{e}")
                    signal(dve.tensor_tensor(k_ah[e][:], k_kk[:], k_gp[:], ALU.mult), f"ah{e}")
                    signal(dve.tensor_tensor(k_rh[e][:], tile(zr), k_g[e][:, T:T2], ALU.mult), f"rh{e}")
                    bo = k_bo if e == 0 else k_x
                    then(dve.scalar_tensor_tensor(bo[:], k_kd[:, T:T2], scale("r_k"), tile(zr), ALU.mult, ALU.mult), f"bo{e}")
                then(dve.tensor_tensor(k_bo[:], k_bo[:], k_x[:], ALU.add), "bo2")
                for x in "cl":
                    for e in range(2):
                        m = 6 + 2 * e
                        dve.wait_ge(*rkp.at(j, f"im{e}{x}"))
                        signal(dve.tensor_tensor(j_a[e][:], quarters(bank[e][0]), bc4(k_masks[:, 6:7, :]), ALU.mult),
                               f"im{e}{x}")
                        dve.wait_ge(*rkp.at(j, f"nt{e}{x}"))
                        signal(dve.tensor_tensor(k_nt[e][:], quarters(bank[e][1]), bc4(k_masks[:, m:m + 1, :]), ALU.mult),
                               f"nt{e}{x}")
                        if x == "l":
                            m = bc4(k_masks[:, m + 1:m + 2, :])
                            dve.wait_ge(*rkp.at(j, f"ab{e}{x}"))
                            signal(dve.tensor_tensor(k_ab[e][:], quarters(bank[e][2]), m, ALU.mult), f"ab{e}{x}")
                            dve.wait_ge(*rkp.at(j, f"ak{e}{x}"))
                            signal(dve.tensor_tensor(k_ak[e][:], quarters(bank[e][3]), m, ALU.mult), f"ak{e}{x}")
                    if x == "c":
                        dve.memset(k_S[0][:], 0.0)
                        dve.memset(k_S[1][:], 0.0).then_inc(rkv.did("init"), 1)
                        dve.wait_ge(*rkv.at(j, "init"))
                        settle(dve)
                    invert_dve(dve, j * 2 + (x == "l"), jinv, k_masks)
                    for s in range(NCH):
                        for e in range(2):
                            c = order(e)[s]
                            r, n = half(c % 2), c // 2
                            dve.wait_ge(*rkp.at(j, f"ks{e}{x}{c}"))
                            dve.wait_ge(*rka.at(j, f"nv{e}{x}"))
                            signal(dve.tensor_tensor(k_ur[e][r], k_nv[e][r, n, :], bank[e][0][r, 0:P], ALU.subtract),
                                   f"ur{e}{x}{c}")
                        for e in range(2):
                            c = order(e)[s]
                            end = off(x) + c * C + (C - 1 if e == 0 else 0)
                            g = k_g[e][:, end:end + 1]
                            dve.wait_ge(*rkp.at(j, f"st{e}{x}{c}"))
                            then(dve.scalar_tensor_tensor(k_st[e][:], bank[e][3][:, 0:P], g, k_bd[:], ALU.mult, ALU.mult),
                                 f"sa{e}{x}{c}")
                            signal(dve.scalar_tensor_tensor(k_S[e][:], k_S[e][:], g, k_st[e][:], ALU.mult, ALU.add),
                                   f"sb{e}{x}{c}")
                dve.wait_ge(*rka.at(j, "y0"))
                dve.wait_ge(*rkv.at(j, f"sb1l{0}"))
                then(dve.tensor_tensor(k_y[:], po[2][:, 0:T], k_y[:], ALU.add), "y1")
                dve.wait_ge(*rkp.at(j, "mean"))
                then(dve.scalar_tensor_tensor(k_y[:], pa[0][:, 0:T], -1.0 / 64, k_y[:], ALU.mult, ALU.add), "yc")
                dve.wait_ge(*rkp.at(j, "var"))
                then(dve.tensor_scalar(k_ln[:], pa[0][:, 0:T], 1.0 / 64, 64e-5, ALU.mult, ALU.add), "eps2")
                dve.wait_ge(*rka.at(j, "sqrt2"))
                then(dve.reciprocal(k_ln[:], k_ln[:]), "rec2")
                then(dve.tensor_tensor(k_y[:], k_y[:], k_ln[:], ALU.mult), "n1")
                then(dve.tensor_scalar(k_y[:], k_y[:], scale("lnx_g"), scale("lnx_b"), ALU.mult, ALU.add), "n2")
                dve.wait_ge(*rkp.at(j, "bonus"))
                then(dve.tensor_tensor(k_x[:], pa[2][:, 0:T], tile(zv, True), ALU.mult), "bv")
                then(dve.tensor_tensor(k_y[:], k_y[:], k_x[:], ALU.add), "add")
                then(dve.tensor_tensor(tile(zr), pa[1][:, 0:T], k_y[:], ALU.mult), "out")

        def rk_pe(pe):
            with pe.Fori(0, 8) as j:
                pe.wait_ge(k_up_in, j * 16 + 16)
                pe.wait_ge(*rkv.at(j, "sq"))
                pe.matmul(pa[2][:], k_bd[:], k_gi[:], start=True, stop=True).then_inc(rkp.did("sum"), 1)
                for e in range(2):
                    for n in range(2):
                        pe.matmul(bank[e][n][:], k_w[half(e), n, :], zl[half(e), n, :], start=True, stop=True)\
                          .then_inc(rkp.did("sa"[n] + str(e)), 1)
                pe.wait_ge(*rkv.at(j, "vs"))
                for n in range(4):
                    mm = pe.transpose(pa[3][:, n * P:n * P + P], k_bh[1][:, n * P:n * P + P], ident[:])
                mm.then_inc(rkp.did("vt"), 1)
                for e in range(2):
                    pe.wait_ge(*rkv.at(j, f"b1{e}"))
                    for n in range(4):
                        mm = pe.transpose(bank[e][2][:, n * P:n * P + P], k_bh[e][:, n * P:n * P + P], ident[:])
                    mm.then_inc(rkp.did(f"bt{e}"), 1)
                    pe.wait_ge(*rkv.at(j, f"kh{e}"))
                    if e == 0:
                        pe.wait_ge(*rka.at(j, "vt"))
                    for n in range(4):
                        mm = pe.transpose(bank[e][3][:, n * P:n * P + P], k_kh[e][:, n * P:n * P + P], ident[:])
                    mm.then_inc(rkp.did(f"kt{e}"), 1)
                pe.wait_ge(*rkv.at(j, "bo1"))
                pe.wait_ge(*rka.at(j, "kt1"))
                for x in "cl":
                    if x == "l":
                        for e in range(2):
                            pe.wait_ge(*rkv.at(j, f"sb{e}c{order(e)[-1]}"))
                    for a in range(2):
                        for e in range(2):
                            lhs, rhs = (k_bh[e], k_ah[e]) if e == 0 else (k_ah[e], k_bh[e])
                            products_of = [("im", lhs, rhs), ("nt", k_kh[e], k_ah[e])]
                            if x == "l":
                                products_of += [("ab", k_bh[e], k_rh[e]), ("ak", k_kh[e], k_rh[e])]
                            if a:
                                pe.wait_ge(*rkp.at(j, f"head{e}{x}"))
                            for out, (name, w, m) in zip(bank[e], products_of):
                                for n in range(2):
                                    at = slice(off(x) + n * P, off(x) + n * P + P)
                                    r_at = slice(n * P, n * P + P) if m is k_rh[e] else at
                                    o = (2 * a + n) * P
                                    mm = pe.matmul(out[:, o:o + P], w[half(a), at], m[half(a), r_at],
                                                   start=True, stop=True)
                                if a:
                                    mm.then_inc(rkp.did(f"{name}{e}{x}"), 1)
                            if a == 0:
                                mm.then_inc(rkp.did(f"head{e}{x}"), 1)
                    for e in range(2):
                        pe.wait_ge(*rkv.at(j, f"nt{e}{x}"))
                        for a in range(2):
                            for n in range(2):
                                o = n * P + 64 * a
                                mm = pe.matmul(bank[e][1][:, o:o + 64], k_nt[e][:, 2 * a + n, :],
                                               k_vt[:, n + (2 if x == "l" else 0), half(a)], start=True, stop=True)
                        mm.then_inc(rkp.did(f"nv{e}{x}"), 1)
                    if x == "c":
                        pe.wait_ge(*rkv.at(j, "init"))
                    else:
                        pe.wait_ge(*rkv.at(j, "ak1l"))
                    pe.wait_ge(*rka.at(j, f"nv1{x}"))
                    settle(pe)
                    n_inv = j * 2 + (x == "l")
                    invert_pe(pe, n_inv, jinv)
                    for s in range(NCH):
                        for e in range(2):
                            c = order(e)[s]
                            r = half(c % 2)
                            if s == 0:
                                pe.wait_ge(jinv[e][1], n_inv * 17 + 17)
                            else:
                                pe.wait_ge(*rkv.at(j, f"sb{e}{x}{order(e)[s - 1]}"))
                            pe.matmul(bank[e][0][r, 0:P], k_ah[e][:, off(x) + c * C:off(x) + c * C + C], k_S[e][:],
                                      start=True, stop=True).then_inc(rkp.did(f"ks{e}{x}{c}"), 1)
                        for e in range(2):
                            c = order(e)[s]
                            r, n = half(c % 2), c // 2
                            inv_t = (j_tt, j_t)[e][e]
                            pe.wait_ge(*rkv.at(j, f"ur{e}{x}{c}"))
                            settle(pe)
                            for a in range(2):
                                mm = pe.matmul(bank[e][1][r, half(a)], inv_t[r, 2 * a + n, r], k_ur[e][r, half(a)],
                                               start=True, stop=True)
                            mm.then_inc(rkp.did(f"u{e}{x}{c}"), 1)
                        for e in range(2):
                            c = order(e)[s]
                            r, n = half(c % 2), c // 2
                            blk = n + (2 if x == "l" else 0)
                            pe.wait_ge(*rka.at(j, f"u{e}{x}{c}"))
                            if x == "l":
                                o = slice(c * C, c * C + C)
                                y = bank[e][2]
                                pe.matmul(y[:, o], k_S[e][:], k_rh[e][:, o], start=True, stop=False)
                                for a in range(2):
                                    pe.matmul(y[half(a), o], k_u[e][r, half(a)], k_ab[e][r, 2 * a + n, r],
                                              start=False, stop=False)
                                    mm = pe.matmul(y[half(a), o], k_vt[r, blk, half(a)], k_ak[e][r, 2 * a + n, r],
                                                   start=False, stop=True)
                                mm.then_inc(rkp.did(f"y{e}{x}{c}"), 1)
                            pe.matmul(bank[e][3][:, 0:P], k_bt[e][r, blk, :], k_u[e][r], start=True, stop=False)
                            pe.matmul(bank[e][3][:, 0:P], k_kt[e][r, blk, :], k_vt[r, blk, :], start=False, stop=True)\
                              .then_inc(rkp.did(f"st{e}{x}{c}"), 1)
                pe.wait_ge(*rkv.at(j, "y1"))
                pe.matmul(pa[0][:, 0:T], k_bd[:], k_y[:], start=True, stop=True).then_inc(rkp.did("mean"), 1)
                pe.wait_ge(k_gate_in, j * 16 + 16)
                pe.matmul(pa[1][:, 0:T], k_w[:, 2, :], zg[:, 0, :], start=True, stop=False)
                pe.matmul(pa[1][:, 0:T], k_w[0:32, 3, :], zg[0:32, 1, :], start=False, stop=True)\
                  .then_inc(rkp.did("gate"), 1)
                pe.matmul(pa[2][:, 0:T], k_bd[:], k_bo[:], start=True, stop=True).then_inc(rkp.did("bonus"), 1)
                pe.wait_ge(*rka.at(j, "sq2"))
                pe.matmul(pa[0][:, 0:T], k_bd[:], k_ln[:], start=True, stop=True).then_inc(rkp.did("var"), 1)

        def after_rwkv(sp):
            sp.wait_ge(*rkp.before(8))
            sp.wait_ge(*rka.before(8))
            sp.wait_ge(*rkv.before(8))

        def block2_sp(sp):
            load_phase(sp, "w_in2", "w_in2", 10)
            load_phase(sp, "w_out2", "w_out2", 4, between=after_rwkv)
            load_phase(sp, "ffn_up2", "ffn_up2", 22)
            load_down(sp, "ffn_down2", "ffn_down2")
            sp.wait_ge(*nv.at(6, "h"))
            sp.dma_start(d["out"], x[:]).then_inc(out_done, 16)
            sp.wait_ge(out_done, 16)

        def block2_pool(pool):
            pool.wait_ge(*nv.at(2, "h"))
            pool.dma_start(xc[:], d["ctx"]).then_inc(xc_in, 16)
            pool.wait_ge(used, 8 * ROUND0["w_out2"])
            for t, n in ((t_cos, "t_cos"), (t_sin, "t_sin"), (t_perm, "t_perm"), (t_band, "t_band")):
                pool.dma_start(t[:], d[n]).then_inc(att_in, 16)
            pool.wait_ge(*ata.before(8))
            pool.wait_ge(*atp.before(8))
            for t, n in ((k_masks, "masks"), (k_bd, "k_bd"), (k_rst, "k_rst")):
                pool.dma_start(t[:], d[n]).then_inc(rwk_in, 16)
            rk_pool(pool)

        def block2_act(act, round_act):
            act.wait_ge(*nv.at(2, "h"))
            norm_act(act, 3)
            act.wait_ge(*nv.at(3, "h"))
            split_act(act, 2, h_hi, hf)
            act.wait_ge(*sv.at(2, "lo3"))
            act.wait_ge(xc_in, 16)
            norm_act(act, 4, xc)
            act.wait_ge(*nv.at(4, "h"))
            split_act(act, 3, hc_hi, hf)

            def on_kv(i, rnd, k):
                if k % 2:
                    act.wait_ge(used, rnd * 8 + k + 1)
                    settle(act)
                    act.activation(kv[:, ds(k // 2, 1), :], po[k // 2][:], ACT.Copy).then_inc(free[k // 2], 1)

            def on_q(i, rnd, k):
                if k % 2:
                    act.wait_ge(used, rnd * 8 + k + 1)
                    settle(act)
                    act.activation(q[:, ds(i * 4 + k // 2, 1), :], po[k // 2][:, 0:T], ACT.Copy)\
                       .then_inc(free[k // 2], 1)
            nothing = lambda i, rnd, k: None
            round_act(act, "w_in2", 4, nothing)
            round_act(act, "w_in2", 1, on_kv, 4)
            round_act(act, "w_in2", 3, nothing, 5)
            round_act(act, "w_in2", 2, on_q, 8)
            act.wait_ge(*rov.before(10))
            att_v_act(act)
            att_act(act, 0)
            att_act(act, 1)
            act.activation(zl[:, 0, :], zl[:, 0, :], ACT.Tanh).then_inc(low_a, 1)
            act.activation(zg[:, 0, :], zg[:, 0, :], ACT.Sigmoid).then_inc(low_a, 1)
            act.activation(zg[:, 1, :], zg[:, 1, :], ACT.Sigmoid).then_inc(low_a, 1)
            rk_act(act)
            act.wait_ge(*rkv.before(8))
            for n, src in enumerate((q, zr)):
                for m in range(2):
                    s = slice(8 * n + 4 * m, 8 * n + 4 * m + 4)
                    act.activation(o_hi[:, s, :], src[:, 4 * m:4 * m + 4, :], ACT.Copy).then_inc(sa.did(f"hi{2 * n + m}"), 1)
            round_act(act, "w_out2", 4, nothing)
            all_freed(act, "ffn_up2")
            norm_act(act, 5)
            act.wait_ge(*nv.at(5, "h"))
            split_act(act, 5, h_hi, hf)
            ffn_up_act(act, "ffn_up2", 1, round_act)
            ffn_down_act(act, "ffn_down2", True)
            all_freed(act, "end")
            norm_act(act, 6)

        def block2_dve(dve, round_dve, conv):
            def link(ins):
                ins.then_inc(dv, 1)
                cc[0] += 1
                dve.wait_ge(dv, cc[0])

            mix_scales(dve, link, 0, mod[:, 16:32], "norm1")
            norm_dve(dve, 3, lambda t: nscale[:, 0, t:t + 1], hf, lambda t: mod[:, t:t + 1])
            dve.wait_ge(*nv.at(3, "h"))
            split_dve(dve, 2, h_lo, h_hi, hf)
            mix_scales(dve, link, 1, modc[:, 16:32], "norm1")
            norm_dve(dve, 4, lambda t: nscale[:, 1, t:t + 1], hf, lambda t: modc[:, t:t + 1], xc)
            dve.wait_ge(*nv.at(4, "h"))
            split_dve(dve, 3, hc_lo, hc_hi, hf)
            dve.wait_ge(*sv.at(3, "lo3"))
            link(dve.tensor_tensor(ts0[:], pcol("ts_prev", 0, 28), pcol("ts_next", 0, 28), ALU.add))
            link(dve.tensor_scalar(ts0[:], ts0[:], -1.0, 1.0, ALU.mult, ALU.add))

            def shift_round(dst, n0, base_n, at0, wide=True):
                def body(i, rnd, k):
                    if k % 2:
                        o = k // 2
                        dve.wait_ge(used, rnd * 8 + k + 1)
                        w = T2 if wide else T
                        out = dst[:, ds(i * 4 + (n0 + o), 1), :].rearrange("p a t -> p (a t)")
                        shifted(dve, out, po[o][:, 0:w], ds(i * 4 + (base_n + o), 1), wide,
                                i * 8 + (at0 + 2 * o), free[o])
                return body

            def low_round(i, rnd, k):
                if k % 2:
                    o = k // 2
                    dve.wait_ge(used, rnd * 8 + k + 1)
                    out = zl[:, o, :] if o < 2 else zg[:, o - 2, :]
                    n = 16 + o if o < 2 else 24 + o
                    shifted(dve, out, po[o][:, 0:T2 if o < 2 else T], slice(n, n + 1), o < 2, i * 8 + (32 + 2 * o), free[o])

            nothing = lambda i, rnd, k: None
            round_dve(dve, "w_in2", 2, shift_round(zk, 0, 0, 0))
            round_dve(dve, "w_in2", 2, shift_round(zv, 0, 8, 16), 2)
            round_dve(dve, "w_in2", 1, nothing, 4)
            round_dve(dve, "w_in2", 1, low_round, 5)
            round_dve(dve, "w_in2", 2, shift_round(zr, 0, 18, 40, False), 6)
            round_dve(dve, "w_in2", 2, nothing, 8)
            dve.wait_ge(att_in, 64)
            all_freed(dve, "w_out2")
            rope_dve(dve, 0, lambda j: kv[:, j, T:T2], 2)
            rope_dve(dve, 2, lambda j: q[:, j, :], 8)
            dve.wait_ge(vta, 2)
            att_dve(dve, 0)
            att_dve(dve, 1)
            dve.wait_ge(rwk_in, 48)
            rk_dve(dve)
            for n, src in enumerate((q, zr)):
                for m in range(2):
                    s = slice(8 * n + 4 * m, 8 * n + 4 * m + 4)
                    dve.wait_ge(*sa.at(4, f"hi{2 * n + m}"))
                    dve.tensor_tensor(o_lo[:, s, :], src[:, 4 * m:4 * m + 4, :], o_hi[:, s, :].bitcast(F32), ALU.subtract)\
                       .then_inc(sv.did(f"lo{2 * n + m}"), 1)

            def on_out(i, rnd, k):
                if k % 2:
                    o = k // 2
                    xt = x[:, ds(i * 4 + o, 1), :]
                    dve.wait_ge(used, rnd * 8 + k + 1)
                    dve.scalar_tensor_tensor(xt, po[o][:, 0:T], mod[:, ds(i * 4 + (32 + o), 1)], xt,
                                             ALU.mult, ALU.add).then_inc(free[o], 1)
            round_dve(dve, "w_out2", 4, on_out)
            mix_scales(dve, link, 0, mod[:, 64:80], "norm2")
            norm_dve(dve, 5, lambda t: nscale[:, 0, t:t + 1], hf, lambda t: mod[:, 48 + t:49 + t])
            dve.wait_ge(*nv.at(5, "h"))
            split_dve(dve, 5, h_lo, h_hi, hf)
            ffn_up_dve(dve, "ffn_up2", 1, round_dve, conv)
            ffn_down_dve(dve, "ffn_down2", 1, True)
            all_freed(dve, "end")
            norm_dve(dve, 6, lambda t: pcol("final2", t), x)

        def block2_pe(pe):
            norm_pe(pe, 3)
            pe.wait_ge(*sv.at(2, "lo3"))
            norm_pe(pe, 4)
            pe.wait_ge(*sv.at(3, "lo3"))
            project2(pe)
            pe.wait_ge(att_in, 64)
            all_freed(pe, "w_out2")
            rope_pe(pe, 0, lambda j: kv[:, j, T:T2], 2)
            rope_pe(pe, 2, lambda j: q[:, j, :], 8)
            att_v_pe(pe)
            pe.wait_ge(vta, 2)
            att_pe(pe, 0)
            att_pe(pe, 1)
            pe.wait_ge(low_a, 3)
            pe.wait_ge(rwk_in, 48)
            rk_pe(pe)
            pe.wait_ge(*sv.at(4, "lo3"))
            project(pe, "w_out2", 4, o_hi, o_lo, 16)
            norm_pe(pe, 5)
            pe.wait_ge(*sv.at(5, "lo3"))
            project(pe, "ffn_up2", 22, h_hi, h_lo, 16)
            pe.wait_ge(ff_lo, 2 * KF)
            project_down(pe, "ffn_down2")
            norm_pe(pe, 6)

        block = ctx.enter_context(nc.Block())

        def chunk_rows(name, per=1):
            return lambda n, c: d[name][ds(n + c, 1)].rearrange("a p w -> p (a w)")

        def down_rows(name):
            return lambda o, s, w: d[name][ds(o, 1), :, s * 2 * PW:s * 2 * PW + w].rearrange("a p w -> p (a w)")

        def load_phase(sp, phase, name, rounds, first=False, between=None):
            if first:
                load_round(sp, chunk_rows(name), 0, 0, first=True)
            elif between is not None:
                load_round(sp, chunk_rows(name), ROUND0[phase], 0, chunks=(0, 1))
                between(sp)
                load_round(sp, chunk_rows(name), ROUND0[phase], 0, chunks=(2, 3))
            with sp.Fori(1 if first or between is not None else 0, rounds) as i:
                load_round(sp, chunk_rows(name), i + ROUND0[phase], i * 4)

        def load_down(sp, phase, name):
            src = down_rows(name)
            with sp.Fori(0, 4) as i:
                for q in range(12):
                    o, s, c = q // 3, q % 3, q % 4
                    rnd = i * 3 + (ROUND0[phase] + q // 4)
                    w = 2 * PW if s < 2 else PW + PW // 2
                    sp.wait_ge(hi_ready, rnd * 8 + (2 * c - 6))
                    sp.wait_ge(lo_ready, rnd * 8 + (2 * c - 6))
                    sp.dma_start(raw[:, c, 0:w], src(i * 4 + o, s, w)).then_inc(landed[c], 16)

        @block.sync
        def _(sp):
            sp.dma_start(cv[:], d["c"]).then_inc(cv_in, 16)
            sp.dma_start(par[:], d["params"]).then_inc(par_in, 16)
            sp.dma_start(ident[:], d["ident"]).then_inc(par_in, 16)
            sp.dma_start(x[:], d["x"]).then_inc(x_in, 16)
            sp.dma_start(w_ab[:], d["w_ab"]).then_inc(ab_in, 16)
            load_phase(sp, "w_in", "w_in", 18, first=True)
            load_phase(sp, "glu", "glu", 4, between=load_ada)
            load_phase(sp, "dn_proj", "dn_proj", 2)
            load_phase(sp, "w_out", "w_out", 4)
            load_phase(sp, "ffn_up", "ffn_up", 22)
            load_down(sp, "ffn_down", "ffn_down")
            block2_sp(sp)

        @block.gpsimd
        def _(pool):
            pool.wait_ge(used, 144)
            pool.dma_start(s_io[:], d["iota"]).then_inc(io_in, 16)
            s5_pool(pool)
            pool.wait_ge(ada_used, 96)
            pool.dma_start(masks[:], d["masks"][:, 0:8, :]).then_inc(mask_in, 16)
            block2_pool(pool)

        @block.scalar
        def _(act):
            ac = [0]

            def evacuate(bank):
                return po[bank][:, 0:T]

            def round_act(act, phase, rounds, body, r_off=0):
                with act.Fori(0, rounds) as i:
                    for k in range(8):
                        split_hi(act, i + (ROUND0[phase] + r_off), k + LOOK)
                        body(i, i + (ROUND0[phase] + r_off), k)

            act.wait_ge(cv_in, 16)
            act.activation(cve[:], cv[:], ACT.Silu).then_inc(cva.did("silu"), 1)
            for k in range(LOOK):
                act.wait_ge(landed[k // 2], 16)
                act.activation(w_hi[:, k, :], raw[:, k // 2, (k % 2) * PW:(k % 2) * PW + PW], ACT.Copy)\
                   .then_inc(hi_ready, 1)
            act.wait_ge(x_in, 16)
            norm_act(act, 0)
            act.wait_ge(*nv.at(0, "h"))
            split_act(act, 0, h_hi, hf)
            act.wait_ge(ab_done, 1)
            act.activation(graw[0:HEADS], pa[1][0:HEADS, :].rearrange("p (a t) -> p a t", a=2), ACT.Copy)\
               .then_inc(ab_read, 1)

            def on_u(i, rnd, k):
                if k % 2:
                    act.wait_ge(used, rnd * 8 + k + 1)
                    settle(act)
                    act.activation(u[:, ds(i * 4 + k // 2, 1), :], evacuate(k // 2), ACT.Copy)\
                       .then_inc(free[k // 2], 1)
            round_act(act, "w_in", 2, on_u)

            def on_qkv(i, rnd, k):
                def silu(o):
                    act.wait_ge(*freed("w_in", i, 4, o, 2))
                    settle(act)
                    act.activation(qkv[:, ds(i * 4 + o, 1), :], cacc[:, o, :], ACT.Silu).then_inc(conv_read, 1)
                if k % 2 == 0 and k:
                    silu(k // 2 - 1)
                if k == 7:
                    silu(3)
            round_act(act, "w_in", 6, on_qkv, 2)

            def on_z(i, rnd, k):
                if k % 2:
                    act.wait_ge(used, rnd * 8 + k + 1)
                    settle(act)
                    act.activation(z[:, ds(i * 4 + k // 2, 1), :], evacuate(k // 2), ACT.Silu)\
                       .then_inc(free[k // 2], 1)
            round_act(act, "w_in", 2, on_z, 8)

            def on_gate(i, rnd, k):
                if k % 2:
                    act.wait_ge(used, rnd * 8 + k + 1)
                    settle(act)
                    act.activation(gates[:, ds(i * 4 + k // 2, 1), :], evacuate(k // 2), ACT.Sigmoid)\
                       .then_inc(free[k // 2], 1)
            round_act(act, "w_in", 8, on_gate, 10)

            act.wait_ge(used, 144)
            s5_coef_act(act)
            s5_act(act)
            act.wait_ge(*s5v.before(8))
            act.wait_ge(*s5p.before(8))
            unit_act(act, 0, 0)
            unit_act(act, 1, 8)
            rows_act(act)
            dn_act(act)
            act.wait_ge(*dnv.before(4))
            act.activation(ys_hi[:], u[:], ACT.Copy).then_inc(branch_done, 1)
            act.activation(yd_hi[:], z[:], ACT.Copy).then_inc(branch_done, 1)

            def on_glu(i, rnd, k):
                if k % 2:
                    act.wait_ge(used, rnd * 8 + k + 1)
                    act.wait_ge(*glu_v.before(i * 4 + k // 2))
                    act.activation(sg[:, 0, :], evacuate(k % 4), ACT.Sigmoid).then_inc(free[k % 4], 1)
            round_act(act, "glu", 4, on_glu)

            def on_merge(i, rnd, k):
                act.wait_ge(*mrg_v.at(i * 8 + k, "sum"))
                o = ds(i * 8 + k, 1)
                settle(act)
                act.activation(m_hi[:, o, :], gates[:, o, :], ACT.Copy).then_inc(mrg_a, 1)
            round_act(act, "dn_proj", 2, on_merge)
            round_act(act, "w_out", 4, lambda i, rnd, k: None)
            all_freed(act, "ffn_up")
            norm_act(act, 1)
            act.wait_ge(*nv.at(1, "h"))
            split_act(act, 1, h_hi, hf)
            ffn_up_act(act, "ffn_up", 0, round_act)
            ffn_down_act(act, "ffn_down")
            all_freed(act, "w_in2")
            norm_act(act, 2)
            block2_act(act, round_act)

        @block.vector
        def _(dve):
            def link(ins):
                ins.then_inc(dv, 1)
                cc[0] += 1
                dve.wait_ge(dv, cc[0])

            def round_dve(dve, phase, rounds, body, r_off=0):
                with dve.Fori(0, rounds) as i:
                    for k in range(8):
                        body(i, i + (ROUND0[phase] + r_off), k)
                        split_lo(dve, i + (ROUND0[phase] + r_off), k + LOOK)

            def nothing(i, rnd, k):
                pass

            dve.memset(ones[:], 1.0).then_inc(ones_set, 1)
            dve.wait_ge(par_in, 32)
            for k in range(LOOK):
                split_lo(dve, 0, k)
            norm_dve(dve, 0, lambda t: pcol("mix_norm", t), hf)
            dve.wait_ge(*nv.at(0, "h"))
            split_dve(dve, 0, h_lo, h_hi, hf)
            round_dve(dve, "w_in", 2, nothing)

            def conv(dve, out, bank, w, taps, at):
                src = po[bank]
                ins = dve.tensor_scalar(out, src[:, 0:T], w(taps - 1), None, ALU.mult)
                for n, j in enumerate(range(taps - 2, -1, -1)):
                    s = taps - 1 - j
                    ins.then_inc(conv_sum, 1)
                    dve.wait_ge(conv_sum, at + (n + 1))
                    ins = dve.scalar_tensor_tensor(out[:, s:T], src[:, 0:T - s], w(j), out[:, s:T],
                                                   ALU.mult, ALU.add)
                return ins

            def on_qkv(i, rnd, k):
                if k % 2:
                    o = k // 2
                    dve.wait_ge(used, rnd * 8 + k + 1)
                    dve.wait_ge(conv_read, i * 4)
                    w = lambda j: par[:, ds(i * 4 + (COL["conv"] + 24 * j + o), 1)]
                    conv(dve, cacc[:, o, :], o, w, 4, i * 12 + 3 * o).then_inc(free[o], 1)
            dve.wait_ge(*sv.at(0, "lo3"))
            dve.wait_ge(ab_done, 1)
            round_dve(dve, "w_in", 6, on_qkv, 2)
            round_dve(dve, "w_in", 2, nothing, 8)
            round_dve(dve, "w_in", 8, nothing, 10)

            dve.wait_ge(used, 144)
            s5_coef_dve(dve, link)
            dve.wait_ge(io_in, 16)
            dve.wait_ge(*s5cv.at(0, "done"))
            s5_dve(dve)
            unit_dve(dve, 0, 0, float(P))
            unit_dve(dve, 1, 8, 1.0)
            ada_dve(dve)
            rows_dve(dve, link)
            dve.wait_ge(mask_in, 16)
            dve.wait_ge(*rwa.at(0, "cols"))
            dn_dve(dve)
            dve.wait_ge(branch_done, 2)
            dve.tensor_tensor(ys_lo[:], u[:], ys_hi[:].bitcast(F32), ALU.subtract).then_inc(branch_lo, 1)
            dve.tensor_tensor(yd_lo[:], z[:], yd_hi[:].bitcast(F32), ALU.subtract).then_inc(branch_lo, 1)

            def on_glu(i, rnd, k):
                if k % 2:
                    n = i * 4 + k // 2
                    dve.wait_ge(*freed("glu", i, 8, k))
                    dve.tensor_tensor(sg[:, 1, :], po[(k - 1) % 4][:, 0:T], sg[:, 0, :], ALU.mult)\
                       .then_inc(free[(k - 1) % 4], 1)
                    dve.wait_ge(*freed("glu", i, 8, k - 1))
                    g = gates[:, ds(n, 1), :]
                    dve.tensor_tensor(g, g, sg[:, 1, :], ALU.mult).then_inc(glu_v.did("out"), 1)
                    dve.wait_ge(*glu_v.at(n, "out"))
            round_dve(dve, "glu", 4, on_glu)

            def on_merge(i, rnd, k):
                n = i * 8 + k
                dve.wait_ge(used, rnd * 8 + k + 1)
                dve.wait_ge(*mrg_v.before(n))
                dve.tensor_tensor(sg[:, 1, :], po[k % 4][:, 0:T], gates[:, ds(n + 16, 1), :], ALU.mult)\
                   .then_inc(free[k % 4], 1)
                dve.wait_ge(*freed("dn_proj", i, 8, k))
                g = gates[:, ds(n, 1), :]
                dve.tensor_tensor(g, g, sg[:, 1, :], ALU.add).then_inc(mrg_v.did("sum"), 1)
                dve.wait_ge(mrg_a, n + 1)
                dve.tensor_tensor(m_lo[:, ds(n, 1), :], g, m_hi[:, ds(n, 1), :].bitcast(F32), ALU.subtract)\
                   .then_inc(mrg_lo, 1)
            round_dve(dve, "dn_proj", 2, on_merge)

            def on_out(i, rnd, k):
                if k % 2:
                    o = k // 2
                    xt = x[:, ds(i * 4 + o, 1), :]
                    dve.wait_ge(used, rnd * 8 + k + 1)
                    dve.tensor_tensor(xt, po[o][:, 0:T], xt, ALU.add).then_inc(free[o], 1)
            round_dve(dve, "w_out", 4, on_out)
            norm_dve(dve, 1, lambda t: pcol("ffn_norm", t), hf)
            dve.wait_ge(*nv.at(1, "h"))
            split_dve(dve, 1, h_lo, h_hi, hf)
            ffn_up_dve(dve, "ffn_up", 0, round_dve, conv)
            ffn_down_dve(dve, "ffn_down", 0)
            all_freed(dve, "w_in2")
            norm_dve(dve, 2, lambda t: pcol("final_norm", t), x)
            block2_dve(dve, round_dve, conv)

        @block.tensor
        def _(pe):
            pe.wait_ge(ones_set, 1)
            norm_pe(pe, 0)
            pe.wait_ge(*nv.at(0, "h"))
            pe.wait_ge(ab_in, 16)
            for n in range(2):
                for t in range(KD):
                    mm = pe.matmul(pa[1][0:HEADS, n * T:n * T + T], w_ab[:, t, n * HEADS:(n + 1) * HEADS], hf[:, t, :],
                                   start=t == 0, stop=t == KD - 1)
            mm.then_inc(ab_done, 1)
            pe.wait_ge(*sv.at(0, "lo3"))
            project(pe, "w_in", 18, h_hi, h_lo, 16)
            all_freed(pe, "glu")
            pe.wait_ge(*cva.at(0, "silu"))
            s5_pe(pe)
            pe.wait_ge(*s5v.before(8))
            unit_pe(pe, 0)
            unit_pe(pe, 1)
            pe.wait_ge(*l2v.before(8))
            rows_pe(pe)
            pe.wait_ge(*rwa.at(0, "cols"))
            dn_pe(pe)
            pe.wait_ge(branch_lo, 2)
            project(pe, "glu", 4, ys_hi, ys_lo, 8)
            project(pe, "dn_proj", 2, yd_hi, yd_lo, 8)
            pe.wait_ge(mrg_lo, 16)
            project(pe, "w_out", 4, m_hi, m_lo, 16)
            norm_pe(pe, 1)
            pe.wait_ge(*sv.at(1, "lo3"))
            project(pe, "ffn_up", 22, h_hi, h_lo, 16)
            pe.wait_ge(ff_lo, KF)
            project_down(pe, "ffn_down")
            norm_pe(pe, 2)
            block2_pe(pe)



def tiles(w):
    k, n = w.shape
    return np.ascontiguousarray(w.reshape(k // P, P, n // P, P).transpose(2, 1, 0, 3).reshape(n // P, P, k))


def paired(t, order):
    n, p, w = t.shape
    return np.ascontiguousarray(t[order].reshape(n // 2, 2, p, w).transpose(0, 2, 1, 3).reshape(n // 2, p, 2 * w))


def cols(v):
    return np.asarray(v).reshape(-1, P).T


def constants():
    t = np.arange(P)
    same = (t[:, None] // C) == (t[None, :] // C)
    levels = []
    for b in (1, 2, 4, 8, 16, 32):
        levels.append(((t[:, None] // (2 * b)) == (t[None, :] // (2 * b)))
                      & (t[:, None] % (2 * b) >= b) & (t[None, :] % (2 * b) < b))
    before = same & (t[:, None] < t[None, :])
    upto = same & (t[:, None] <= t[None, :])
    masks = np.stack(levels + [before, upto], 1).astype(np.float32)
    masks[:, 6] *= -1.0
    return {"ident": np.eye(P, dtype=np.float32), "masks": np.ascontiguousarray(masks),
            "iota": np.tile(np.arange(T, dtype=np.float32), (P, 1))}


def layout(i):
    a = {k: np.asarray(v) for k, v in i.items()}
    f32 = np.float32
    w_in = a["w_in"][0]
    main = np.concatenate([w_in[:, :5120], w_in[:, 5136:]], axis=1)
    ab = w_in[:, 5120:5136]
    two = np.arange(16)
    inter = lambda n: np.stack([np.arange(n), np.arange(n) + n], 1).reshape(-1)
    out = {
        "w_in": tiles(main),
        "w_ab": np.ascontiguousarray(ab.reshape(KD, P, 16).transpose(1, 0, 2)),
        "glu": paired(tiles(a["s5_glu_w"][0]), inter(16)),
        "dn_proj": paired(tiles(a["dn_proj_w"][0]), two),
        "w_out": tiles(a["w_out"][0]),
        "ffn_up": tiles(a["ffn_up"][0])[inter(KF)],
        "ffn_down": tiles(a["ffn_down"][0]),
        "x": np.ascontiguousarray(a["x"][0].T.reshape(KD, P, T).transpose(1, 0, 2)),
    }
    b = np.stack([a["s5_b_re"][0], a["s5_b_im"][0]])
    c = np.stack([a["s5_c_re"][0], a["s5_c_im"][0]])
    bt = np.zeros((8, P, 2, P), f32)
    ct = np.zeros((8, P, 4, 2, 32), f32)
    for g in range(64):
        j, e = g // 2, g % 2
        t, q = j // 4, j % 4
        for r in range(2):
            bt[t, 32 * q + 16 * e:32 * q + 16 * e + 16, r, 64 * e:64 * e + 64] = b[r, g].T
            ct[t, 64 * e:64 * e + 64, q, r, 16 * e:16 * e + 16] = c[r, g].T
    out["s5_b"], out["s5_c"] = bt, ct
    one = lambda v: np.pad(np.asarray(v, f32)[:, None], ((0, P - len(v)), (0, 0)))
    inter44 = inter(KF)
    parts = {
        "mix_norm": cols(a["mix_norm_w"][0]), "ffn_norm": cols(a["ffn_norm_w"][0]),
        "final_norm": cols(a["final_norm_w"]),
        "a_re": cols(a["s5_a_re"][0].reshape(-1)), "a_im": cols(a["s5_a_im"][0].reshape(-1)),
        "log_dt": cols(np.repeat(a["s5_log_dt"][0], 64)), "s5_d": cols(a["s5_d"][0]),
        "conv": np.concatenate([cols(a["dn_conv_w"][0, j]) for j in range(4)], 1),
        "dn_norm": cols(a["dn_norm_w"][0]), "a_log": one(a["dn_a_log"][0]), "dt_bias": one(a["dn_dt_bias"][0]),
        "ffn_conv": np.concatenate([cols(a["ffn_conv_w"][0, j])[:, inter44] for j in range(3)], 1),
    }
    block2_layout(a, out, parts)
    out["params"] = np.ascontiguousarray(np.concatenate(
        [parts.get(n, np.zeros((P, w), f32)) for n, w in PARAMS], 1), dtype=f32)
    assert out["params"].shape == (P, NPAR)
    out.update(constants())
    constants2(out)
    return out


def kernel(**inputs):
    import concourse.bacc as bacc
    from concourse.bass_utils import run_bass_kernel_spmd

    nc = bacc.Bacc("TRN2", target_bir_lowering=False, num_devices=1)
    arrays = layout(inputs)
    dram = {n: nc.dram_tensor(n, v.shape, mybir.dt.from_np(v.dtype), kind="ExternalInput").ap()
            for n, v in arrays.items()}
    dram["out"] = nc.dram_tensor("out", (P, KD, T), F32, kind="ExternalOutput").ap()
    program(nc, dram)
    r = run_bass_kernel_spmd(nc, [arrays], core_ids=[0])
    y = np.asarray(r.results[0]["out"])
    return np.ascontiguousarray(y.transpose(2, 1, 0).reshape(1, T, D))


def block2_layout(a, out, parts):
    g = {k[:-2]: v for k, v in a.items() if k.endswith("_2")}
    f32 = np.float32
    fm = lambda v: np.ascontiguousarray(v.T.reshape(KD, P, -1).transpose(1, 0, 2))
    out["c"] = np.ascontiguousarray(np.stack([cols(g["c"][0]), cols(g["c_ctx"])], 2))
    out["ctx"] = fm(g["ctx"][0])
    out["ada"] = np.ascontiguousarray(g["ada_w"][0].reshape(4, 4, P, 24, 512).transpose(3, 0, 2, 1, 4)).reshape(96, P, 2048)
    w = g["w_in"][0]
    heads = [h for j in range(8) for h in ((j, 4 + j) if j < 4 else (4 + j, 8 + j))]
    q_cols = np.concatenate([np.arange(64) + 64 * h for h in heads])
    r0 = 1536
    sel = lambda lo, n: w[:, lo:lo + n]
    k0, v0, l0 = r0 + 1024, r0 + 2048, r0 + 3072
    pad = np.zeros((D, 96), f32)
    out["w_in2"] = tiles(np.concatenate([
        sel(k0, 1024), sel(v0, 1024), sel(1024, 512), sel(l0, 416), pad, sel(r0, 1024), w[:, q_cols]], 1))
    w_out = g["w_out"][0]
    out["w_out2"] = tiles(np.concatenate([w_out[q_cols], w_out[1024:]], 0))
    inter = np.stack([np.arange(KF), np.arange(KF) + KF], 1).reshape(-1)
    out["ffn_up2"] = tiles(np.concatenate([g["ffn_w1"][0], g["ffn_w3"][0]], 1))[inter]
    out["ffn_down2"] = tiles(g["ffn_w2"][0])
    rk_w = np.zeros((8, P, 4, P), f32)
    wu, au, gu = (v[0].reshape(-1, 8, P) for v in (g["w_up"], g["a_up"], g["g_up"]))
    rk_w[:, :, 0] = wu.transpose(1, 0, 2)
    rk_w[:, :, 1] = au.transpose(1, 0, 2)
    rk_w[:, :, 2] = gu[:P].transpose(1, 0, 2)
    rk_w[:, :32, 3] = gu[P:].transpose(1, 0, 2)
    out["rk_w"] = rk_w
    ts = lambda v: cols(np.concatenate([v[1024:3072], v[3072:3328], v[:1024], v[3328:3488], np.zeros(96, f32)]))
    parts.update({
        "ada_b": cols(g["ada_b"][0]), "norm1": cols(g["norm1_g"][0]), "norm2": cols(g["norm2_g"][0]),
        "final2": cols(g["final_norm_g"]), "sink": np.tile(g["attn_sink"][0][heads], (P, 1)),
        "ts_prev": ts(g["ts_prev"][0]), "ts_next": ts(g["ts_next"][0]),
        "w0": np.concatenate([cols(g["w0"][0, e]) for e in range(2)], 1),
        "a0": np.concatenate([cols(g["a0"][0, e]) for e in range(2)], 1),
        "k_k": cols(g["k_k"][0]), "k_a": cols(g["k_a"][0]), "r_k": cols(g["r_k"][0]),
        "lnx_g": cols(g["lnx_g"][0]), "lnx_b": cols(g["lnx_b"][0]),
    })


def constants2(out):
    t = np.arange(P)
    same = (t[:, None] // C) == (t[None, :] // C)
    extra = np.stack([-(same & (t[:, None] > t[None, :])).astype(np.float32),
                      (same & (t[:, None] >= t[None, :])).astype(np.float32)], 1)
    out["masks"] = np.ascontiguousarray(np.concatenate([out["masks"], extra], 1), dtype=np.float32)
    out["k_bd"] = np.ascontiguousarray(same.astype(np.float32))
    out["k_rst"] = np.tile((np.arange(2 * T) % C != 0).astype(np.float32), (P, 1))
    freqs = (1.0 / (10000.0 ** (np.arange(16, dtype=np.float32) / 16))).astype(np.float32)
    tok = np.arange(T)
    pos = np.stack([tok // 64, tok % 64]).astype(np.float32)
    p = np.arange(P) % 64
    ang = pos[p // 32] * freqs[p % 16][:, None]
    out["t_cos"], out["t_sin"] = np.cos(ang).astype(np.float32), np.sin(ang).astype(np.float32)
    perm = np.zeros((P, P), np.float32)
    for m in range(P):
        if m % 32 < 16:
            perm[m + 16, m] = -1.0
        else:
            perm[m - 16, m] = 1.0
    out["t_perm"] = perm
    qi = np.arange(T).reshape(2, P).T
    band = np.zeros((P, 2, 2 * T), np.float32)
    far = np.abs(qi[:, :, None] - np.arange(T)[None, None, :]) > 128
    band[:, :, T:][far] = -8e30
    out["t_band"] = band
```
